# Optimizing a Trainium2 kernel written in Bass

```python
import math
import jax, jax.numpy as jnp
from jax import lax
import numpy as np

D_MODEL = 1024
BATCH = 1
SEQ = 1024
DEPTH = 2

GRID_W = 64
CTX_LEN = 256
MIX_WIDTH = D_MODEL
F_GROUPS = 4
F_CH = MIX_WIDTH // 2 // F_GROUPS
F_WIDTH = F_GROUPS * F_CH
H_DIFF = 4
DH = MIX_WIDTH // 2 // H_DIFF // 2
DV = 2 * DH
QK_WIDTH = H_DIFF * 2 * DH
ATT_WIDTH = H_DIFF * DV
F0 = 0
Q0 = F0 + F_WIDTH
K0 = Q0 + QK_WIDTH
V0 = K0 + QK_WIDTH
G0 = V0 + ATT_WIDTH
EVEN_IN = G0 + MIX_WIDTH
CONV_WIDTH = MIX_WIDTH
CONV_K = 3
ODD_IN = 4 * CONV_WIDTH
N_EVEN = (DEPTH + 1) // 2
N_ODD = DEPTH // 2
ROPE_BASE = 10000.0
Q_BLOCK = 128
EPS = 1e-6
ATTN_SCALE = DH ** -0.5


def rms_norm(x, g):
    x32 = x.astype(jnp.float32)
    y = x32 * lax.rsqrt(jnp.mean(x32 * x32, axis=-1, keepdims=True) + EPS)
    return (y * g.astype(jnp.float32)).astype(x.dtype)

def ada_params(cvec, w, b):
    m = jax.nn.silu(cvec) @ w + b
    return jnp.split(m, 3, axis=-1)

def modulate(x, g, shift, scale):
    return rms_norm(x, g) * (1.0 + scale) + shift

def need_ctx_after(i):
    return any(j % 2 == 0 for j in range(i + 1, DEPTH))

def lambda_init_fn(layer_idx):
    return 0.8 - 0.6 * math.exp(-0.3 * layer_idx)

def axial_rope_tables(rows):
    pos_r = jnp.repeat(jnp.arange(rows, dtype=jnp.float32), GRID_W)
    pos_c = jnp.tile(jnp.arange(GRID_W, dtype=jnp.float32), rows)
    half = DH // 2
    freqs = ROPE_BASE ** (-jnp.arange(0, half, 2, dtype=jnp.float32) / half)
    ang_r = pos_r[:, None] * freqs
    ang_c = pos_c[:, None] * freqs
    return (jnp.cos(ang_r), jnp.sin(ang_r), jnp.cos(ang_c), jnp.sin(ang_c))

def _rotate(x, cos, sin):
    x1, x2 = jnp.split(x, 2, axis=-1)
    return jnp.concatenate([x1 * cos - x2 * sin, x1 * sin + x2 * cos], axis=-1)

def apply_axial_rope(x, tabs):
    cos_r, sin_r, cos_c, sin_c = [t[None, :, None, None, :].astype(x.dtype) for t in tabs]
    xr, xc = jnp.split(x, 2, axis=-1)
    return jnp.concatenate([_rotate(xr, cos_r, sin_r), _rotate(xc, cos_c, sin_c)], axis=-1)

def fourier_mix(u):
    b, n, _ = u.shape
    u32 = u.reshape(b, n, F_GROUPS, F_CH).astype(jnp.float32)
    f = jnp.fft.fftn(u32, axes=(1, 3), norm="ortho").real
    return f.reshape(b, n, F_WIDTH).astype(u.dtype)

def split_kv(kv, k_g):
    b, n, _ = kv.shape
    k = rms_norm(kv[..., :QK_WIDTH].reshape(b, n, H_DIFF, 2, DH), k_g)
    v = kv[..., QK_WIDTH:].reshape(b, n, H_DIFF, DV)
    return k, v

def split_qkv(proj, q_g, k_g):
    b, n, _ = proj.shape
    q = rms_norm(proj[..., Q0:K0].reshape(b, n, H_DIFF, 2, DH), q_g)
    k, v = split_kv(proj[..., K0:G0], k_g)
    return q, k, v

def diff_attention(q, k, v, lam):
    b, n = q.shape[:2]
    nblk = n // Q_BLOCK
    qb = q.reshape(b, nblk, Q_BLOCK, H_DIFF, 2, DH).swapaxes(0, 1)

    def one_block(qblk):
        s = jnp.einsum('bqhmd,bkhmd->bhmqk', qblk, k,
                       preferred_element_type=jnp.float32) * ATTN_SCALE
        p = jax.nn.softmax(s, axis=-1)
        a = p[:, :, 0] - lam * p[:, :, 1]
        return jnp.einsum('bhqk,bkhv->bqhv', a.astype(v.dtype), v)

    o = lax.map(one_block, qb)
    return o.swapaxes(0, 1).reshape(b, n, H_DIFF, DV)

def even_output(proj, attn_o, subln_g, lam_init, w_out):
    b, n, _ = proj.shape
    fo = fourier_mix(proj[..., F0:Q0])
    ao = (rms_norm(attn_o, subln_g) * (1.0 - lam_init)).reshape(b, n, ATT_WIDTH)
    y = jnp.concatenate([fo, ao], axis=-1) * jax.nn.silu(proj[..., G0:])
    return y @ w_out

def short_conv_mixer(proj, conv_w, w_out):
    bg, cg, xt, g = jnp.split(proj, 4, axis=-1)
    u = cg * xt
    n = u.shape[1]
    pad = CONV_K // 2
    up = jnp.pad(u, ((0, 0), (pad, pad), (0, 0)))
    conv = sum(conv_w[t] * up[:, t:t + n] for t in range(CONV_K))
    return (bg * conv * jax.nn.silu(g)) @ w_out

def first_inputs(seed: int = 0) -> dict:
    key = jax.random.key(seed)
    ks = jax.random.split(key, 20)
    f32 = jnp.float32
    D = D_MODEL
    nrm = lambda k, shape, s: (jax.random.normal(k, shape, f32) * s)
    return {
        "x": nrm(ks[0], (BATCH, SEQ, D), 1.0),
        "c": nrm(ks[1], (BATCH, D), 1.0),
        "ctx": nrm(ks[2], (BATCH, CTX_LEN, D), 1.0),
        "c_ctx": nrm(ks[3], (D,), 1.0),
        "norm_g": 1.0 + nrm(ks[4], (DEPTH, D), 0.02),
        "ada_w": nrm(ks[5], (DEPTH, D, 3 * D), D ** -0.5),
        "ada_b": nrm(ks[6], (DEPTH, 3 * D), 0.01),
        "even_w_in": nrm(ks[7], (N_EVEN, D, EVEN_IN), D ** -0.5),
        "even_q_norm": 1.0 + nrm(ks[8], (N_EVEN, DH), 0.02),
        "even_k_norm": 1.0 + nrm(ks[9], (N_EVEN, DH), 0.02),
        "even_lambda_q1": nrm(ks[10], (N_EVEN, DH), 0.1),
        "even_lambda_k1": nrm(ks[11], (N_EVEN, DH), 0.1),
        "even_lambda_q2": nrm(ks[12], (N_EVEN, DH), 0.1),
        "even_lambda_k2": nrm(ks[13], (N_EVEN, DH), 0.1),
        "even_subln": 1.0 + nrm(ks[14], (N_EVEN, DV), 0.02),
        "even_w_out": nrm(ks[15], (N_EVEN, MIX_WIDTH, D), MIX_WIDTH ** -0.5),
        "odd_w_in": nrm(ks[16], (N_ODD, D, ODD_IN), D ** -0.5),
        "odd_conv_w": nrm(ks[17], (N_ODD, CONV_K, CONV_WIDTH), CONV_K ** -0.5),
        "odd_w_out": nrm(ks[18], (N_ODD, CONV_WIDTH, D), CONV_WIDTH ** -0.5),
    }

def first_block(x, c, ctx, c_ctx, norm_g, ada_w, ada_b, even_w_in, even_q_norm, even_k_norm,
              even_lambda_q1, even_lambda_k1, even_lambda_q2, even_lambda_k2, even_subln,
              even_w_out, odd_w_in, odd_conv_w, odd_w_out):
    n = x.shape[1]
    ROWS = n // GRID_W
    tabs = axial_rope_tables(ROWS)
    x_lat = x
    x_ctx = ctx
    for i in range(DEPTH):
        ctx_out = need_ctx_after(i)
        shift, scale, gate = ada_params(c, ada_w[i], ada_b[i])
        shift_c, scale_c, gate_c = ada_params(c_ctx, ada_w[i], ada_b[i])
        h = modulate(x_lat, norm_g[i], shift[:, None, :], scale[:, None, :])
        if i % 2 == 0:
            e = i // 2
            w_in = even_w_in[e]
            lam_init = lambda_init_fn(i)
            lam = (jnp.exp(jnp.sum(even_lambda_q1[e].astype(jnp.float32) * even_lambda_k1[e].astype(jnp.float32)))
                   - jnp.exp(jnp.sum(even_lambda_q2[e].astype(jnp.float32) * even_lambda_k2[e].astype(jnp.float32)))
                   + lam_init)
            hc = modulate(x_ctx, norm_g[i], shift_c, scale_c)
            if ctx_out:
                proj_c = hc @ w_in
                qc, kc, vc = split_qkv(proj_c, even_q_norm[e], even_k_norm[e])
                oc = diff_attention(qc, kc, vc, lam)
                yc = even_output(proj_c, oc, even_subln[e], lam_init, even_w_out[e])
            else:
                kc, vc = split_kv(hc @ w_in[:, K0:G0], even_k_norm[e])
            proj = h @ w_in
            q, k, v = split_qkv(proj, even_q_norm[e], even_k_norm[e])
            q = apply_axial_rope(q, tabs)
            k = apply_axial_rope(k, tabs)
            k_all = jnp.concatenate([kc, k], axis=1)
            v_all = jnp.concatenate([vc, v], axis=1)
            o = diff_attention(q, k_all, v_all, lam)
            y = even_output(proj, o, even_subln[e], lam_init, even_w_out[e])
        else:
            o_i = i // 2
            y = short_conv_mixer(h @ odd_w_in[o_i], odd_conv_w[o_i], odd_w_out[o_i])
            if ctx_out:
                hc = modulate(x_ctx, norm_g[i], shift_c, scale_c)
                yc = short_conv_mixer(hc @ odd_w_in[o_i], odd_conv_w[o_i], odd_w_out[o_i])
        x_lat = x_lat + gate[:, None, :] * y
        if ctx_out:
            x_ctx = x_ctx + gate_c * yc
    return x_lat


DEPTH_2 = 1

N_MIXERS = 4
POOL_WINDOWS = (2, 4, 8, 16)
POOL_GROUP = D_MODEL // len(POOL_WINDOWS)
S5_GROUP = 16
S5_GROUPS = D_MODEL // S5_GROUP
S5_STATE = 64
S5_DT_MIN = 1e-3
S5_DT_MAX = 1e-1
LRU_WIDTH = D_MODEL
LRU_BLOCKS = 4
LRU_BLOCK = LRU_WIDTH // LRU_BLOCKS
LRU_CONV = 4
LRU_C = 8.0
SB_HEADS = 16
SB_HEAD_DIM = D_MODEL // SB_HEADS
SB_Q_BLOCK = 128
FFN_HIDDEN = 2816
FFN_CONV = 3


def n_layers_of(m):
    return len(range(m, DEPTH_2, N_MIXERS))

def rms_norm_2(x, g):
    xf = x.astype(jnp.float32)
    y = xf * lax.rsqrt(jnp.mean(xf * xf, axis=-1, keepdims=True) + EPS)
    return (y * g.astype(jnp.float32)).astype(x.dtype)

def causal_depthwise_conv(x, w, b):
    k_width = w.shape[0]
    seq = x.shape[1]
    xp = jnp.pad(x, ((0, 0), (k_width - 1, 0), (0, 0)))
    y = b
    for k in range(k_width):
        y = y + w[k] * xp[:, k:k + seq]
    return y

def linear_scan_combine(left, right):
    a_l, b_l = left
    a_r, b_r = right
    return a_r * a_l, a_r * b_l + b_r

def pool_mixer(x, w, b, scale):
    bsz, seq, _ = x.shape
    xf = x.astype(jnp.float32)
    cs = jnp.pad(jnp.cumsum(xf, axis=1), ((0, 0), (1, 0), (0, 0)))
    pos = jnp.arange(seq)
    groups = []
    for gi, w_len in enumerate(POOL_WINDOWS):
        c = cs[..., gi * POOL_GROUP:(gi + 1) * POOL_GROUP]
        lo = jnp.maximum(pos + 1 - w_len, 0)
        window_sum = c[:, 1:] - jnp.take(c, lo, axis=1)
        count = (pos + 1 - lo).astype(jnp.float32)[:, None]
        groups.append(window_sum / count - xf[..., gi * POOL_GROUP:(gi + 1) * POOL_GROUP])
    d = jnp.stack(groups, axis=2)
    y = jnp.einsum('bsgc,gcd->bsgd', d, w.astype(jnp.float32)).reshape(bsz, seq, D_MODEL) + b
    return (scale * y).astype(x.dtype)

def s5_mixer(x, lam_re, lam_im, log_dt, b_re, b_im, c_re, c_im, d_skip, w_out, b_out):
    f32 = jnp.float32
    bsz, seq, _ = x.shape
    xf = x.astype(f32)
    u = xf.reshape(bsz, seq, S5_GROUPS, S5_GROUP)
    lam = lax.complex(jnp.minimum(lam_re.astype(f32), -1e-4), lam_im.astype(f32))
    dt = jnp.exp(log_dt.astype(f32))[:, None]
    lam_bar = jnp.exp(lam * dt)
    b_bar = ((lam_bar - 1.0) / lam)[..., None] * lax.complex(b_re.astype(f32), b_im.astype(f32))
    bu = lax.complex(jnp.einsum('bsgh,gph->bsgp', u, jnp.real(b_bar)),
                     jnp.einsum('bsgh,gph->bsgp', u, jnp.imag(b_bar)))
    a = jnp.broadcast_to(lam_bar, (seq,) + lam_bar.shape)[None]
    _, states = lax.associative_scan(linear_scan_combine, (a, bu), axis=1)
    y = (jnp.einsum('bsgp,ghp->bsgh', jnp.real(states), c_re.astype(f32))
         - jnp.einsum('bsgp,ghp->bsgh', jnp.imag(states), c_im.astype(f32)))
    y = y.reshape(bsz, seq, D_MODEL) + d_skip.astype(f32) * xf
    y = jax.nn.gelu(y).astype(x.dtype)
    val, gate = jnp.split(y @ w_out + b_out, 2, axis=-1)
    return val * jax.nn.sigmoid(gate)

def rglru_mixer(x, w_in, conv_w, conv_b, w_a, b_a, w_x, b_x, lam, w_out):
    f32 = jnp.float32
    bsz, seq, _ = x.shape
    gate_branch, rec = jnp.split(x @ w_in, 2, axis=-1)
    rec = causal_depthwise_conv(rec, conv_w, conv_b).astype(f32)
    rb = rec.reshape(bsz, seq, LRU_BLOCKS, LRU_BLOCK)
    r = jax.nn.sigmoid(jnp.einsum('bsnc,ncd->bsnd', rb, w_a.astype(f32)).reshape(bsz, seq, LRU_WIDTH) + b_a)
    i = jax.nn.sigmoid(jnp.einsum('bsnc,ncd->bsnd', rb, w_x.astype(f32)).reshape(bsz, seq, LRU_WIDTH) + b_x)
    log_a = -LRU_C * r * jax.nn.softplus(-lam.astype(f32))
    a = jnp.exp(log_a)
    mult = jnp.sqrt(-jnp.expm1(2.0 * log_a))
    _, h = lax.associative_scan(linear_scan_combine, (a, mult * (i * rec)), axis=1)
    y = jax.nn.gelu(gate_branch.astype(f32)) * h
    return y.astype(x.dtype) @ w_out

def stick_breaking_mixer(x, w_qkv, q_g, k_g, w_o):
    bsz, seq, _ = x.shape
    q, k, v = jnp.split(x @ w_qkv, 3, axis=-1)
    to_heads = lambda t: t.reshape(bsz, seq, SB_HEADS, SB_HEAD_DIM).transpose(0, 2, 1, 3)
    q = rms_norm_2(to_heads(q), q_g)
    k = rms_norm_2(to_heads(k), k_g)
    v = to_heads(v)
    scale = 1.0 / math.sqrt(SB_HEAD_DIM)
    outs = []
    for start in range(0, seq, SB_Q_BLOCK):
        end = start + SB_Q_BLOCK
        kb, vb = k[:, :, :end], v[:, :, :end]
        z = jnp.einsum('bhtd,bhsd->bhts', q[:, :, start:end], kb).astype(jnp.float32) * scale
        t_pos = start + jnp.arange(SB_Q_BLOCK)[:, None]
        s_pos = jnp.arange(end)[None, :]
        mask = s_pos < t_pos
        log_1m_beta = jnp.where(mask, jax.nn.log_sigmoid(-z), 0.0)
        rest = lax.cumsum(log_1m_beta, axis=3, reverse=True) - log_1m_beta
        att = jnp.where(mask, jnp.exp(jax.nn.log_sigmoid(z) + rest), 0.0)
        outs.append(jnp.einsum('bhts,bhsd->bhtd', att.astype(v.dtype), vb))
    o = jnp.concatenate(outs, axis=2).transpose(0, 2, 1, 3).reshape(bsz, seq, D_MODEL)
    return o @ w_o

def conv_ffn(x, w_in, conv_w, conv_b, w_out):
    h = causal_depthwise_conv(x @ w_in, conv_w, conv_b)
    val, gate = jnp.split(h, 2, axis=-1)
    return (jax.nn.silu(gate) * val) @ w_out

def second_inputs(seed: int = 0) -> dict:
    key = jax.random.key(seed)
    ks = iter(jax.random.split(key, 40))
    nrm = lambda shape, std: jax.random.normal(next(ks), shape, jnp.float32) * std
    gain = lambda shape: 1.0 + nrm(shape, 0.02)
    nA, nB, nC, nD = (n_layers_of(m) for m in range(N_MIXERS))
    G, P, H = S5_GROUPS, S5_STATE, S5_GROUP
    a0 = jax.random.uniform(next(ks), (nC, LRU_WIDTH), jnp.float32, 0.9, 0.999)
    return {
        "x": nrm((BATCH, SEQ, D_MODEL), 1.0),
        "norm_mix_g": gain((DEPTH_2, D_MODEL)),
        "norm_ffn_g": gain((DEPTH_2, D_MODEL)),
        "pool_w": nrm((nA, len(POOL_WINDOWS), POOL_GROUP, POOL_GROUP), POOL_GROUP ** -0.5),
        "pool_b": nrm((nA, D_MODEL), 0.01),
        "pool_scale": 1.0 + nrm((nA, D_MODEL), 0.1),
        "s5_lam_re": -0.5 + nrm((nA * 0 + nB, G, P), 0.01),
        "s5_lam_im": math.pi * jnp.arange(P, dtype=jnp.float32) + nrm((nB, G, P), 0.01),
        "s5_log_dt": jax.random.uniform(next(ks), (nB, G), jnp.float32, math.log(S5_DT_MIN), math.log(S5_DT_MAX)),
        "s5_b_re": nrm((nB, G, P, H), (2 * H) ** -0.5),
        "s5_b_im": nrm((nB, G, P, H), (2 * H) ** -0.5),
        "s5_c_re": nrm((nB, G, H, P), P ** -0.5),
        "s5_c_im": nrm((nB, G, H, P), P ** -0.5),
        "s5_d": nrm((nB, D_MODEL), 1.0),
        "s5_w_out": nrm((nB, D_MODEL, 2 * D_MODEL), D_MODEL ** -0.5),
        "s5_b_out": nrm((nB, 2 * D_MODEL), 0.01),
        "lru_w_in": nrm((nC, D_MODEL, 2 * LRU_WIDTH), D_MODEL ** -0.5),
        "lru_conv_w": nrm((nC, LRU_CONV, LRU_WIDTH), LRU_CONV ** -0.5),
        "lru_conv_b": nrm((nC, LRU_WIDTH), 0.01),
        "lru_w_a": nrm((nC, LRU_BLOCKS, LRU_BLOCK, LRU_BLOCK), LRU_BLOCK ** -0.5),
        "lru_b_a": nrm((nC, LRU_WIDTH), 0.01),
        "lru_w_x": nrm((nC, LRU_BLOCKS, LRU_BLOCK, LRU_BLOCK), LRU_BLOCK ** -0.5),
        "lru_b_x": nrm((nC, LRU_WIDTH), 0.01),
        "lru_lam": jnp.log(a0) - jnp.log1p(-a0),
        "lru_w_out": nrm((nC, LRU_WIDTH, D_MODEL), LRU_WIDTH ** -0.5),
        "sb_w_qkv": nrm((nD, D_MODEL, 3 * D_MODEL), D_MODEL ** -0.5),
        "sb_q_g": gain((nD, SB_HEAD_DIM)),
        "sb_k_g": gain((nD, SB_HEAD_DIM)),
        "sb_w_o": nrm((nD, D_MODEL, D_MODEL), D_MODEL ** -0.5),
        "ffn_w_in": nrm((DEPTH_2, D_MODEL, 2 * FFN_HIDDEN), D_MODEL ** -0.5),
        "ffn_conv_w": nrm((DEPTH_2, FFN_CONV, 2 * FFN_HIDDEN), FFN_CONV ** -0.5),
        "ffn_conv_b": nrm((DEPTH_2, 2 * FFN_HIDDEN), 0.01),
        "ffn_w_out": nrm((DEPTH_2, FFN_HIDDEN, D_MODEL), FFN_HIDDEN ** -0.5),
    }

def second_block(x, norm_mix_g, norm_ffn_g,
              pool_w, pool_b, pool_scale,
              s5_lam_re, s5_lam_im, s5_log_dt, s5_b_re, s5_b_im, s5_c_re, s5_c_im, s5_d, s5_w_out, s5_b_out,
              lru_w_in, lru_conv_w, lru_conv_b, lru_w_a, lru_b_a, lru_w_x, lru_b_x, lru_lam, lru_w_out,
              sb_w_qkv, sb_q_g, sb_k_g, sb_w_o,
              ffn_w_in, ffn_conv_w, ffn_conv_b, ffn_w_out):
    for layer in range(DEPTH_2):
        m, j = layer % N_MIXERS, layer // N_MIXERS
        h = rms_norm_2(x, norm_mix_g[layer])
        if m == 0:
            y = pool_mixer(h, pool_w[j], pool_b[j], pool_scale[j])
        elif m == 1:
            y = s5_mixer(h, s5_lam_re[j], s5_lam_im[j], s5_log_dt[j], s5_b_re[j], s5_b_im[j],
                         s5_c_re[j], s5_c_im[j], s5_d[j], s5_w_out[j], s5_b_out[j])
        elif m == 2:
            y = rglru_mixer(h, lru_w_in[j], lru_conv_w[j], lru_conv_b[j], lru_w_a[j], lru_b_a[j],
                            lru_w_x[j], lru_b_x[j], lru_lam[j], lru_w_out[j])
        else:
            y = stick_breaking_mixer(h, sb_w_qkv[j], sb_q_g[j], sb_k_g[j], sb_w_o[j])
        x = x + y.astype(x.dtype)
        f = conv_ffn(rms_norm_2(x, norm_ffn_g[layer]), ffn_w_in[layer], ffn_conv_w[layer], ffn_conv_b[layer], ffn_w_out[layer])
        x = x + f.astype(x.dtype)
    return x


def setup_inputs(seed=0):
    out = dict(first_inputs(seed))
    for name, value in second_inputs(seed + 1).items():
        if name != "x":
            out[name + "_2"] = value
    return out


def reference(
    x, c, ctx, c_ctx, norm_g, ada_w, ada_b, even_w_in, even_q_norm, even_k_norm, even_lambda_q1,
    even_lambda_k1, even_lambda_q2, even_lambda_k2, even_subln, even_w_out, odd_w_in,
    odd_conv_w, odd_w_out, norm_mix_g_2, norm_ffn_g_2, pool_w_2, pool_b_2, pool_scale_2,
    s5_lam_re_2, s5_lam_im_2, s5_log_dt_2, s5_b_re_2, s5_b_im_2, s5_c_re_2, s5_c_im_2, s5_d_2,
    s5_w_out_2, s5_b_out_2, lru_w_in_2, lru_conv_w_2, lru_conv_b_2, lru_w_a_2, lru_b_a_2,
    lru_w_x_2, lru_b_x_2, lru_lam_2, lru_w_out_2, sb_w_qkv_2, sb_q_g_2, sb_k_g_2, sb_w_o_2,
    ffn_w_in_2, ffn_conv_w_2, ffn_conv_b_2, ffn_w_out_2,
):
    x = first_block(
        x, c, ctx, c_ctx, norm_g, ada_w, ada_b, even_w_in, even_q_norm, even_k_norm,
        even_lambda_q1, even_lambda_k1, even_lambda_q2, even_lambda_k2, even_subln, even_w_out,
        odd_w_in, odd_conv_w, odd_w_out,
    )
    return second_block(
        x, norm_mix_g_2, norm_ffn_g_2, pool_w_2, pool_b_2, pool_scale_2, s5_lam_re_2,
        s5_lam_im_2, s5_log_dt_2, s5_b_re_2, s5_b_im_2, s5_c_re_2, s5_c_im_2, s5_d_2,
        s5_w_out_2, s5_b_out_2, lru_w_in_2, lru_conv_w_2, lru_conv_b_2, lru_w_a_2, lru_b_a_2,
        lru_w_x_2, lru_b_x_2, lru_lam_2, lru_w_out_2, sb_w_qkv_2, sb_q_g_2, sb_k_g_2, sb_w_o_2,
        ffn_w_in_2, ffn_conv_w_2, ffn_conv_b_2, ffn_w_out_2,
    )


_drawn_inputs = setup_inputs


def setup_inputs(seed=0):
    import zlib

    import numpy as np

    out = dict(_drawn_inputs(seed))
    spreads = {}
    factors = {'even_q_norm': 8.0,
     'even_k_norm': 8.0,
     'even_lambda_q1': 8.0,
     'even_lambda_q2': 3.421,
     'even_subln': 7.271,
     'norm_mix_g_2': 5.918,
     'norm_ffn_g_2': 6.403,
     'pool_b_2': 23.373,
     'ffn_conv_b_2': 25.628}
    for name, (base, spread) in spreads.items():
        noise = np.random.default_rng([zlib.crc32(name.encode()), seed]).standard_normal(out[name].shape)
        drawn = base * np.exp(spread * noise) if base else spread * noise
        out[name] = __import__('jax').numpy.asarray(drawn.astype(out[name].dtype))
    for name, factor in factors.items():
        out[name] = (out[name] * factor).astype(out[name].dtype)
    return out
```

```python
from contextlib import ExitStack

import concourse.bass as bass
from concourse import mybir

ALU = mybir.AluOpType
ACT = mybir.ActivationFunctionType
F32 = mybir.dt.float32
F32R = mybir.dt.float32r
AX_X = mybir.AxisListType.X

P = 128
D = 1024
KT = D // P
SEQ = 1024
RT = SEQ // P
CTX = 256
CT = CTX // P
BANK = 512
EPS = 1e-6
HEADS = 4
DH = 64
DV = 2 * DH
QK = HEADS * 2 * DH
KEYS = CTX + SEQ
KEYT = KEYS // P
ATTN_SCALE = DH ** -0.5
LAMBDA_INIT = 0.2
F_GROUPS = 4
RADIX = 8
HALF_GROUP = 256
ADA = 3 * D
ADA_T = ADA // P
FFN = 2816
FFN_T = FFN // P
WINDOWS = (2, 4, 8, 16)
PAD = 16
GATE_COL = 2048
KV_COL = 1024

NORM_G, ADA_B, ODD_CONV, MIX_G, FFN_G, C_VEC, C_CTX = ((0, o) for o in (0, 16, 64, 88, 96, 104, 112))
POOL_B, POOL_SCALE, FFN_B, FFN_TAP0 = ((1, o) for o in (0, 8, 16, 60))
FFN_TAP1, FFN_TAP2, SUBLN = ((2, o) for o in (0, 44, 88))
ROWS = (120, 104, 89)


def program(nc, a, out):
    ctx = ExitStack()
    with ctx:
        sems = {}

        def sem(name):
            if name not in sems:
                sems[name] = nc.alloc_semaphore(name)
            return sems[name]

        def end_stage():
            nc.clear_and_free_semaphores(list(sems.values()))
            sems.clear()
            nc.all_engine_barrier()

        def sb(stack, name, shape, dt=F32):
            return stack.enter_context(nc.sbuf_tensor(name, shape, dt))

        ps = ctx.enter_context(nc.psum_tensor("ps", [P, 8, BANK], F32))
        pair = [ps[:, 2 * i:2 * i + 2, :].rearrange("p b n -> p (b n)") for i in range(4)]

        ident = sb(ctx, "ident", [P, P])
        ones = sb(ctx, "ones", [P, P])
        eps = sb(ctx, "eps", [P, 1])
        cols = sb(ctx, "cols", [P, 3, P])
        ada_col = sb(ctx, "ada_col", [P, 2, ADA_T, 2])
        mod_gain = sb(ctx, "mod_gain", [P, 3, KT])
        neg_lam = sb(ctx, "neg_lam", [P, 1])
        residual = sb(ctx, "residual", [P, KEYT, D])
        fq_stack = ExitStack()
        fq = sb(fq_stack, "fq", [P, 2, RT, QK])

        x_scratch = nc.dram_tensor("x_scratch", [KT, P, SEQ], F32).ap()
        gate_scratch = nc.dram_tensor("gate_scratch", [KT, P, SEQ], F32).ap()

        def col(where, j):
            return cols[:, where[0], where[1] + j:where[1] + j + 1]

        def matmul3(pe, psum, w_hi, w_lo, a_hi, a_lo, n_k, n):
            for k in range(n_k):
                for w, act in ((w_hi, a_hi), (w_hi, a_lo), (w_lo, a_hi)):
                    for c in range(0, n, BANK):
                        e = min(c + BANK, n)
                        last = pe.matmul(psum[:, c:e], w(k), act(k, c, e), start=(k == 0 and w is w_hi and act is a_hi),
                                         stop=(k == n_k - 1 and w is w_lo))
            return last

        def split_high(act, dst, src, done):
            return act.activation(dst, src, ACT.Copy).then_inc(done, 1)

        def split_low(eng, dst, src, high, done):
            return eng.tensor_tensor(dst, src, high.bitcast(F32), ALU.subtract).then_inc(done, 1)

        class Norm:
            def __init__(self, stack, tag, x, n, gain, shift, high, low, plain=None):
                self.tag, self.x, self.n, self.gain, self.shift = tag, x, n, gain, shift
                self.high, self.low, self.plain = high, low, plain
                self.square = sb(stack, tag + "_square", [P, 2, n])
                self.total = sb(stack, tag + "_total", [P, n])
                self.rstd = sb(stack, tag + "_rstd", [P, n])
                self.scaled = sb(stack, tag + "_scaled", [P, 2, n]) if plain is None else None

            def s(self, what):
                return sem(self.tag + "_" + what)

            def scalar_squares(self, act):
                for k in range(KT):
                    if k == 0:
                        dst = self.total[:, :]
                    else:
                        dst = self.square[:, k % 2, :]
                        if k >= 3:
                            act.wait_ge(self.s("summed"), k - 2)
                    act.activation(dst, self.x(k), ACT.Square).then_inc(self.s("squared"), 1)
                act.wait_ge(self.s("meaned"), 1)
                act.activation(self.rstd[:, :], pair[0][:, 0:self.n], ACT.Sqrt, bias=eps[:, 0:1], scale=1.0 / D)\
                   .then_inc(self.s("rooted"), 1)

            def scalar_highs(self, act):
                for k in range(KT):
                    act.wait_ge(self.s("scaled"), k + 1)
                    act.activation(self.high(k), self.scaled[:, k % 2, :], ACT.Identity, bias=self.shift(k))\
                       .then_inc(self.s("high"), 1)

            def vector(self, dve):
                for k in range(1, KT):
                    dve.wait_ge(self.s("squared"), k + 1)
                    if k > 1:
                        dve.wait_ge(self.s("summed"), k - 1)
                    dve.tensor_tensor(self.total[:, :], self.total[:, :], self.square[:, k % 2, :], ALU.add)\
                       .then_inc(self.s("summed"), 1)
                dve.wait_ge(self.s("rooted"), 1)
                dve.reciprocal(self.rstd[:, :], self.rstd[:, :]).then_inc(self.s("inverse"), 1)
                dve.wait_ge(self.s("inverse"), 1)

                def scale(k):
                    dst = self.plain(k) if self.plain else self.scaled[:, k % 2, :]
                    dve.scalar_tensor_tensor(out=dst, in0=self.x(k), scalar=self.gain(k), in1=self.rstd[:, :],
                                             op0=ALU.mult, op1=ALU.mult).then_inc(self.s("scaled"), 1)

                scale(0)
                for k in range(KT):
                    if k + 1 < KT:
                        if k >= 1 and not self.plain:
                            dve.wait_ge(self.s("low"), k)
                        scale(k + 1)
                    if not self.plain:
                        dve.wait_ge(self.s("high"), k + 1)
                        dve.scalar_tensor_tensor(out=self.low(k), in0=self.scaled[:, k % 2, :], scalar=self.shift(k),
                                                 in1=self.high(k).bitcast(F32), op0=ALU.add, op1=ALU.subtract)\
                           .then_inc(self.s("low"), 1)

            def tensor(self, pe):
                pe.wait_ge(self.s("summed"), KT - 1)
                for c in range(0, self.n, BANK):
                    e = min(c + BANK, self.n)
                    last = pe.matmul(pair[0][:, c:e], ones[:, :], self.total[:, c:e], start=True, stop=True)
                last.then_inc(self.s("meaned"), 1)

        def adaptive_parameters():
            with ExitStack() as st:
                rows = sb(st, "rows", [P, 3, P])
                sel = sb(st, "sel", [P, 2])
                lam_in = sb(st, "lam_in", [P, 4, DH])
                lam_pair = sb(st, "lam_pair", [P, 2, DH])
                lam_dot = sb(st, "lam_dot", [P, 2])
                lam_exp = sb(st, "lam_exp", [P, 2])
                cond = sb(st, "cond", [P, KT, 32])
                ada_raw = sb(st, "ada_raw", [P, 2, ADA])
                ada_sb = sb(st, "ada_sb", [P, ADA // BANK, BANK])
                ctx_t = ctx_xt
                x_t = fq[:, :, :, :].rearrange("p a b n -> p (a b n)").rearrange("p (k n) -> p k n", k=KT)
                nat = residual
                row_sources = [
                    (0, NORM_G[1], a["norm_g"].rearrange("l (k p) -> (l k) p", p=P)),
                    (0, ADA_B[1], a["ada_b"].rearrange("l (k p) -> (l k) p", p=P)),
                    (0, ODD_CONV[1], a["odd_conv_w"].rearrange("a t (k p) -> (a t k) p", p=P)),
                    (0, MIX_G[1], a["norm_mix_g_2"].rearrange("a (k p) -> (a k) p", p=P)),
                    (0, FFN_G[1], a["norm_ffn_g_2"].rearrange("a (k p) -> (a k) p", p=P)),
                    (0, C_VEC[1], a["c"].rearrange("a (k p) -> (a k) p", p=P)),
                    (0, C_CTX[1], a["c_ctx"].rearrange("(k p) -> k p", p=P)),
                    (1, POOL_B[1], a["pool_b_2"].rearrange("a (k p) -> (a k) p", p=P)),
                    (1, POOL_SCALE[1], a["pool_scale_2"].rearrange("a (k p) -> (a k) p", p=P)),
                    (1, FFN_B[1], a["ffn_conv_b_2"].rearrange("a (k p) -> (a k) p", p=P)),
                    (1, FFN_TAP0[1], a["ffn_conv_w_2"][0, 0:1, :].rearrange("a (k p) -> (a k) p", p=P)),
                    (2, FFN_TAP1[1], a["ffn_conv_w_2"][0, 1:3, :].rearrange("a (k p) -> (a k) p", p=P)),
                    (2, SUBLN[1], a["even_subln"]),
                ]
                x_rows = a["x"].rearrange("b (r p) d -> p (b r) d", p=P)
                ctx_rows = a["ctx"].rearrange("b (r p) d -> p (b r) d", p=P)

                with nc.Block(name="ada") as block:
                    @block.sync
                    def _(sp):
                        sp.dma_start(ident[:, :], a["identity"]).then_inc(sem("rows_in"), 16)
                        for t, r, src in row_sources:
                            sp.dma_start(rows[r:r + src.shape[0], t, :], src).then_inc(sem("rows_in"), 16)
                        sp.dma_start(nat[:, 0:4, :], x_rows[:, 0:4, :]).then_inc(sem("x_in_lo"), 16)
                        sp.dma_start(nat[:, 4:8, :], x_rows[:, 4:8, :]).then_inc(sem("x_in_hi"), 16)
                        sp.dma_start(nat[:, RT:KEYT, :], ctx_rows).then_inc(sem("ctx_in"), 16)
                        sp.dma_start(sel[:, :], a["selector"]).then_inc(sem("sel_in"), 16)
                        for n, name in enumerate(("even_lambda_q1", "even_lambda_k1", "even_lambda_q2", "even_lambda_k2")):
                            sp.dma_start(lam_in[:, n, :], a[name].broadcast_to([P, DH])).then_inc(sem("lam_in"), 16)
                        for l in range(2):
                            for k in range(KT):
                                n = l * KT + k
                                if n >= 2:
                                    sp.wait_ge(sem("ada_used"), n - 1)
                                sp.dma_start(ada_raw[:, n % 2, :], a["ada_w"][l, k * P:(k + 1) * P, :])\
                                  .then_inc(sem(f"ada_in{n % 2}"), 16)
                        for k in range(KT):
                            sp.wait_ge(sem("xt_copied"), k + 1)
                            sp.dma_start(x_scratch[k], x_t[:, k, :]).then_inc(sem("x_spilled"), 16)
                        sp.wait_ge(sem("x_spilled"), 16 * KT)

                    @block.tensor
                    def _(pe):
                        pe.wait_ge(sem("rows_in"), 16 * (1 + len(row_sources)))
                        for t in range(3):
                            last = pe.transpose(ps[:, 7, t * P:t * P + ROWS[t]], rows[0:ROWS[t], t, :],
                                                ident[0:ROWS[t], 0:ROWS[t]])
                        last.then_inc(sem("rows_turned"), 1)
                        pe.wait_ge(sem("x_in_lo"), 16)
                        pe.wait_ge(sem("x_in_hi"), 16)
                        for k in range(KT):
                            if k >= 2:
                                pe.wait_ge(sem("xt_copied"), k - 1)
                            for r in range(RT):
                                last = pe.transpose(pair[k % 2][:, r * P:(r + 1) * P], nat[:, r, k * P:(k + 1) * P],
                                                    ident[:, :])
                            last.then_inc(sem("xt_turned"), 1)
                        pe.wait_ge(sem("ctx_in"), 16)
                        for k in range(0, KT, 4):
                            for i in range(4):
                                for r in range(CT):
                                    last = pe.transpose(pair[2][:, (i * CT + r) * P:(i * CT + r + 1) * P],
                                                        nat[:, RT + r, (k + i) * P:(k + i + 1) * P], ident[:, :])
                            last.then_inc(sem("ct_turned"), 1)
                            pe.wait_ge(sem("ct_copied"), k // 4 + 1)
                        pe.wait_ge(sem("cond_ready"), 1)
                        pe.wait_ge(sem("xt_copied"), KT)
                        for l in range(2):
                            if l:
                                pe.wait_ge(sem("ada_rows"), 1)
                            for k in range(KT):
                                n = l * KT + k
                                pe.wait_ge(sem(f"ada_in{n % 2}"), 16 * (n // 2 + 1))
                                for m in range(ADA // BANK):
                                    j = 32 * (m % 4)
                                    last = pe.matmul(ps[j:j + 32, m, :], cond[:, k, :],
                                                     ada_raw[:, n % 2, m * BANK:(m + 1) * BANK],
                                                     start=(k == 0), stop=(k == KT - 1))
                                last.then_inc(sem("ada_used"), 1)
                            pe.wait_ge(sem("ada_rows"), l + 1)
                            pe.wait_ge(sem("sel_in"), 16)
                            for t in range(ADA_T):
                                m, j = t // 4, 32 * (t // 4 % 4)
                                last = pe.matmul(ps[:, m % 4, 2 * t:2 * t + 2],
                                                 ada_sb[j:j + 32, m, (t % 4) * P:(t % 4 + 1) * P], sel[j:j + 32, :],
                                                 start=True, stop=True)
                            last.then_inc(sem("ada_turned"), 1)
                            pe.wait_ge(sem("ada_cols"), l + 1)

                    @block.scalar
                    def _(act):
                        act.wait_ge(sem("cols_copied"), 3)
                        act.wait_ge(sem("cond_zero"), 1)
                        for v, vec in enumerate((C_VEC, C_CTX)):
                            last = act.activation(cond[:, :, v], cols[:, vec[0], vec[1]:vec[1] + KT], ACT.Silu)
                        last.then_inc(sem("cond_ready"), 1)
                        for k in range(KT):
                            act.wait_ge(sem("xt_turned"), k + 1)
                            act.activation(x_t[:, k, :], pair[k % 2], ACT.Copy).then_inc(sem("xt_copied"), 1)
                        for k in range(0, KT, 4):
                            act.wait_ge(sem("ct_turned"), k // 4 + 1)
                            act.activation(ctx_t[:, k:k + 4, :].rearrange("p k n -> p (k n)"), pair[2], ACT.Copy)\
                               .then_inc(sem("ct_copied"), 1)
                        act.wait_ge(sem("lam_dots"), 2)
                        act.activation(lam_exp[:, :], lam_dot[:, :], ACT.Exp).then_inc(sem("lam_exped"), 1)

                    @block.vector
                    def _(dve):
                        dve.memset(ones[:, :], 1.0)
                        dve.memset(eps[:, :], EPS)
                        dve.memset(cond[:, :, :], 0.0).then_inc(sem("cond_zero"), 1)
                        dve.wait_ge(sem("rows_turned"), 1)
                        for t in range(3):
                            dve.tensor_copy(cols[:, t, 0:ROWS[t]], ps[:, 7, t * P:t * P + ROWS[t]])\
                               .then_inc(sem("cols_copied"), 1)
                        dve.wait_ge(sem("lam_in"), 64)
                        for n in range(2):
                            dve.tensor_tensor(lam_pair[:, n, :], lam_in[:, 2 * n, :], lam_in[:, 2 * n + 1, :], ALU.mult)\
                               .then_inc(sem("lam_pairs"), 1)
                        dve.wait_ge(sem("lam_pairs"), 2)
                        for n in range(2):
                            dve.tensor_reduce(lam_dot[:, n:n + 1], lam_pair[:, n, :], AX_X, ALU.add)\
                               .then_inc(sem("lam_dots"), 1)
                        dve.wait_ge(sem("lam_exped"), 1)
                        dve.tensor_tensor(lam_dot[:, 0:1], lam_exp[:, 1:2], lam_exp[:, 0:1], ALU.subtract)\
                           .then_inc(sem("lam_diff"), 1)
                        dve.wait_ge(sem("lam_diff"), 1)
                        dve.tensor_scalar(neg_lam[:, :], lam_dot[:, 0:1], -LAMBDA_INIT, None, ALU.add)
                        for l in range(2):
                            dve.wait_ge(sem("ada_used"), KT * (l + 1))
                            for m in range(ADA // BANK):
                                j = 32 * (m % 4)
                                last = dve.tensor_copy(ada_sb[j:j + 32, m, :], ps[j:j + 32, m, :])
                            last.then_inc(sem("ada_rows"), 1)
                            dve.wait_ge(sem("ada_turned"), l + 1)
                            for m in range(ADA // BANK):
                                b = ADA_B[1] + l * ADA_T + 4 * m
                                last = dve.tensor_tensor(
                                    ada_col[:, l, 4 * m:4 * m + 4, :],
                                    ps[:, m % 4, 8 * m:8 * m + 8].rearrange("p (t v) -> p t v", v=2),
                                    cols[:, ADA_B[0], b:b + 4].unsqueeze(2).broadcast_to([P, 4, 2]), ALU.add)
                            last.then_inc(sem("ada_cols"), 1)
                        dve.wait_ge(sem("ada_cols"), 2)
                        for n, (l, v) in enumerate(((0, 0), (0, 1), (1, 0))):
                            dve.scalar_tensor_tensor(
                                out=mod_gain[:, n, :], in0=ada_col[:, l, KT:2 * KT, v], scalar=1.0,
                                in1=cols[:, NORM_G[0], NORM_G[1] + l * KT:NORM_G[1] + (l + 1) * KT],
                                op0=ALU.add, op1=ALU.mult)

        def gain_col(n):
            return lambda k: mod_gain[:, n, k:k + 1]

        def shift_col(l, v):
            return lambda k: ada_col[:, l, k, v:v + 1]

        h_stack = ExitStack()
        ctx_xt = residual[:, 0:CT, :].rearrange("p r n -> p (r n)").rearrange("p (k n) -> p k n", k=KT)
        adaptive_parameters()
        h_hi = sb(h_stack, "h_hi", [P, KT, SEQ], F32R)
        h_lo = sb(h_stack, "h_lo", [P, KT, SEQ], F32R)
        hc_hi = sb(h_stack, "hc_hi", [P, KT, CTX], F32R)
        hc_lo = sb(h_stack, "hc_lo", [P, KT, CTX], F32R)
        x_t = fq[:, :, :, :].rearrange("p a b n -> p (a b n)").rearrange("p (k n) -> p k n", k=KT)

        def run_norms(norms, name):
            with nc.Block(name=name) as block:
                @block.scalar
                def _(act):
                    for n in norms:
                        n.scalar_squares(act)
                        if not n.plain:
                            n.scalar_highs(act)

                @block.vector
                def _(dve):
                    for n in norms:
                        n.vector(dve)

                @block.tensor
                def _(pe):
                    for n in norms:
                        n.tensor(pe)

        with ExitStack() as st:
            norm_c = Norm(st, "norm0c", lambda k: ctx_xt[:, k, :], CTX, gain_col(1), shift_col(0, 1),
                          lambda k: hc_hi[:, k, :], lambda k: hc_lo[:, k, :])
            run_norms([norm_c], "norm0c")
        with ExitStack() as st:
            norm_x = Norm(st, "norm0", lambda k: x_t[:, k, :], SEQ, gain_col(0), shift_col(0, 0),
                          lambda k: h_hi[:, k, :], lambda k: h_lo[:, k, :])
            run_norms([norm_x], "norm0")
        end_stage()

        kv = residual[:, :, :].rearrange("p r n -> p (r n)").rearrange("p (g t n) -> p g t n", g=2, t=KEYT)
        w_in = a["even_w_in"].rearrange("e (k p) n -> p (e k) n", p=P)

        def even_projections():
            with ExitStack() as st:
                raw = sb(st, "in_raw", [P, KT, HALF_GROUP])
                w_hi = sb(st, "in_hi", [P, 2, KT, HALF_GROUP], F32R)
                w_lo = sb(st, "in_lo", [P, 2, KT, HALF_GROUP], F32R)
                gate = sb(st, "gate", [P, 2, SEQ])
                g_raw = raw[:, :, :].rearrange("p k n -> p (k n)").rearrange("p (s k n) -> p s k n", s=2, k=KT)
                g_hi, g_lo = (w[:, :, :, :].rearrange("p s k n -> p (s k n)").rearrange("p (s k n) -> p s k n", s=4, k=KT)
                              for w in (w_hi, w_lo))
                N_UNITS = 8
                tiles_of = [KEYT if u < 4 else RT for u in range(N_UNITS)]
                first_tile = [sum(tiles_of[:u]) for u in range(N_UNITS + 1)]

                with nc.Block(name="even_in") as block:
                    @block.sync
                    def _(sp):
                        for u in range(N_UNITS):
                            c = (KV_COL + HALF_GROUP * u) if u < 4 else HALF_GROUP * (u - 4)
                            if u >= 1:
                                sp.wait_ge(sem("in_low"), u)
                            sp.dma_start(raw[:, :, :], w_in[:, :, c:c + HALF_GROUP]).then_inc(sem("in_landed"), 16)
                        sp.wait_ge(sem("in_low"), N_UNITS)
                        for m in range(KT + 2):
                            if 2 <= m < KT:
                                sp.wait_ge(sem("gw_low"), m - 1)
                            if m < KT:
                                c = GATE_COL + m * P
                                sp.dma_start(g_raw[:, m % 2], w_in[:, :, c:c + P]).then_inc(sem(f"gw_landed{m % 2}"), 16)
                            if m >= 2:
                                sp.wait_ge(sem("gate_ready"), m - 1)
                                sp.dma_start(gate_scratch[m - 2], gate[:, m % 2, :]).then_inc(sem(f"gate_spilled{m % 2}"), 16)
                        for s in range(2):
                            sp.wait_ge(sem(f"gate_spilled{s}"), 16 * KT // 2)

                    @block.scalar
                    def _(act):
                        def high(u):
                            act.wait_ge(sem("in_landed"), 16 * (u + 1))
                            if u >= 2:
                                act.wait_ge(sem("in_done"), first_tile[u - 1])
                            split_high(act, w_hi[:, u % 2], raw[:, :, :], sem("in_high"))

                        def g_high(m):
                            act.wait_ge(sem(f"gw_landed{m % 2}"), 16 * (m // 2 + 1))
                            if m >= 2:
                                act.wait_ge(sem("gw_done"), m - 1)
                            else:
                                act.wait_ge(sem("in_done"), first_tile[7])
                            split_high(act, g_hi[:, m % 2], g_raw[:, m % 2], sem("gw_high"))

                        high(0)
                        for u in range(N_UNITS):
                            if u + 1 < N_UNITS:
                                high(u + 1)
                            if u == N_UNITS - 1:
                                g_high(0)
                                g_high(1)
                            half = HALF_GROUP * (u % 2)
                            for i in range(tiles_of[u]):
                                n = first_tile[u] + i
                                act.wait_ge(sem("in_done"), n + 1)
                                if u < 4:
                                    dst = kv[:, u // 2, i, half:half + HALF_GROUP]
                                else:
                                    dst = fq[:, (u - 4) // 2, i, half:half + HALF_GROUP]
                                act.activation(dst, ps[:, n % 4, 0:HALF_GROUP], ACT.Copy).then_inc(sem("in_copied"), 1)
                        for m in range(KT):
                            act.wait_ge(sem("gw_done"), m + 1)
                            if m >= 2:
                                act.wait_ge(sem(f"gate_spilled{m % 2}"), 16 * (m // 2))
                            act.activation(gate[:, m % 2, :], pair[2 + m % 2], ACT.Silu).then_inc(sem("gate_ready"), 1)
                            if m + 2 < KT:
                                g_high(m + 2)

                    @block.gpsimd
                    def _(pool):
                        for u in range(N_UNITS):
                            pool.wait_ge(sem("in_high"), u + 1)
                            if u >= 2:
                                pool.wait_ge(sem("in_done"), first_tile[u - 1])
                            split_low(pool, w_lo[:, u % 2], raw[:, :, :], w_hi[:, u % 2], sem("in_low"))
                        for m in range(KT):
                            pool.wait_ge(sem("gw_high"), m + 1)
                            split_low(pool, g_lo[:, m % 2], g_raw[:, m % 2], g_hi[:, m % 2], sem("gw_low"))

                    @block.tensor
                    def _(pe):
                        for u in range(N_UNITS):
                            pe.wait_ge(sem("in_low"), u + 1)
                            for i in range(tiles_of[u]):
                                n = first_tile[u] + i
                                if n >= 4:
                                    pe.wait_ge(sem("in_copied"), n - 3)
                                ctx_tile = u < 4 and i < CT
                                r = i if (u >= 4 or ctx_tile) else i - CT
                                hi, lo = (hc_hi, hc_lo) if ctx_tile else (h_hi, h_lo)
                                for k in range(KT):
                                    for x, w in ((hi, w_hi), (hi, w_lo), (lo, w_hi)):
                                        last = pe.matmul(ps[:, n % 4, 0:HALF_GROUP], x[:, k, r * P:(r + 1) * P],
                                                         w[:, u % 2, k, :], start=(k == 0 and x is hi and w is w_hi),
                                                         stop=(k == KT - 1 and x is lo))
                                last.then_inc(sem("in_done"), 1)
                        for m in range(KT):
                            pe.wait_ge(sem("gw_low"), m + 1)
                            if m >= 2:
                                pe.wait_ge(sem("gate_ready"), m - 1)
                            matmul3(pe, pair[2 + m % 2], lambda k: g_hi[:, m % 2, k, :], lambda k: g_lo[:, m % 2, k, :],
                                    lambda k, c, e: h_hi[:, k, c:e], lambda k, c, e: h_lo[:, k, c:e], KT, SEQ)\
                                .then_inc(sem("gw_done"), 1)

        even_projections()
        end_stage()
        h_stack.close()

        def fourier_and_rotation():
            with ExitStack() as st:
                z = sb(st, "z", [P, RADIX, BANK])
                even = sb(st, "even", [P, 4, BANK])
                odd = sb(st, "odd", [P, 4, BANK])
                tables = sb(st, "tables", [P, RADIX, 2, 2 * P])
                channel_dft = sb(st, "channel_dft", [P, 2, P])
                ft = sb(st, "ft", [P, 2, RADIX, 2, P])
                cos = sb(st, "cos", [P, RT, 2, 16])
                sin = sb(st, "sin", [P, RT, 2, 16])
                gains = sb(st, "qk_gains", [P, 2, DH])
                sq = sb(st, "sq", [P, KEYT * QK])
                stat = sb(st, "stat", [P, KEYT * 8])
                turn = sb(st, "turn", [P, 2, 4, RT * 8 * 16])
                u = fq[:, 0]
                k_nat, q_nat = kv[:, 0], fq[:, 1]
                y_f = fq[:, 0].rearrange("p r n -> p (r n)").rearrange("p (g n) -> p g n", g=F_GROUPS)
                ROOT = 0.5 ** 0.5

                with nc.Block(name="fourier") as block:
                    @block.sync
                    def _(sp):
                        sp.dma_start(tables[:, :, :, :], a["seq_dft"]).then_inc(sem("tables_in"), 16)
                        sp.dma_start(channel_dft[:, :, :], a["channel_dft"]).then_inc(sem("tables_in"), 16)
                        for tile, name in ((cos, "rope_cos"), (sin, "rope_sin")):
                            sp.dma_start(tile[:, :, :, :], a[name].rearrange("(r p) c f -> p r c f", p=P))\
                              .then_inc(sem("rope_in"), 16)
                        for n, name in enumerate(("even_k_norm", "even_q_norm")):
                            sp.dma_start(gains[:, n, :], a[name].broadcast_to([P, DH])).then_inc(sem("rope_in"), 16)

                    @block.vector
                    def _(dve):
                        fs = sem("fold_step")
                        count = [0]

                        def step(instruction):
                            instruction.then_inc(fs, 1)
                            count[0] += 1
                            return count[0]

                        for i in range(4):
                            step(dve.tensor_tensor(even[:, i], u[:, i], u[:, i + 4], ALU.add))
                            step(dve.tensor_tensor(odd[:, i], u[:, i], u[:, i + 4], ALU.subtract))
                        dve.wait_ge(fs, count[0])
                        step(dve.tensor_tensor(z[:, 2], even[:, 0], even[:, 2], ALU.subtract))
                        step(dve.tensor_tensor(z[:, 6], even[:, 3], even[:, 1], ALU.subtract))
                        step(dve.tensor_tensor(z[:, 0], even[:, 0], even[:, 2], ALU.add))
                        step(dve.tensor_tensor(z[:, 4], even[:, 1], even[:, 3], ALU.add))
                        step(dve.tensor_tensor(z[:, 1], odd[:, 1], odd[:, 3], ALU.subtract))
                        step(dve.tensor_tensor(z[:, 5], odd[:, 1], odd[:, 3], ALU.add))
                        dve.wait_ge(fs, count[0])
                        step(dve.tensor_tensor(even[:, 0], z[:, 0], z[:, 4], ALU.add))
                        step(dve.tensor_tensor(even[:, 1], z[:, 0], z[:, 4], ALU.subtract))
                        for s, d, src, base, op in ((ROOT, even[:, 2], z[:, 1], odd[:, 0], ALU.add),
                                                    (-ROOT, z[:, 3], z[:, 1], odd[:, 0], ALU.add),
                                                    (-ROOT, even[:, 3], z[:, 5], odd[:, 2], ALU.subtract),
                                                    (-ROOT, z[:, 7], z[:, 5], odd[:, 2], ALU.add)):
                            step(dve.scalar_tensor_tensor(out=d, in0=src, scalar=s, in1=base, op0=ALU.mult, op1=op))
                        dve.wait_ge(fs, count[0])
                        step(dve.tensor_copy(z[:, 0], even[:, 0]))
                        step(dve.tensor_copy(z[:, 4], even[:, 1]))
                        step(dve.tensor_copy(z[:, 1], even[:, 2]))
                        dve.tensor_copy(z[:, 5], even[:, 3]).then_inc(sem("folded"), 1)

                        rs = sem("rot_step")
                        n_rs = [0]

                        def rot(instruction):
                            instruction.then_inc(rs, 1)
                            n_rs[0] += 1

                        dve.wait_ge(sem("rope_in"), 64)
                        for n, (nat, t) in enumerate(((k_nat, KEYT), (q_nat, RT))):
                            flat = nat.rearrange("p t n -> p (t n)")
                            heads = flat.rearrange("p (h d) -> p h d", d=DH)
                            if n:
                                dve.wait_ge(rs, n_rs[0])
                            rot(dve.tensor_tensor(sq[:, 0:t * QK], flat, flat, ALU.mult))
                            dve.wait_ge(rs, n_rs[0])
                            dve.tensor_reduce(stat[:, 0:t * 8], sq[:, 0:t * QK].rearrange("p (h d) -> p h d", d=DH),
                                              AX_X, ALU.add).then_inc(sem("qk_summed"), 1)
                            dve.wait_ge(sem("qk_rooted"), n + 1)
                            rot(dve.reciprocal(stat[:, 0:t * 8], stat[:, 0:t * 8]))
                            dve.wait_ge(rs, n_rs[0])
                            rot(dve.tensor_tensor(heads, heads, stat[:, 0:t * 8].unsqueeze(2).broadcast_to([P, t * 8, DH]),
                                                  ALU.mult))
                            dve.wait_ge(rs, n_rs[0])
                            rot(dve.tensor_tensor(heads, heads, gains[:, n:n + 1, :].broadcast_to([P, t * 8, DH]), ALU.mult))
                            dve.wait_ge(rs, n_rs[0])
                            x_rows = nat[:, t - RT:t, :].rearrange("p t (h c j f) -> p t h c j f", c=2, j=2, f=16)
                            for half in range(2):
                                x1, x2 = x_rows[:, :, :, half, 0, :], x_rows[:, :, :, half, 1, :]
                                cs, sn = (tab[:, :, half, :].unsqueeze(2).broadcast_to([P, RT, 8, 16]) for tab in (cos, sin))
                                b = [turn[:, half, i, :].rearrange("p (t h f) -> p t h f", t=RT, h=8) for i in range(4)]
                                for dst, x, tab in ((b[0], x1, cs), (b[1], x2, sn), (b[2], x1, sn), (b[3], x2, cs)):
                                    rot(dve.tensor_tensor(dst, x, tab, ALU.mult))
                                dve.wait_ge(rs, n_rs[0])
                                rot(dve.tensor_tensor(x1, b[0], b[1], ALU.subtract))
                                rot(dve.tensor_tensor(x2, b[2], b[3], ALU.add))

                    @block.tensor
                    def _(pe):
                        pe.wait_ge(sem("folded"), 1)
                        pe.wait_ge(sem("tables_in"), 32)
                        for g in range(F_GROUPS):
                            for k1 in range(RADIX):
                                n = g * RADIX + k1
                                if n >= 4:
                                    pe.wait_ge(sem("ft_copied"), n - 3)
                                m = min(k1, RADIX - k1)
                                bank = ps[:, n % 4, 0:2 * P]
                                complex_part = m not in (0, 4)
                                last = pe.matmul(bank, z[:, m, g * P:(g + 1) * P], tables[:, k1, 0, :], start=True,
                                                 stop=not complex_part)
                                if complex_part:
                                    last = pe.matmul(bank, z[:, m + 4, g * P:(g + 1) * P], tables[:, k1, 1, :],
                                                     start=False, stop=True)
                                last.then_inc(sem("ft_done"), 1)
                            pe.wait_ge(sem("ft_copied"), (g + 1) * RADIX)
                            if g >= 2:
                                pe.wait_ge(sem("y_f_copied"), g - 1)
                            for half in range(2):
                                for part in range(2):
                                    last = pe.matmul(pair[2 + g % 2][:, half * BANK:(half + 1) * BANK],
                                                     channel_dft[:, part, :], ft[:, g % 2, 4 * half:4 * half + 4, part, :],
                                                     start=(part == 0), stop=(part == 1))
                            last.then_inc(sem("y_f_done"), 1)

                    @block.scalar
                    def _(act):
                        def root(n):
                            act.wait_ge(sem("qk_summed"), n + 1)
                            t = KEYT if n == 0 else RT
                            act.activation(stat[:, 0:t * 8], stat[:, 0:t * 8], ACT.Sqrt, bias=eps[:, 0:1], scale=1.0 / DH)\
                               .then_inc(sem("qk_rooted"), 1)

                        for g in range(F_GROUPS):
                            for k1 in range(RADIX):
                                n = g * RADIX + k1
                                act.wait_ge(sem("ft_done"), n + 1)
                                if g >= 2 and k1 == 0:
                                    act.wait_ge(sem("y_f_done"), g - 1)
                                act.activation(ft[:, g % 2, k1, :, :].rearrange("p c n -> p (c n)"), ps[:, n % 4, 0:2 * P],
                                               ACT.Copy).then_inc(sem("ft_copied"), 1)
                            act.wait_ge(sem("y_f_done"), g + 1)
                            act.activation(y_f[:, g, :].rearrange("p (k2 k1) -> p k1 k2", k1=RADIX),
                                           pair[2 + g % 2].rearrange("p (k1 k2) -> p k1 k2", k1=RADIX), ACT.Copy)\
                               .then_inc(sem("y_f_copied"), 1)
                        for n in range(2):
                            root(n)

        fourier_and_rotation()
        end_stage()

        def attention():
            with ExitStack() as st:
                k_parts = sb(st, "k_parts", [P, KEYT, 2, 4, DH], F32R)
                q_parts = sb(st, "q_parts", [P, RT, 2, 2, DH], F32R)
                k_turned = sb(st, "k_turned", [P, 2, 2, KEYS], F32R)
                q_turned = sb(st, "q_turned", [P, 2, SEQ], F32R)
                prob = sb(st, "prob", [P, 2, 2, KEYS])
                mixed = sb(st, "mixed", [P, 2, KEYS])
                mixed_t = sb(st, "mixed_t", [P, 2, KEYS])
                v_head = sb(st, "v_head", [P, KEYT, DV])
                o_all = sb(st, "o_all", [P, HEADS, RT, DV])
                o_sq = prob[:, :, :, :].rearrange("p b m n -> p (b m n)")[:, 0:HEADS * RT * DV]
                o_stat = sb(st, "o_stat", [P, HEADS * RT])
                peak = sb(st, "peak", [P, RT, 2])
                neg_peak = sb(st, "neg_peak", [P, RT, 2])
                total = sb(st, "total", [P, RT, 2])
                inverse = sb(st, "inverse", [P, RT, 2])
                weight = sb(st, "weight", [P, RT])
                subln_gain = sb(st, "subln_gain", [P, 1])
                k_nat, v_nat, q_nat = kv[:, 0], kv[:, 1], fq[:, 1]
                ao_t = fq[:, 1].rearrange("p r n -> p (r n)").rearrange("p (h n) -> p h n", h=HEADS)
                score = [ps[:, 3 * m:3 * m + 3, :].rearrange("p b n -> p (b n)")[:, 0:KEYS] for m in range(2)]
                SPLIT, COMBINE = 1, 2
                chunks = [(k_turned[:, m, part, t * P:min(t + 4, KEYT) * P], [k_parts[:, i, m, 2 * part:2 * part + 2, :]
                           for i in range(t, min(t + 4, KEYT))]) for m in range(2) for part in range(2)
                          for t in range(0, KEYT, 4)]
                chunks += [(q_turned[:, m, t * P:(t + 4) * P], [q_parts[:, i, m, :, :] for i in range(t, t + 4)])
                           for m in range(2) for t in range(0, RT, 4)]
                NC = len(chunks)
                rounds = [(t, min(t + 4, KEYT)) for t in range(0, KEYT, 4)]
                NR = len(rounds)

                with nc.Block(name="attention") as block:
                    @block.scalar
                    def _(act):
                        with act.Fori(0, HEADS) as h:
                            hd = bass.ds(h * DV, DV)
                            k_src = k_nat[:, :, hd].rearrange("p t (m d) -> p t m d", m=2)
                            q_src = q_nat[:, :, hd].rearrange("p t (m d) -> p t m d", m=2)
                            act.wait_ge(sem("head_start"), h + 1)
                            act.activation(k_parts[:, :, :, 0, :], k_src, ACT.Copy).then_inc(sem("k_high"), 1)
                            act.activation(q_parts[:, :, :, 0, :], q_src, ACT.Copy).then_inc(sem("q_high"), 1)
                            act.activation(v_head[:, :, :], v_nat[:, :, hd], ACT.Copy).then_inc(sem("v_ready"), 1)
                            for c in range(0, NC, 2):
                                act.wait_ge(sem("part_turned"), h * NC + c + 1)
                                act.activation(chunks[c][0], ps[:, c % 8, 0:len(chunks[c][1]) * P], ACT.Copy)\
                                   .then_inc(sem("part_copied_act"), 1)

                            def turn_out(t, i):
                                b, e = rounds[i]
                                act.wait_ge(sem("mix_turned"), h * RT * NR + t * NR + i + 1)
                                if i == 0 and t >= 2:
                                    act.wait_ge(sem("o_done"), h * RT + t - 1)
                                act.activation(mixed_t[:, t % 2, b * P:e * P], ps[:, 6, 0:(e - b) * P], ACT.Copy)\
                                   .then_inc(sem(f"mix_copied{i}"), 1)

                            for t in range(RT):
                                if t >= 1:
                                    turn_out(t - 1, 0)
                                for m in range(2):
                                    act.wait_ge(sem("peaked"), h * 2 * RT + 2 * t + m + 1)
                                    if t >= 2 and m == 0:
                                        act.wait_ge(sem("mixed"), h * RT + t - 1)
                                    act.activation(prob[:, t % 2, m, :], score[m], ACT.Exp, bias=neg_peak[:, t, m:m + 1],
                                                   scale=ATTN_SCALE, accum_out=total[:, t, m:m + 1]).then_inc(sem("exped"), 1)
                                if t >= 1:
                                    turn_out(t - 1, 2)
                            turn_out(RT - 1, 0)
                            turn_out(RT - 1, 2)
                        act.wait_ge(sem("o_squared"), 1)
                        act.activation(o_stat[:, :], o_stat[:, :], ACT.Sqrt, bias=eps[:, 0:1], scale=1.0 / DV)\
                           .then_inc(sem("o_rooted"), 1)
                        for c in range(HEADS * RT // 4):
                            act.wait_ge(sem("o_turned"), c + 1)
                            act.activation(ao_t[:, c // 2, (c % 2) * BANK:(c % 2 + 1) * BANK], ps[:, c, :], ACT.Copy,
                                           scale=subln_gain[:, 0:1])

                    @block.vector
                    def _(dve):
                        dve.tensor_scalar(subln_gain[:, :], col(SUBLN, 0), 1.0 - LAMBDA_INIT, None, ALU.mult)
                        dve.sem_inc(sem("head_start"), 1)
                        with dve.Fori(0, HEADS) as h:
                            hd = bass.ds(h * DV, DV)
                            k_src = k_nat[:, :, hd].rearrange("p t (m d) -> p t m d", m=2)
                            q_src = q_nat[:, :, hd].rearrange("p t (m d) -> p t m d", m=2)
                            dve.wait_ge(sem("k_high"), h + 1)
                            for m in range(2):
                                dve.tensor_tensor(k_parts[:, :, m, 2, :], k_src[:, :, m, :], k_parts[:, :, m, 0, :].bitcast(F32),
                                                  ALU.subtract).then_inc(sem("k_low"), 1)
                            dve.wait_ge(sem("q_high"), h + 1)
                            for m in range(2):
                                dve.tensor_tensor(q_parts[:, :, m, 1, :], q_src[:, :, m, :], q_parts[:, :, m, 0, :].bitcast(F32),
                                                  ALU.subtract).then_inc(sem("q_low"), 1)
                            dve.wait_ge(sem("k_low"), h * 2 + 2)
                            for m in range(2):
                                for part in range(2):
                                    dve.tensor_copy(k_parts[:, :, m, 2 * part + 1, :],
                                                    k_parts[:, :, m, 2 * part, :].bitcast(F32)).then_inc(sem("k_twice"), 1)
                            for c in range(1, NC, 2):
                                dve.wait_ge(sem("part_turned"), h * NC + c + 1)
                                dve.tensor_copy(chunks[c][0], ps[:, c % 8, 0:len(chunks[c][1]) * P])\
                                   .then_inc(sem("part_copied_dve"), 1)

                            def combine(t):
                                dve.wait_ge(sem("exped"), h * 2 * RT + 2 * t + 2)
                                dve.reciprocal(inverse[:, t, :], total[:, t, :]).then_inc(sem("inverted"), 1)
                                dve.wait_ge(sem("inverted"), h * RT + t + 1)
                                dve.scalar_tensor_tensor(out=weight[:, t:t + 1], in0=total[:, t, 0:1], scalar=neg_lam[:, 0:1],
                                                         in1=inverse[:, t, 1:2], op0=ALU.mult, op1=ALU.mult)\
                                   .then_inc(sem("weighed"), 1)
                                dve.wait_ge(sem("weighed"), h * RT + t + 1)
                                if t >= 2:
                                    dve.wait_ge(sem("mix_turned"), h * RT * NR + (t - 1) * NR)
                                dve.scalar_tensor_tensor(out=mixed[:, t % 2, :], in0=prob[:, t % 2, 1, :],
                                                         scalar=weight[:, t:t + 1], in1=prob[:, t % 2, 0, :],
                                                         op0=ALU.mult, op1=ALU.add).then_inc(sem("mixed"), 1)

                            def finish(t):
                                dve.wait_ge(sem("o_done"), h * RT + t + 1)
                                dst = o_all[:, h, t, :]
                                dve.tensor_scalar(dst, ps[:, 7, (t % 2) * P:(t % 2 + 1) * P], inverse[:, t, 0:1], None, ALU.mult)\
                                   .then_inc(sem("o_scaled"), 1)

                            def turn_out(t):
                                b, e = rounds[1]
                                dve.wait_ge(sem("mix_turned"), h * RT * NR + t * NR + 2)
                                if t >= 2:
                                    dve.wait_ge(sem("o_done"), h * RT + t - 1)
                                dve.tensor_copy(mixed_t[:, t % 2, b * P:e * P], ps[:, 6, 0:(e - b) * P])\
                                   .then_inc(sem("mix_copied1"), 1)

                            for t in range(RT + 2):
                                if 1 <= t <= RT:
                                    combine(t - 1)
                                if t < RT:
                                    for m in range(2):
                                        n = h * 2 * RT + 2 * t + m
                                        dve.wait_ge(sem("scored"), n + 1)
                                        dve.tensor_reduce(peak[:, t, m:m + 1], score[m], AX_X, ALU.max).then_inc(sem("peak"), 1)
                                        dve.wait_ge(sem("peak"), n + 1)
                                        dve.tensor_scalar(neg_peak[:, t, m:m + 1], peak[:, t, m:m + 1], -ATTN_SCALE, None,
                                                          ALU.mult).then_inc(sem("peaked"), 1)
                                if 1 <= t <= RT:
                                    turn_out(t - 1)
                                if t >= 2:
                                    finish(t - 2)
                            dve.wait_ge(sem("o_scaled"), h * RT + RT)
                            dve.sem_inc(sem("head_start"), 1)
                        flat = o_all[:, :, :, :].rearrange("p h t d -> p (h t d)")
                        rows = flat.rearrange("p (n d) -> p n d", d=DV)
                        dve.tensor_tensor(o_sq, flat, flat, ALU.mult).then_inc(sem("o_sq"), 1)
                        dve.wait_ge(sem("o_sq"), 1)
                        dve.tensor_reduce(o_stat[:, :], o_sq.rearrange("p (n d) -> p n d", d=DV), AX_X, ALU.add)\
                           .then_inc(sem("o_squared"), 1)
                        dve.wait_ge(sem("o_rooted"), 1)
                        dve.reciprocal(o_stat[:, :], o_stat[:, :]).then_inc(sem("o_sq"), 1)
                        dve.wait_ge(sem("o_sq"), 2)
                        dve.tensor_tensor(rows, rows, o_stat[:, :].unsqueeze(2).broadcast_to([P, HEADS * RT, DV]), ALU.mult)\
                           .then_inc(sem("o_normed"), 1)

                    @block.tensor
                    def _(pe):
                        with pe.Fori(0, HEADS) as h:
                            pe.wait_ge(sem("k_twice"), h * 4 + 4)
                            pe.wait_ge(sem("q_low"), h * 2 + 2)
                            for c, (_, tiles) in enumerate(chunks):
                                if c >= 8:
                                    pe.wait_ge(sem("part_copied_act" if c % 2 == 0 else "part_copied_dve"),
                                               h * (NC // 2) + (c - 8) // 2 + 1)
                                for i, tile in enumerate(tiles):
                                    last = pe.transpose(ps[:, c % 8, i * P:(i + 1) * P],
                                                        tile.rearrange("p a d -> p (a d)").bitcast(F32), ident[:, :])
                                last.then_inc(sem("part_turned"), 1)
                            pe.wait_ge(sem("part_copied_act"), h * (NC // 2) + NC // 2)
                            pe.wait_ge(sem("part_copied_dve"), h * (NC // 2) + NC // 2)
                            pe.wait_ge(sem("v_ready"), h + 1)

                            def scores(t):
                                for m in range(2):
                                    if t >= 1:
                                        pe.wait_ge(sem("exped"), h * 2 * RT + 2 * (t - 1) + m + 1)
                                    for b in range(0, KEYS, BANK):
                                        e = min(b + BANK, KEYS)
                                        for part in range(2):
                                            last = pe.matmul(score[m][:, b:e], q_turned[:, m, t * P:(t + 1) * P],
                                                             k_turned[:, m, part, b:e], start=(part == 0), stop=(part == 1))
                                    last.then_inc(sem("scored"), 1)

                            def turn(t, i):
                                b, e = rounds[i]
                                if i == 0:
                                    pe.wait_ge(sem("mixed"), h * RT + t + 1)
                                if i or t:
                                    pe.wait_ge(sem(f"mix_copied{(i - 1) % NR}"), h * RT + t + (i > 0))
                                for j in range(b, e):
                                    last = pe.transpose(ps[:, 6, (j - b) * P:(j - b + 1) * P],
                                                        mixed[:, t % 2, j * P:(j + 1) * P], ident[:, :])
                                last.then_inc(sem("mix_turned"), 1)

                            def values(t, b, e):
                                if b == 0:
                                    for i in range(NR):
                                        pe.wait_ge(sem(f"mix_copied{i}"), h * RT + t + 1)
                                    if t >= 1:
                                        pe.wait_ge(sem("o_scaled"), h * RT + t)
                                for j in range(b, e):
                                    last = pe.matmul(ps[:, 7, (t % 2) * P:(t % 2 + 1) * P],
                                                     mixed_t[:, t % 2, j * P:(j + 1) * P], v_head[:, j, :],
                                                     start=(j == 0), stop=(j == KEYT - 1))
                                if e == KEYT:
                                    last.then_inc(sem("o_done"), 1)

                            for t in range(RT + 2):
                                if t < RT:
                                    scores(t)
                                turns, vals = 1 <= t <= RT, t >= 2
                                if turns:
                                    turn(t - 1, 0)
                                if vals:
                                    values(t - 2, 0, KEYT // 2)
                                if turns:
                                    turn(t - 1, 1)
                                if vals:
                                    values(t - 2, KEYT // 2, KEYT)
                                if turns:
                                    turn(t - 1, 2)
                        pe.wait_ge(sem("o_normed"), 1)
                        for c in range(HEADS * RT // 4):
                            for i in range(4):
                                t = 4 * (c % 2) + i
                                last = pe.transpose(ps[:, c, i * P:(i + 1) * P], o_all[:, c // 2, t, :], ident[:, :])
                            last.then_inc(sem("o_turned"), 1)

        attention()
        end_stage()

        res = residual[:, 0:KT, :]

        def even_output():
            with ExitStack() as st:
                y_hi = sb(st, "y_hi", [P, KT, SEQ], F32R)
                y_lo = sb(st, "y_lo", [P, KT, SEQ], F32R)
                gate = sb(st, "gate_in", [P, KT, SEQ])
                raw = sb(st, "out_raw", [P, 2, KT, P])
                w_hi = sb(st, "out_hi", [P, 2, KT, P], F32R)
                w_lo = sb(st, "out_lo", [P, 2, KT, P], F32R)
                w_out = a["even_w_out"].rearrange("e (k p) n -> p (e k) n", p=P)
                mixed = fq[:, :, :, :].rearrange("p a r n -> p (a r n)").rearrange("p (k n) -> p k n", k=KT)

                with nc.Block(name="even_out") as block:
                    @block.sync
                    def _(sp):
                        for m in range(2):
                            sp.dma_start(raw[:, m], w_out[:, :, m * P:(m + 1) * P]).then_inc(sem(f"ow_landed{m}"), 16)
                        for k in range(0, KT, 4):
                            sp.dma_start(gate[:, k:k + 4, :], gate_scratch[k:k + 4].rearrange("k p n -> p k n"))\
                              .then_inc(sem(f"gate_back{k // 4}"), 16)
                        sp.dma_start(res, x_scratch.rearrange("k p n -> p k n")).then_inc(sem("x_back"), 16)
                        for m in range(2, KT):
                            sp.wait_ge(sem("ow_low"), m - 1)
                            sp.dma_start(raw[:, m % 2], w_out[:, :, m * P:(m + 1) * P]).then_inc(sem(f"ow_landed{m % 2}"), 16)

                    @block.scalar
                    def _(act):
                        def high(m):
                            act.wait_ge(sem(f"ow_landed{m % 2}"), 16 * (m // 2 + 1))
                            if m >= 2:
                                act.wait_ge(sem("ow_done"), m - 1)
                            split_high(act, w_hi[:, m % 2], raw[:, m % 2], sem("ow_high"))

                        high(0)
                        high(1)
                        for k in range(KT):
                            act.wait_ge(sem("y_gated"), k + 1)
                            split_high(act, y_hi[:, k, :], gate[:, k, :], sem("y_high"))
                        for m in range(2, KT):
                            high(m)

                    @block.gpsimd
                    def _(pool):
                        for m in range(KT):
                            pool.wait_ge(sem("ow_high"), m + 1)
                            split_low(pool, w_lo[:, m % 2], raw[:, m % 2], w_hi[:, m % 2], sem("ow_low"))

                    @block.vector
                    def _(dve):
                        def low(k):
                            dve.wait_ge(sem("y_high"), k + 1)
                            split_low(dve, y_lo[:, k, :], gate[:, k, :], y_hi[:, k, :], sem("y_low"))

                        for k in range(KT):
                            dve.wait_ge(sem(f"gate_back{k // 4}"), 16)
                            dve.tensor_tensor(gate[:, k, :], gate[:, k, :], mixed[:, k, :], ALU.mult).then_inc(sem("y_gated"), 1)
                            if k:
                                low(k - 1)
                        low(KT - 1)
                        dve.wait_ge(sem("x_back"), 16)
                        for m in range(KT):
                            dve.wait_ge(sem("ow_done"), m + 1)
                            dve.scalar_tensor_tensor(out=res[:, m, :], in0=pair[m % 2], scalar=ada_col[:, 0, 2 * KT + m, 0:1],
                                                     in1=res[:, m, :], op0=ALU.mult, op1=ALU.add).then_inc(sem("ow_added"), 1)

                    @block.tensor
                    def _(pe):
                        pe.wait_ge(sem("y_low"), KT)
                        for m in range(KT):
                            pe.wait_ge(sem("ow_low"), m + 1)
                            if m >= 2:
                                pe.wait_ge(sem("ow_added"), m - 1)
                            matmul3(pe, pair[m % 2], lambda k: w_hi[:, m % 2, k, :], lambda k: w_lo[:, m % 2, k, :],
                                    lambda k, c, e: y_hi[:, k, c:e], lambda k, c, e: y_lo[:, k, c:e], KT, SEQ)\
                                .then_inc(sem("ow_done"), 1)

        even_output()
        end_stage()
        fq_stack.close()

        def load_unit(sp, kind, i, raw, src):
            sp.wait_ge(sem(kind + "_low"), i + 1)
            sp.dma_start(raw, src).then_inc(sem(kind + "_landed"), 16)

        def high_unit(act, kind, i, raw, hi, done_per_unit=1):
            act.wait_ge(sem(kind + "_landed"), (i + 1) * 16)
            act.wait_ge(sem(kind + "_done"), i * done_per_unit + 1)
            split_high(act, hi, raw, sem(kind + "_high"))

        def low_unit(pool, kind, i, raw, hi, lo, done_per_unit=1):
            pool.wait_ge(sem(kind + "_high"), i + 1)
            pool.wait_ge(sem(kind + "_done"), i * done_per_unit + 1)
            split_low(pool, lo, raw, hi, sem(kind + "_low"))

        def up_product(pe, kind, i, psum, hi, lo, h_hi, h_lo):
            pe.wait_ge(sem(kind + "_low"), i + 2)
            pe.wait_ge(sem(kind + "_free"), i + 1)
            matmul3(pe, psum, lambda k: hi[:, k, :], lambda k: lo[:, k, :],
                    lambda k, c, e: h_hi[:, k, c:e], lambda k, c, e: h_lo[:, k, c:e], KT, SEQ)\
                .then_inc(sem(kind + "_done"), 1)

        def down_product(pe, kind, i, psums, hi, lo, y_hi, y_lo):
            pe.wait_ge(sem(kind + "_low"), i + 2)
            pe.wait_ge(sem(kind + "_y_low"), i + 1)
            for d in range(KT):
                pe.wait_ge(sem(kind + "_free"), i * KT + d + 1)
                matmul3(pe, psums[d % 2], lambda k: hi[:, d * P:(d + 1) * P], lambda k: lo[:, d * P:(d + 1) * P],
                        lambda k, c, e: y_hi[:, c:e], lambda k, c, e: y_lo[:, c:e], 1, SEQ)\
                    .then_inc(sem(kind + "_done"), 1)

        def mixer_norm(tag, gain, shift, high, low, plain=None):
            with ExitStack() as st:
                n = Norm(st, tag, lambda k: res[:, k, :], SEQ, gain, shift, high, low, plain)
                run_norms([n], tag)

        def odd_layer():
            with ExitStack() as st:
                h1_hi = sb(st, "h1_hi", [P, KT, SEQ], F32R)
                h1_lo = sb(st, "h1_lo", [P, KT, SEQ], F32R)
                mixer_norm("norm1", gain_col(2), shift_col(1, 0), lambda k: h1_hi[:, k, :], lambda k: h1_lo[:, k, :])
                kinds = ("cg", "xt", "bg", "gt")
                quarter = {"bg": 0, "cg": 1, "xt": 2, "gt": 3}
                raw = {k: sb(st, "raw_" + k, [P, KT, P]) for k in kinds}
                hi = {k: sb(st, "hi_" + k, [P, KT, P], F32R) for k in kinds}
                lo = {k: sb(st, "lo_" + k, [P, KT, P], F32R) for k in kinds}
                d_raw, d_hi, d_lo = sb(st, "d_raw", [P, D]), sb(st, "d_hi", [P, D], F32R), sb(st, "d_lo", [P, D], F32R)
                c_gate = sb(st, "c_gate", [P, SEQ])
                u = sb(st, "u", [P, SEQ + 2])
                conv = sb(st, "conv", [P, SEQ])
                silu = sb(st, "silu", [P, SEQ])
                y_hi = sb(st, "yo_hi", [P, SEQ], F32R)
                y_lo = sb(st, "yo_lo", [P, SEQ], F32R)
                taps = sb(st, "taps", [P, 3, KT])
                w_in = a["odd_w_in"].rearrange("e (k p) n -> p (e k) n", p=P)
                w_out = a["odd_w_out"].rearrange("e k n -> (e k) n")
                N = KT
                up_pair = {"cg": 0, "xt": 1, "bg": 0, "gt": 1}

                with nc.Block(name="odd") as block:
                    @block.sync
                    def _(sp):
                        def loads(j):
                            for k in ("bg", "cg", "xt", "gt"):
                                load_unit(sp, k, j, raw[k][:, :, :], w_in[:, :, bass.ds(j * P + quarter[k] * D, P)])
                            load_unit(sp, "dn", j, d_raw[:, :], w_out[bass.ds(j * P, P), :])

                        with sp.Fori(0, N) as j:
                            loads(j)

                    @block.scalar
                    def _(act):
                        def block_step(j, splits=True):
                            def next_high(k):
                                if splits:
                                    high_unit(act, k, j + 1, raw[k][:, :, :], hi[k][:, :, :])

                            act.wait_ge(sem("cg_done"), j + 2)
                            act.wait_ge(sem("u_done"), j + 1)
                            act.activation(c_gate[:, :], pair[0], ACT.Copy).then_inc(sem("cg_copied"), 1)
                            next_high("cg")
                            next_high("xt")
                            next_high("bg")
                            act.wait_ge(sem("gt_done"), j + 2)
                            act.wait_ge(sem("y_done"), j + 1)
                            act.activation(silu[:, :], pair[1], ACT.Silu).then_inc(sem("gt_silu"), 1)
                            next_high("gt")
                            act.wait_ge(sem("y_done"), j + 2)
                            high_unit(act, "dn", j, d_raw[:, :], d_hi[:, :], KT)
                            split_high(act, y_hi[:, :], conv[:, :], sem("y_split"))

                        for k in kinds:
                            high_unit(act, k, 0, raw[k][:, :, :], hi[k][:, :, :])
                        with act.Fori(0, N - 1) as j:
                            block_step(j)
                        block_step(N - 1, splits=False)

                    @block.gpsimd
                    def _(pool):
                        def lows(j):
                            for k in kinds:
                                low_unit(pool, k, j, raw[k][:, :, :], hi[k][:, :, :], lo[k][:, :, :])

                        def rest(j):
                            low_unit(pool, "dn", j, d_raw[:, :], d_hi[:, :], d_lo[:, :], KT)
                            pool.wait_ge(sem("y_split"), j + 1)
                            split_low(pool, y_lo[:, :], conv[:, :], y_hi[:, :], sem("dn_y_low"))

                        lows(0)
                        with pool.Fori(0, N - 1) as j:
                            lows(j + 1)
                            rest(j)
                        rest(N - 1)

                    @block.vector
                    def _(dve):
                        for t in range(3):
                            dve.tensor_copy(taps[:, t, :], cols[:, ODD_CONV[0], ODD_CONV[1] + t * KT:ODD_CONV[1] + (t + 1) * KT])\
                               .then_inc(sem("taps_ready"), 1)
                        dve.memset(u[:, 0:1], 0.0).then_inc(sem("taps_ready"), 1)
                        dve.memset(u[:, SEQ + 1:SEQ + 2], 0.0).then_inc(sem("taps_ready"), 1)
                        dve.wait_ge(sem("taps_ready"), 5)
                        for name in [k + "_low" for k in kinds] + [k + "_done" for k in kinds] + \
                                [k + "_free" for k in ("cg", "xt")] + ["dn_low", "dn_done", "u_done", "y_done"]:
                            dve.sem_inc(sem(name), 1)
                        dve.sem_inc(sem("dn_free"), 2)

                        def block_step(j):
                            dve.wait_ge(sem("cg_copied"), j + 1)
                            dve.wait_ge(sem("xt_done"), j + 2)
                            dve.tensor_tensor(u[:, 1:SEQ + 1], c_gate[:, :], pair[1], ALU.mult).then_inc(sem("u_done"), 1)
                            dve.wait_ge(sem("u_done"), j + 2)
                            dve.wait_ge(sem("dn_y_low"), j) if not isinstance(j, int) or j > 0 else None
                            conv_step = sem("conv_step")
                            dve.tensor_scalar(conv[:, :], u[:, 1:SEQ + 1], taps[:, 1, bass.ds(j, 1)], None, ALU.mult)\
                               .then_inc(conv_step, 1)
                            dve.wait_ge(conv_step, j * 3 + 1)
                            dve.scalar_tensor_tensor(out=conv[:, :], in0=u[:, 0:SEQ], scalar=taps[:, 0, bass.ds(j, 1)],
                                                     in1=conv[:, :], op0=ALU.mult, op1=ALU.add).then_inc(conv_step, 1)
                            dve.wait_ge(conv_step, j * 3 + 2)
                            dve.scalar_tensor_tensor(out=conv[:, :], in0=u[:, 2:SEQ + 2], scalar=taps[:, 2, bass.ds(j, 1)],
                                                     in1=conv[:, :], op0=ALU.mult, op1=ALU.add).then_inc(conv_step, 1)
                            dve.wait_ge(conv_step, j * 3 + 3)
                            dve.wait_ge(sem("bg_done"), j + 2)
                            dve.tensor_tensor(conv[:, :], pair[0], conv[:, :], ALU.mult).then_inc(sem("bg_used"), 1)

                        def last_product(j):
                            dve.wait_ge(sem("bg_used"), j + 1)
                            dve.wait_ge(sem("gt_silu"), j + 1)
                            dve.tensor_tensor(conv[:, :], conv[:, :], silu[:, :], ALU.mult).then_inc(sem("y_done"), 1)

                        def add(j):
                            for d in range(KT):
                                dve.wait_ge(sem("dn_done"), j * KT + d + 2)
                                dve.scalar_tensor_tensor(out=res[:, d, :], in0=pair[2 + d % 2],
                                                         scalar=ada_col[:, 1, 2 * KT + d, 0:1], in1=res[:, d, :],
                                                         op0=ALU.mult, op1=ALU.add).then_inc(sem("dn_free"), 1)

                        block_step(0)
                        last_product(0)
                        with dve.Fori(1, N) as j:
                            block_step(j)
                            add(j - 1)
                            last_product(j)
                        add(N - 1)

                    @block.tensor
                    def _(pe):
                        def up(j):
                            for k, free in (("cg", "bg_used"), ("xt", "gt_silu"), ("bg", "cg_copied"), ("gt", "u_done")):
                                pe.wait_ge(sem(k + "_low"), j + 2)
                                if k in ("cg", "xt"):
                                    if not isinstance(j, int) or j > 0:
                                        pe.wait_ge(sem(free), j)
                                elif k == "bg":
                                    pe.wait_ge(sem(free), j + 1)
                                else:
                                    pe.wait_ge(sem(free), j + 2)
                                matmul3(pe, pair[up_pair[k]], lambda q: hi[k][:, q, :], lambda q: lo[k][:, q, :],
                                        lambda q, c, e: h1_hi[:, q, c:e], lambda q, c, e: h1_lo[:, q, c:e], KT, SEQ)\
                                    .then_inc(sem(k + "_done"), 1)

                        def down(j):
                            down_product(pe, "dn", j, pair[2:4], d_hi[:, :], d_lo[:, :], y_hi[:, :], y_lo[:, :])

                        up(0)
                        with pe.Fori(1, N) as j:
                            up(j)
                            down(j - 1)
                        down(N - 1)

        odd_layer()
        end_stage()

        def pool_layer():
            with ExitStack() as st:
                h = sb(st, "hp", [P, KT, PAD + SEQ])
                raw = sb(st, "pw_raw", [P, 4 * 2, HALF_GROUP])
                w_hi = sb(st, "pw_hi", [P, 4 * 2, HALF_GROUP], F32R)
                w_lo = sb(st, "pw_lo", [P, 4 * 2, HALF_GROUP], F32R)
                inv = sb(st, "inv_count", [P, 4, PAD])
                d_hi = sb(st, "dp_hi", [P, KT, SEQ], F32R)
                window = sb(st, "window", [P, 2, PAD + SEQ])
                bias = sb(st, "pool_bias", [P, KT])
                d_lo = sb(st, "dp_lo", [P, KT, SEQ], F32R)
                edge = sb(st, "edge", [P, PAD])
                with nc.Block(name="pool_pad") as block:
                    @block.vector
                    def _(dve):
                        for k in range(KT):
                            dve.memset(h[:, k, 0:PAD], 0.0)
                        for b in range(2):
                            dve.memset(window[:, b, 0:PAD], 0.0)
                        dve.tensor_tensor(bias[:, :], cols[:, POOL_B[0], POOL_B[1]:POOL_B[1] + KT],
                                          cols[:, POOL_SCALE[0], POOL_SCALE[1]:POOL_SCALE[1] + KT], ALU.mult)

                    @block.sync
                    def _(sp):
                        sp.dma_start(raw[:, :, :], a["pool_w_2"].rearrange("a g (k p) n -> p (a g k) n", p=P))\
                          .then_inc(sem("pw_landed"), 16)
                        sp.dma_start(inv[:, :, :], a["inv_count"].partition_broadcast(P)).then_inc(sem("inv_landed"), 16)

                mixer_norm("norm2", lambda k: col(MIX_G, k), None, None, None, plain=lambda k: h[:, k, PAD:PAD + SEQ])

                with nc.Block(name="pool") as block:
                    @block.scalar
                    def _(act):
                        act.wait_ge(sem("pw_landed"), 16)
                        split_high(act, w_hi[:, :, :], raw[:, :, :], sem("pw_high"))
                        for k in range(KT):
                            act.wait_ge(sem("pool_diff"), k + 1)
                            split_high(act, d_hi[:, k, :], h[:, k, PAD:PAD + SEQ], sem("pool_high"))
                        for m in range(KT):
                            act.wait_ge(sem("pool_done"), m + 1)
                            act.activation(h[:, m, PAD:PAD + SEQ], pair[m % 4], ACT.Identity, scale=col(POOL_SCALE, m),
                                           bias=bias[:, m:m + 1]).then_inc(sem("pool_scaled"), 1)

                    @block.gpsimd
                    def _(pool):
                        pool.wait_ge(sem("pw_high"), 1)
                        split_low(pool, w_lo[:, :, :], raw[:, :, :], w_hi[:, :, :], sem("pw_low"))
                        for k in range(KT):
                            pool.wait_ge(sem("pool_high"), k + 1)
                            split_low(pool, d_lo[:, k, :], h[:, k, PAD:PAD + SEQ], d_hi[:, k, :], sem("pool_low"))

                    @block.vector
                    def _(dve):
                        ws = sem("window_step")
                        n_ws = 0
                        dve.wait_ge(sem("inv_landed"), 16)
                        for k in range(KT):
                            w = WINDOWS[k // 2]
                            src, width, b = h[:, k], 1, 0
                            while width < w:
                                if n_ws:
                                    dve.wait_ge(ws, n_ws)
                                dve.tensor_tensor(window[:, b, PAD:PAD + SEQ], src[:, PAD:PAD + SEQ],
                                                  src[:, PAD - width:PAD + SEQ - width], ALU.add).then_inc(ws, 1)
                                n_ws += 1
                                src, width, b = window[:, b], 2 * width, 1 - b
                            dve.wait_ge(ws, n_ws)
                            dve.tensor_tensor(edge[:, :], src[:, PAD:2 * PAD], inv[:, k // 2, :], ALU.mult).then_inc(ws, 1)
                            n_ws += 1
                            dve.wait_ge(ws, n_ws)
                            dve.tensor_tensor(h[:, k, PAD:2 * PAD], edge[:, :], h[:, k, PAD:2 * PAD], ALU.subtract)\
                               .then_inc(ws, 1)
                            n_ws += 1
                            dve.scalar_tensor_tensor(out=h[:, k, 2 * PAD:PAD + SEQ], in0=src[:, 2 * PAD:PAD + SEQ],
                                                     scalar=1.0 / w, in1=h[:, k, 2 * PAD:PAD + SEQ], op0=ALU.mult,
                                                     op1=ALU.subtract).then_inc(sem("pool_diff"), 1)
                            dve.wait_ge(sem("pool_diff"), k + 1)
                        for m in range(KT):
                            dve.wait_ge(sem("pool_scaled"), m + 1)
                            dve.tensor_tensor(res[:, m, :], res[:, m, :], h[:, m, PAD:PAD + SEQ], ALU.add)

                    @block.tensor
                    def _(pe):
                        pe.wait_ge(sem("pw_low"), 1)
                        for m in range(KT):
                            g, half = m // 2, (m % 2) * P
                            pe.wait_ge(sem("pool_low"), 2 * g + 2)
                            if m >= 4:
                                pe.wait_ge(sem("pool_scaled"), m - 3)
                            matmul3(pe, pair[m % 4], lambda k: w_hi[:, 2 * g + k, half:half + P],
                                    lambda k: w_lo[:, 2 * g + k, half:half + P],
                                    lambda k, c, e: d_hi[:, 2 * g + k, c:e], lambda k, c, e: d_lo[:, 2 * g + k, c:e], 2, SEQ)\
                                .then_inc(sem("pool_done"), 1)

        pool_layer()
        end_stage()

        def ffn_layer():
            with ExitStack() as st:
                zero = sb(st, "zero", [P, KT])
                h2_hi = sb(st, "h2_hi", [P, KT, SEQ], F32R)
                h2_lo = sb(st, "h2_lo", [P, KT, SEQ], F32R)
                with nc.Block(name="zero") as block:
                    @block.vector
                    def _(dve):
                        dve.memset(zero[:, :], 0.0)
                mixer_norm("norm3", lambda k: col(FFN_G, k), lambda k: zero[:, k:k + 1],
                           lambda k: h2_hi[:, k, :], lambda k: h2_lo[:, k, :])
                kinds = ("va", "ga")
                raw = {k: sb(st, "raw_" + k, [P, KT, P]) for k in kinds}
                hi = {k: sb(st, "hi_" + k, [P, KT, P], F32R) for k in kinds}
                lo = {k: sb(st, "lo_" + k, [P, KT, P], F32R) for k in kinds}
                f_raw, f_hi, f_lo = sb(st, "f_raw", [P, D]), sb(st, "f_hi", [P, D], F32R), sb(st, "f_lo", [P, D], F32R)
                branch = {k: sb(st, "branch_" + k, [P, SEQ]) for k in kinds}
                y_hi = sb(st, "yf_hi", [P, SEQ], F32R)
                y_lo = sb(st, "yf_lo", [P, SEQ], F32R)
                w_in = a["ffn_w_in_2"].rearrange("e (k p) n -> p (e k) n", p=P)
                w_out = a["ffn_w_out_2"].rearrange("e k n -> (e k) n")
                first = {"va": 0, "ga": FFN_T}
                up_pair = {"va": 0, "ga": 1}
                N = FFN_T

                def tap(where, k, j):
                    return cols[:, where[0], bass.ds(j + (where[1] + first[k]), 1)]

                with nc.Block(name="ffn") as block:
                    @block.sync
                    def _(sp):
                        with sp.Fori(0, N) as j:
                            for k in kinds:
                                load_unit(sp, k, j, raw[k][:, :, :], w_in[:, :, bass.ds(j * P + first[k] * P, P)])
                            load_unit(sp, "fd", j, f_raw[:, :], w_out[bass.ds(j * P, P), :])

                    @block.scalar
                    def _(act):
                        def block_step(j, splits=True):
                            for k in kinds:
                                act.wait_ge(sem(k + "_done"), j + 2)
                                act.wait_ge(sem("fd_y_free"), j + 1)
                                act.activation(branch[k][:, :], pair[up_pair[k]], ACT.Identity, scale=tap(FFN_TAP2, k, j),
                                               bias=tap(FFN_B, k, j)).then_inc(sem(k + "_tap2"), 1)
                                if splits:
                                    high_unit(act, k, j + 1, raw[k][:, :, :], hi[k][:, :, :])
                            high_unit(act, "fd", j, f_raw[:, :], f_hi[:, :], KT)
                            act.wait_ge(sem("ga_free"), j + 2)
                            act.activation(branch["ga"][:, :], branch["ga"][:, :], ACT.Silu).then_inc(sem("ga_silu"), 1)
                            act.wait_ge(sem("fy_done"), j + 1)
                            split_high(act, y_hi[:, :], branch["va"][:, :], sem("fy_split"))

                        for k in kinds:
                            high_unit(act, k, 0, raw[k][:, :, :], hi[k][:, :, :])
                        with act.Fori(0, N - 1) as j:
                            block_step(j)
                        block_step(N - 1, splits=False)

                    @block.gpsimd
                    def _(pool):
                        def lows(j):
                            for k in kinds:
                                low_unit(pool, k, j, raw[k][:, :, :], hi[k][:, :, :], lo[k][:, :, :])

                        def rest(j):
                            low_unit(pool, "fd", j, f_raw[:, :], f_hi[:, :], f_lo[:, :], KT)
                            pool.wait_ge(sem("fy_split"), j + 1)
                            split_low(pool, y_lo[:, :], branch["va"][:, :], y_hi[:, :], sem("fd_y_low"))
                            pool.wait_ge(sem("fd_y_low"), j + 1)
                            pool.sem_inc(sem("fd_y_free"), 1)

                        lows(0)
                        with pool.Fori(0, N - 1) as j:
                            lows(j + 1)
                            rest(j)
                        rest(N - 1)

                    @block.vector
                    def _(dve):
                        for name in [k + s for k in kinds for s in ("_low", "_done", "_free")] + ["fd_low", "fd_done", "fd_y_free"]:
                            dve.sem_inc(sem(name), 1)
                        dve.sem_inc(sem("fd_free"), 2)

                        def taps(k, j):
                            x, y = pair[up_pair[k]], branch[k]
                            dve.wait_ge(sem(k + "_tap2"), j + 1)
                            dve.scalar_tensor_tensor(out=y[:, 1:SEQ], in0=x[:, 0:SEQ - 1], scalar=tap(FFN_TAP1, k, j),
                                                     in1=y[:, 1:SEQ], op0=ALU.mult, op1=ALU.add).then_inc(sem(k + "_tap1"), 1)
                            dve.wait_ge(sem(k + "_tap1"), j + 1)
                            dve.scalar_tensor_tensor(out=y[:, 2:SEQ], in0=x[:, 0:SEQ - 2], scalar=tap(FFN_TAP0, k, j),
                                                     in1=y[:, 2:SEQ], op0=ALU.mult, op1=ALU.add).then_inc(sem(k + "_free"), 1)

                        def product(j):
                            dve.wait_ge(sem("ga_silu"), j + 1)
                            dve.wait_ge(sem("va_free"), j + 2)
                            dve.tensor_tensor(branch["va"][:, :], branch["va"][:, :], branch["ga"][:, :], ALU.mult)\
                               .then_inc(sem("fy_done"), 1)

                        def add(j):
                            for d in range(KT):
                                dve.wait_ge(sem("fd_done"), j * KT + d + 2)
                                dve.tensor_tensor(res[:, d, :], pair[2 + d % 2], res[:, d, :], ALU.add).then_inc(sem("fd_free"), 1)

                        taps("va", 0)
                        taps("ga", 0)
                        product(0)
                        with dve.Fori(1, N) as j:
                            taps("va", j)
                            add(j - 1)
                            taps("ga", j)
                            product(j)
                        add(N - 1)

                    @block.tensor
                    def _(pe):
                        def up(j):
                            for k in kinds:
                                up_product(pe, k, j, pair[up_pair[k]], hi[k], lo[k], h2_hi, h2_lo)

                        def down(j):
                            down_product(pe, "fd", j, pair[2:4], f_hi[:, :], f_lo[:, :], y_hi[:, :], y_lo[:, :])

                        up(0)
                        with pe.Fori(1, N) as j:
                            up(j)
                            down(j - 1)
                        down(N - 1)

        ffn_layer()
        end_stage()

        with ExitStack() as st:
            rows_out = sb(st, "rows_out", [P, RT, D])
            out_rows = out.rearrange("b (r p) d -> p (b r) d", p=P)
            with nc.Block(name="out") as block:
                @block.tensor
                def _(pe):
                    for r in range(RT):
                        if r >= 4:
                            pe.wait_ge(sem("row_copied_act" if r % 2 == 0 else "row_copied_dve"), (r - 4) // 2 + 1)
                        for k in range(KT):
                            last = pe.transpose(pair[r % 4][:, k * P:(k + 1) * P], res[:, k, r * P:(r + 1) * P], ident[:, :])
                        last.then_inc(sem("row_turned"), 1)

                @block.scalar
                def _(act):
                    for r in range(0, RT, 2):
                        act.wait_ge(sem("row_turned"), r + 1)
                        act.activation(rows_out[:, r, :], pair[r % 4], ACT.Copy).then_inc(sem("row_copied_act"), 1)

                @block.vector
                def _(dve):
                    for r in range(1, RT, 2):
                        dve.wait_ge(sem("row_turned"), r + 1)
                        dve.tensor_copy(rows_out[:, r, :], pair[r % 4]).then_inc(sem("row_copied_dve"), 1)

                @block.sync
                def _(sp):
                    for r in range(RT):
                        sp.wait_ge(sem("row_copied_act" if r % 2 == 0 else "row_copied_dve"), r // 2 + 1)
                        sp.dma_start(out_rows[:, r, :], rows_out[:, r, :]).then_inc(sem("stored"), 16)
                    sp.wait_ge(sem("stored"), 16 * RT)


_INS = ["x", "c", "ctx", "c_ctx", "norm_g", "ada_w", "ada_b", "even_w_in", "even_q_norm", "even_k_norm",
        "even_lambda_q1", "even_lambda_k1", "even_lambda_q2", "even_lambda_k2", "even_subln", "even_w_out",
        "odd_w_in", "odd_conv_w", "odd_w_out", "norm_mix_g_2", "norm_ffn_g_2", "pool_w_2", "pool_b_2",
        "pool_scale_2", "ffn_w_in_2", "ffn_conv_w_2", "ffn_conv_b_2", "ffn_w_out_2"]


def _constants():
    import numpy as np
    c = {"identity": np.eye(P, dtype=np.float32)}
    sel = np.zeros((P, 2), np.float32)
    for j in range(0, P, 32):
        sel[j, 0] = sel[j + 1, 1] = 1
    c["selector"] = sel
    grid = 64
    pos = np.arange(SEQ)
    half = DH // 2
    freqs = np.float32(10000.0) ** (-np.arange(0, half, 2, dtype=np.float32) / np.float32(half))
    ang = np.stack([(p.astype(np.float32)[:, None] * freqs) for p in (pos // grid, pos % grid)], axis=1)
    c["rope_cos"] = np.cos(ang.astype(np.float64)).astype(np.float32)
    c["rope_sin"] = np.sin(ang.astype(np.float64)).astype(np.float32)
    p, k2 = np.arange(P)[:, None], np.arange(P)[None, :]
    dft = np.zeros((P, RADIX, 2, 2 * P))
    for k1 in range(RADIX):
        th = 2 * np.pi * ((p * (k1 + RADIX * k2)) % SEQ) / SEQ
        conj = -1.0 if k1 > RADIX // 2 else 1.0
        dft[:, k1, 0] = np.concatenate([np.cos(th), -np.sin(th)], axis=1)
        dft[:, k1, 1] = conj * np.concatenate([np.sin(th), np.cos(th)], axis=1)
    c["seq_dft"] = dft.astype(np.float32)
    th = 2 * np.pi * ((p * k2) % P) / P
    c["channel_dft"] = (np.stack([np.cos(th), np.sin(th)], axis=1) / np.sqrt(SEQ * P)).astype(np.float32)
    t = np.arange(PAD)
    c["inv_count"] = np.stack([1.0 / np.minimum(t + 1, w) for w in WINDOWS]).astype(np.float32)
    return c


def kernel(**inputs):
    import numpy as np
    import concourse.bacc as bacc
    from concourse.bass_utils import run_bass_kernel_spmd

    nc = bacc.Bacc("TRN2", target_bir_lowering=False, num_devices=1)
    arrays, aps = {}, {}
    named = {n: np.ascontiguousarray(inputs[n]) for n in _INS}
    for name, value in {**named, **_constants()}.items():
        arrays[f"in_{name}"] = value
        aps[name] = nc.dram_tensor(f"in_{name}", value.shape, mybir.dt.from_np(value.dtype), kind="ExternalInput").ap()
    out = nc.dram_tensor("out", (1, SEQ, D), F32, kind="ExternalOutput").ap()
    program(nc, aps, out)
    result = run_bass_kernel_spmd(nc, [arrays], core_ids=[0])
    return result.results[0]["out"]
```

```python
from contextlib import ExitStack

import concourse.bass as bass
from concourse import mybir

ALU = mybir.AluOpType
ACT = mybir.ActivationFunctionType
F32 = mybir.dt.float32
F32R = mybir.dt.float32r
AX_X = mybir.AxisListType.X

P = 128
D = 1024
KT = D // P
SEQ = 1024
RT = SEQ // P
CTX = 256
CT = CTX // P
BANK = 512
EPS = 1e-6
HEADS = 4
DH = 64
DV = 2 * DH
QK = HEADS * 2 * DH
KEYS = CTX + SEQ
KEYT = KEYS // P
ATTN_SCALE = DH ** -0.5
LAMBDA_INIT = 0.2
F_GROUPS = 4
RADIX = 8
HALF_GROUP = 256
ADA = 3 * D
ADA_T = ADA // P
FFN = 2816
FFN_T = FFN // P
WINDOWS = (2, 4, 8, 16)
PAD = 16
GATE_COL = 2048
KV_COL = 1024

NORM_G, ADA_B, ODD_CONV, MIX_G, FFN_G, C_VEC, C_CTX = ((0, o) for o in (0, 16, 64, 88, 96, 104, 112))
POOL_B, POOL_SCALE, FFN_B, FFN_TAP0 = ((1, o) for o in (0, 8, 16, 60))
FFN_TAP1, FFN_TAP2, SUBLN = ((2, o) for o in (0, 44, 88))
ROWS = (120, 104, 89)


def program(nc, a, out):
    ctx = ExitStack()
    with ctx:
        sems = {}

        def sem(name):
            if name not in sems:
                sems[name] = nc.alloc_semaphore(name)
            return sems[name]

        def end_stage():
            nc.clear_and_free_semaphores(list(sems.values()))
            sems.clear()
            nc.all_engine_barrier()

        def sb(stack, name, shape, dt=F32):
            return stack.enter_context(nc.sbuf_tensor(name, shape, dt))

        ps = ctx.enter_context(nc.psum_tensor("ps", [P, 8, BANK], F32))
        pair = [ps[:, 2 * i:2 * i + 2, :].rearrange("p b n -> p (b n)") for i in range(4)]

        ident = sb(ctx, "ident", [P, P])
        ones = sb(ctx, "ones", [P, P])
        eps = sb(ctx, "eps", [P, 1])
        cols = sb(ctx, "cols", [P, 3, P])
        ada_col = sb(ctx, "ada_col", [P, 2, ADA_T, 2])
        mod_gain = sb(ctx, "mod_gain", [P, 3, KT])
        neg_lam = sb(ctx, "neg_lam", [P, 1])
        cond_col = sb(ctx, "cond_col", [P, KT, 2])
        residual = sb(ctx, "residual", [P, KEYT, D])
        fq_stack = ExitStack()
        fq = sb(fq_stack, "fq", [P, 2, RT, QK])

        x_scratch = nc.dram_tensor("x_scratch", [KT, P, SEQ], F32).ap()
        gate_scratch = nc.dram_tensor("gate_scratch", [KT, P, SEQ], F32).ap()

        def col(where, j):
            return cols[:, where[0], where[1] + j:where[1] + j + 1]

        def matmul3(pe, psum, w_hi, w_lo, a_hi, a_lo, n_k, n):
            for k in range(n_k):
                for w, act in ((w_hi, a_hi), (w_hi, a_lo), (w_lo, a_hi)):
                    for c in range(0, n, BANK):
                        e = min(c + BANK, n)
                        last = pe.matmul(psum[:, c:e], w(k), act(k, c, e), start=(k == 0 and w is w_hi and act is a_hi),
                                         stop=(k == n_k - 1 and w is w_lo))
            return last

        def channel_products(pe, psum, k, w_hi, w_lo, a_hi, a_lo):
            for w, act in ((w_hi, a_hi), (w_hi, a_lo), (w_lo, a_hi)):
                for c in range(0, SEQ, BANK):
                    last = pe.matmul(psum[:, c:c + BANK], w, act[:, k, c:c + BANK], start=(k == 0 and w is w_hi and act is a_hi),
                                     stop=(k == KT - 1 and w is w_lo))
            return last

        def split_high(act, dst, src, done):
            return act.activation(dst, src, ACT.Copy).then_inc(done, 1)

        def split_low(eng, dst, src, high, done):
            return eng.tensor_tensor(dst, src, high.bitcast(F32), ALU.subtract).then_inc(done, 1)

        class Norm:

            def __init__(self, tag, x, n, gain, shift, high, low, totals, rstd, square=None, scaled=None,
                         mean=None, compact=None, kept=None, rstd_elsewhere=False):
                self.tag, self.x, self.n, self.gain, self.shift = tag, x, n, gain, shift
                self.high, self.low, self.mean = high, low, mean
                self.square, self.totals, self.rstd, self.scaled = square, totals, rstd, scaled
                self.compact, self.kept = compact, kept
                self.rstd_elsewhere = rstd_elsewhere

            def s(self, what):
                return sem(self.tag + "_" + what)

            def scalar_square(self, act, k):
                dst = self.totals[0] if k == 0 else self.square[:, k % 2, 0:self.n]
                if k >= 3:
                    act.wait_ge(self.s("summed"), k - 2)
                act.activation(dst, self.x(k), ACT.Square).then_inc(self.s("squared"), 1)

            def scalar_root(self, act):
                act.wait_ge(self.s("meaned"), 1)
                act.activation(self.compact, self.mean, ACT.Sqrt, bias=eps[:, 0:1], scale=1.0 / D)\
                   .then_inc(self.s("rooted"), 1)

            def scalar_high(self, act, k):
                act.wait_ge(self.s("scaled"), k + 1)
                act.activation(self.high(k), self.scaled[:, k % 2, 0:self.n], ACT.Identity, bias=self.shift(k))\
                   .then_inc(self.s("high"), 1)

            def vector_sum(self, dve):
                for k in range(1, KT):
                    dve.wait_ge(self.s("squared"), k + 1)
                    if k > 1:
                        dve.wait_ge(self.s("summed"), k - 1)
                    dve.tensor_tensor(self.totals[0], self.totals[0], self.square[:, k % 2, 0:self.n], ALU.add)\
                       .then_inc(self.s("summed"), 1)

            def vector_inverse(self, dve):
                dve.wait_ge(self.s("rooted"), 1)
                dve.reciprocal(self.compact, self.compact).then_inc(self.s("inverse"), 1)

            def vector_keep(self, dve):
                dve.wait_ge(self.s("spread"), 1)
                return dve.tensor_copy(self.kept, self.rstd)

            def vector_scale(self, dve):
                if not self.rstd_elsewhere:
                    dve.wait_ge(self.s("spread"), 1)

                def scale(k):
                    dst = self.scaled[:, k % 2, 0:self.n]
                    dve.scalar_tensor_tensor(out=dst, in0=self.x(k), scalar=self.gain(k), in1=self.rstd,
                                             op0=ALU.mult, op1=ALU.mult).then_inc(self.s("scaled"), 1)

                scale(0)
                for k in range(KT):
                    if k + 1 < KT:
                        if k >= 1:
                            dve.wait_ge(self.s("low"), k)
                        scale(k + 1)
                    dve.wait_ge(self.s("high"), k + 1)
                    dve.scalar_tensor_tensor(out=self.low(k), in0=self.scaled[:, k % 2, 0:self.n], scalar=self.shift(k),
                                             in1=self.high(k).bitcast(F32), op0=ALU.add, op1=ALU.subtract)\
                       .then_inc(self.s("low"), 1)

            def tensor(self, pe):
                if self.square is not None:
                    pe.wait_ge(self.s("summed"), KT - 1)
                for r in range(self.n // P):
                    for i, total in enumerate(self.totals):
                        last = pe.matmul(self.mean[:, r:r + 1], total[:, r * P:(r + 1) * P], ones[:, 0:1],
                                         start=(i == 0), stop=(i == len(self.totals) - 1))
                last.then_inc(self.s("meaned"), 1)
                pe.wait_ge(self.s("inverse"), 1)
                for r in range(self.n // P):
                    last = pe.matmul(self.rstd[:, r * P:(r + 1) * P], self.compact[:, r:r + 1].broadcast_to([P, P]),
                                     ident[:, :], start=True, stop=True)
                last.then_inc(self.s("spread"), 1)

        class SquareSum:

            def __init__(self, tag, buffers):
                self.tag, self.buffers = tag, buffers

            def s(self, what):
                return sem(self.tag + "_" + what)

            def scalar(self, act, m):
                p = m % 2
                if m >= 4:
                    act.wait_ge(self.s(f"summed{p}"), m // 2 - 1)
                act.activation(square_totals[p] if m < 2 else self.buffers[p], res[:, m, :], ACT.Square)\
                   .then_inc(self.s("squared"), 1)

            def add(self, eng, m):
                p = m % 2
                eng.wait_ge(self.s("squared"), m + 1)
                if m >= 4:
                    eng.wait_ge(self.s(f"summed{p}"), m // 2 - 1)
                eng.tensor_tensor(square_totals[p], square_totals[p], self.buffers[p], ALU.add)\
                   .then_inc(self.s(f"summed{p}"), 1)

        ADA_FIRST = [(0, m) for m in range(4)]
        ADA_REST = [(0, 4), (0, 5)] + [(1, m) for m in range(6)]

        def ada_product(pe, pieces, first_bank, k, cond, raw):
            for i in range(len(pieces)):
                j = 32 * (i % 4)
                last = pe.matmul(ps[j:j + 32, first_bank + i // 4, :], cond[:, k, :], raw[:, i * BANK:(i + 1) * BANK],
                                 start=(k == 0), stop=(k == KT - 1))
            return last

        def ada_turn(pe, pieces, rows):
            for b in range(len(pieces) // 4):
                for t in range(4):
                    last = pe.transpose(ps[:, b, t * P:(t + 1) * P], rows[:, b, t * P:(t + 1) * P], ident[:, :])
            return last

        def ada_bias(dve, pieces):
            for i, (l, m) in enumerate(pieces):
                b = ADA_B[1] + l * ADA_T + 4 * m
                j = 32 * (i % 4)
                last = dve.tensor_tensor(ada_col[:, l, 4 * m:4 * m + 4, :],
                                         ps[:, i // 4, :].rearrange("p (t n) -> p t n", n=P)[:, :, j:j + 2],
                                         cols[:, ADA_B[0], b:b + 4].unsqueeze(2).broadcast_to([P, 4, 2]), ALU.add)
            return last

        def ada_gain(dve, n, l, v):
            dve.scalar_tensor_tensor(out=mod_gain[:, n, :], in0=ada_col[:, l, KT:2 * KT, v], scalar=1.0,
                                     in1=cols[:, NORM_G[0], NORM_G[1] + l * KT:NORM_G[1] + (l + 1) * KT],
                                     op0=ALU.add, op1=ALU.mult)

        def adaptive_parameters():
            with ExitStack() as st:
                rows = sb(st, "rows", [P, 3, P])
                lam_in = sb(st, "lam_in", [P, 4, DH])
                lam_pair = sb(st, "lam_pair", [P, 2, DH])
                lam_dot = sb(st, "lam_dot", [P, 2])
                lam_exp = sb(st, "lam_exp", [P, 2])
                cond = sb(st, "cond", [P, KT, 32])
                ada_raw = sb(st, "ada_raw", [P, KT, len(ADA_FIRST) * BANK])
                ada_rows = sb(st, "ada_rows", [P, 1, BANK])
                square = sb(st, "square", [P, 2, SEQ])
                square_c = sb(st, "square_c", [P, 2, CTX])
                total = sb(st, "square_sum", [P, SEQ])
                total_c = sb(st, "square_sum_c", [P, CTX])
                compact = sb(st, "compact", [P, KEYT])
                stats = Norm("stats", lambda k: x_t[:, k, :], SEQ, None, None, None, None, [total[:, :]], pair[2], square,
                             mean=ps[:, 7, 0:RT], compact=compact[:, 0:RT], kept=rstd_x)
                stats_c = Norm("stats_c", lambda k: ctx_t[:, k, :], CTX, None, None, None, None, [total_c[:, :]],
                               ps[:, 0, 0:CTX], square_c, mean=ps[:, 1, 0:CT], compact=compact[:, RT:KEYT], kept=rstd_c)
                ctx_t = ctx_xt
                x_t = fq[:, :, :, :].rearrange("p a b n -> p (a b n)").rearrange("p (k n) -> p k n", k=KT)
                nat = residual
                row_sources = [
                    (0, NORM_G[1], a["norm_g"].rearrange("l (k p) -> (l k) p", p=P)),
                    (0, ADA_B[1], a["ada_b"].rearrange("l (k p) -> (l k) p", p=P)),
                    (0, ODD_CONV[1], a["odd_conv_w"].rearrange("a t (k p) -> (a t k) p", p=P)),
                    (0, MIX_G[1], a["norm_mix_g_2"].rearrange("a (k p) -> (a k) p", p=P)),
                    (0, FFN_G[1], a["norm_ffn_g_2"].rearrange("a (k p) -> (a k) p", p=P)),
                    (0, C_VEC[1], a["c"].rearrange("a (k p) -> (a k) p", p=P)),
                    (0, C_CTX[1], a["c_ctx"].rearrange("(k p) -> k p", p=P)),
                    (1, POOL_B[1], a["pool_b_2"].rearrange("a (k p) -> (a k) p", p=P)),
                    (1, POOL_SCALE[1], a["pool_scale_2"].rearrange("a (k p) -> (a k) p", p=P)),
                    (1, FFN_B[1], a["ffn_conv_b_2"].rearrange("a (k p) -> (a k) p", p=P)),
                    (1, FFN_TAP0[1], a["ffn_conv_w_2"][0, 0:1, :].rearrange("a (k p) -> (a k) p", p=P)),
                    (2, FFN_TAP1[1], a["ffn_conv_w_2"][0, 1:3, :].rearrange("a (k p) -> (a k) p", p=P)),
                    (2, SUBLN[1], a["even_subln"]),
                ]
                x_rows = a["x"].rearrange("b (r p) d -> p (b r) d", p=P)
                ctx_rows = a["ctx"].rearrange("b (r p) d -> p (b r) d", p=P)

                with nc.Block(name="ada") as block:
                    @block.sync
                    def _(sp):
                        sp.dma_start(ident[:, :], a["identity"]).then_inc(sem("rows_in"), 16)
                        sp.dma_start(nat[:, 0:4, :], x_rows[:, 0:4, :]).then_inc(sem("x_in_lo"), 16)
                        sp.dma_start(nat[:, 4:8, :], x_rows[:, 4:8, :]).then_inc(sem("x_in_hi"), 16)
                        for t, r, src in row_sources:
                            sp.dma_start(rows[r:r + src.shape[0], t, :], src).then_inc(sem("rows_in"), 16)
                        sp.dma_start(nat[:, RT:KEYT, :], ctx_rows).then_inc(sem("ctx_in"), 16)
                        for k in range(KT):
                            sp.dma_start(ada_raw[:, k, :], a["ada_w"][0, k * P:(k + 1) * P, 0:len(ADA_FIRST) * BANK])\
                              .then_inc(sem(f"ada_in{k}"), 16)
                        for n, name in enumerate(("even_lambda_q1", "even_lambda_k1", "even_lambda_q2", "even_lambda_k2")):
                            sp.dma_start(lam_in[:, n, :], a[name].broadcast_to([P, DH])).then_inc(sem("lam_in"), 16)
                        sp.dma_start(in_raw[:, :, :], w_in[:, :, KV_COL:KV_COL + HALF_GROUP]).then_inc(sem("in_landed"), 16)
                        for k in range(KT):
                            sp.wait_ge(sem("xt_copied"), k + 1)
                            sp.dma_start(x_scratch[k], x_t[:, k, :]).then_inc(sem("x_spilled"), 16)

                    @block.tensor
                    def _(pe):
                        pe.wait_ge(sem("rows_in"), 16 * (1 + len(row_sources)))
                        for t in range(3):
                            last = pe.transpose(ps[:, 7, t * P:t * P + ROWS[t]], rows[0:ROWS[t], t, :],
                                                ident[0:ROWS[t], 0:ROWS[t]])
                        last.then_inc(sem("rows_turned"), 1)
                        pe.wait_ge(sem("x_in_lo"), 16)
                        pe.wait_ge(sem("x_in_hi"), 16)
                        for k in range(KT):
                            if k >= 2:
                                pe.wait_ge(sem("xt_copied"), k - 1)
                            for r in range(RT):
                                last = pe.transpose(pair[k % 2][:, r * P:(r + 1) * P], nat[:, r, k * P:(k + 1) * P],
                                                    ident[:, :])
                            last.then_inc(sem("xt_turned"), 1)
                        pe.wait_ge(sem("ctx_in"), 16)
                        for k in range(0, KT, 4):
                            for i in range(4):
                                for r in range(CT):
                                    last = pe.transpose(pair[2][:, (i * CT + r) * P:(i * CT + r + 1) * P],
                                                        nat[:, RT + r, (k + i) * P:(k + i + 1) * P], ident[:, :])
                            last.then_inc(sem("ct_turned"), 1)
                            pe.wait_ge(sem("ct_copied"), k // 4 + 1)
                        pe.wait_ge(sem("cols_copied"), 3)
                        stats.tensor(pe)
                        pe.wait_ge(sem("xt_copied"), KT)
                        stats_c.tensor(pe)
                        pe.wait_ge(sem("cond_ready"), 1)
                        for k in range(KT):
                            pe.wait_ge(sem(f"ada_in{k}"), 16)
                            last = ada_product(pe, ADA_FIRST, 6, k, cond, ada_raw[:, k, :])
                        last.then_inc(sem("ada_summed"), 1)
                        pe.wait_ge(sem("ada_rows"), 1)
                        pe.wait_ge(sem("stats_kept"), 1)
                        ada_turn(pe, ADA_FIRST, ada_rows).then_inc(sem("ada_turned"), 1)

                    @block.scalar
                    def _(act):
                        act.wait_ge(sem("cols_copied"), 3)
                        act.wait_ge(sem("cond_zero"), 1)
                        for v, vec in enumerate((C_VEC, C_CTX)):
                            act.activation(cond_col[:, :, v], cols[:, vec[0], vec[1]:vec[1] + KT], ACT.Silu)\
                               .then_inc(sem("cond_col"), 1)
                        act.wait_ge(sem("cond_col"), 2)
                        act.activation(cond[:, :, 0:2], cond_col[:, :, :], ACT.Copy).then_inc(sem("cond_ready"), 1)
                        for k in range(KT):
                            act.wait_ge(sem("xt_turned"), k + 1)
                            act.activation(x_t[:, k, :], pair[k % 2], ACT.Copy).then_inc(sem("xt_copied"), 1)
                            if k:
                                act.wait_ge(sem("xt_copied"), k)
                                stats.scalar_square(act, k - 1)
                        for k in range(0, KT, 4):
                            act.wait_ge(sem("ct_turned"), k // 4 + 1)
                            act.activation(ctx_t[:, k:k + 4, :].rearrange("p k n -> p (k n)"), pair[2], ACT.Copy)\
                               .then_inc(sem("ct_copied"), 1)
                        act.wait_ge(sem("xt_copied"), KT)
                        stats.scalar_square(act, KT - 1)
                        act.wait_ge(sem("ct_copied"), 2)
                        for k in range(KT):
                            stats_c.scalar_square(act, k)
                        stats.scalar_root(act)
                        stats_c.scalar_root(act)
                        act.wait_ge(sem("in_landed"), 16)
                        split_high(act, in_hi[:, 0], in_raw[:, :, :], sem("in_high"))
                        act.wait_ge(sem("lam_dots"), 2)
                        act.activation(lam_exp[:, :], lam_dot[:, :], ACT.Exp).then_inc(sem("lam_exped"), 1)

                    @block.gpsimd
                    def _(pool):
                        pool.wait_ge(sem("in_high"), 1)
                        split_low(pool, in_lo[:, 0], in_raw[:, :, :], in_hi[:, 0], sem("in_low"))

                    @block.vector
                    def _(dve):
                        dve.memset(ones[:, :], 1.0)
                        dve.memset(eps[:, :], EPS)
                        dve.memset(cond[:, :, :], 0.0).then_inc(sem("cond_zero"), 1)
                        dve.wait_ge(sem("rows_turned"), 1)
                        for t in range(3):
                            dve.tensor_copy(cols[:, t, 0:ROWS[t]], ps[:, 7, t * P:t * P + ROWS[t]])\
                               .then_inc(sem("cols_copied"), 1)
                        stats.vector_sum(dve)
                        stats_c.vector_sum(dve)
                        stats.vector_inverse(dve)
                        stats_c.vector_inverse(dve)
                        stats.vector_keep(dve)
                        stats_c.vector_keep(dve).then_inc(sem("stats_kept"), 1)
                        dve.wait_ge(sem("lam_in"), 64)
                        for n in range(2):
                            dve.tensor_tensor(lam_pair[:, n, :], lam_in[:, 2 * n, :], lam_in[:, 2 * n + 1, :], ALU.mult)\
                               .then_inc(sem("lam_pairs"), 1)
                        dve.wait_ge(sem("lam_pairs"), 2)
                        for n in range(2):
                            dve.tensor_reduce(lam_dot[:, n:n + 1], lam_pair[:, n, :], AX_X, ALU.add)\
                               .then_inc(sem("lam_dots"), 1)
                        dve.wait_ge(sem("lam_exped"), 1)
                        dve.tensor_tensor(lam_dot[:, 0:1], lam_exp[:, 1:2], lam_exp[:, 0:1], ALU.subtract)\
                           .then_inc(sem("lam_diff"), 1)
                        dve.wait_ge(sem("lam_diff"), 1)
                        dve.tensor_scalar(neg_lam[:, :], lam_dot[:, 0:1], -LAMBDA_INIT, None, ALU.add)
                        dve.wait_ge(sem("ada_summed"), 1)
                        dve.tensor_copy(ada_rows[:, 0, :], ps[:, 6, :]).then_inc(sem("ada_rows"), 1)
                        dve.wait_ge(sem("ada_turned"), 1)
                        ada_bias(dve, ADA_FIRST).then_inc(sem("ada_cols"), 1)
                        dve.wait_ge(sem("ada_cols"), 1)
                        ada_gain(dve, 0, 0, 0)
                        ada_gain(dve, 1, 0, 1)

        def gain_col(n):
            return lambda k: mod_gain[:, n, k:k + 1]

        def shift_col(l, v):
            return lambda k: ada_col[:, l, k, v:v + 1]

        h_stack = ExitStack()
        ctx_xt = residual[:, 5:7, :].rearrange("p r n -> p (r n)").rearrange("p (k n) -> p k n", k=KT)
        rstd_x, rstd_c = residual[:, 7, :], residual[:, 8, 0:CTX]
        in_raw = sb(h_stack, "in_raw", [P, KT, HALF_GROUP])
        in_hi = sb(h_stack, "in_hi", [P, 2, KT, HALF_GROUP], F32R)
        in_lo = sb(h_stack, "in_lo", [P, 2, KT, HALF_GROUP], F32R)
        w_in = a["even_w_in"].rearrange("e (k p) n -> p (e k) n", p=P)
        adaptive_parameters()
        h_hi = sb(h_stack, "h_hi", [P, KT, SEQ], F32R)
        h_lo = sb(h_stack, "h_lo", [P, KT, SEQ], F32R)
        hc_hi = sb(h_stack, "hc_hi", [P, KT, CTX], F32R)
        hc_lo = sb(h_stack, "hc_lo", [P, KT, CTX], F32R)
        x_t = fq[:, :, :, :].rearrange("p a b n -> p (a b n)").rearrange("p (k n) -> p k n", k=KT)

        kv = residual[:, :, :].rearrange("p r n -> p (r n)").rearrange("p (g t n) -> p g t n", g=2, t=KEYT)
        ROOT = 0.5 ** 0.5
        FOLDED = (7, 3, 1, 4, 0, 5, 2, 6)

        def even_projections():
            with ExitStack() as st:
                raw, w_hi, w_lo = in_raw, in_hi, in_lo
                gate = sb(st, "gate", [P, 2, SEQ])
                cos = sb(st, "cos", [P, RT, 2, 16])
                sin = sb(st, "sin", [P, RT, 2, 16])
                gain = sb(st, "qk_gain", [P, DH])
                stat = sb(st, "stat", [P, KEYT * 8])
                turn = sb(st, "turn", [P, BANK])
                u_f = fq[:, 0]
                k_nat, q_nat = kv[:, 0], fq[:, 1]
                norm_x = Norm("norm0", lambda k: x_t[:, k, :], SEQ, gain_col(0), shift_col(0, 0), lambda k: h_hi[:, k, :],
                              lambda k: h_lo[:, k, :], None, rstd_x, scaled=gate, rstd_elsewhere=True)
                norm_c = Norm("norm0c", lambda k: ctx_xt[:, k, :], CTX, gain_col(1), shift_col(0, 1),
                              lambda k: hc_hi[:, k, :], lambda k: hc_lo[:, k, :], None, rstd_c, scaled=gate,
                              rstd_elsewhere=True)
                g_raw = raw[:, :, :].rearrange("p k n -> p (k n)").rearrange("p (s k n) -> p s k n", s=2, k=KT)
                g_hi, g_lo = (w[:, :, :, :].rearrange("p s k n -> p (s k n)").rearrange("p (s k n) -> p s k n", s=4, k=KT)
                              for w in (w_hi, w_lo))
                N_UNITS = 8
                tiles_of = [KEYT if u < 4 else RT for u in range(N_UNITS)]
                first_tile = [sum(tiles_of[:u]) for u in range(N_UNITS + 1)]
                N_TILES = first_tile[N_UNITS]

                def row_tile(u, i):
                    return i if u >= 4 else (i + CT) % KEYT

                with nc.Block(name="even_in") as block:
                    @block.sync
                    def _(sp):
                        for tile, name in ((cos, "rope_cos"), (sin, "rope_sin")):
                            sp.dma_start(tile[:, :, :, :], a[name].rearrange("(r p) c f -> p r c f", p=P))\
                              .then_inc(sem("rope_in"), 16)
                        sp.dma_start(gain[:, :], a["even_k_norm"].broadcast_to([P, DH])).then_inc(sem("rope_in"), 16)
                        for u in range(1, N_UNITS):
                            c = (KV_COL + HALF_GROUP * u) if u < 4 else HALF_GROUP * (u - 4)
                            sp.wait_ge(sem("in_low"), u)
                            sp.dma_start(raw[:, :, :], w_in[:, :, c:c + HALF_GROUP]).then_inc(sem("in_landed"), 16)
                        sp.wait_ge(sem("k_scaled"), 1)
                        sp.dma_start(gain[:, :], a["even_q_norm"].broadcast_to([P, DH])).then_inc(sem("q_gain_in"), 16)
                        sp.wait_ge(sem("in_low"), N_UNITS)
                        for m in range(KT + 2):
                            if 2 <= m < KT:
                                sp.wait_ge(sem("gw_low"), m - 1)
                            if m < KT:
                                c = GATE_COL + m * P
                                sp.dma_start(g_raw[:, m % 2], w_in[:, :, c:c + P]).then_inc(sem(f"gw_landed{m % 2}"), 16)
                            if m >= 2:
                                sp.wait_ge(sem("gate_ready"), m - 1)
                                sp.dma_start(gate_scratch[m - 2], gate[:, m % 2, :]).then_inc(sem(f"gate_spilled{m % 2}"), 16)
                        for s in range(2):
                            sp.wait_ge(sem(f"gate_spilled{s}"), 16 * KT // 2)

                    @block.scalar
                    def _(act):
                        def high(u):
                            act.wait_ge(sem("in_landed"), 16 * (u + 1))
                            if u >= 2:
                                act.wait_ge(sem("in_done"), first_tile[u - 1])
                            split_high(act, w_hi[:, u % 2], raw[:, :, :], sem("in_high"))

                        def g_high(m):
                            act.wait_ge(sem(f"gw_landed{m % 2}"), 16 * (m // 2 + 1))
                            if m >= 2:
                                act.wait_ge(sem("gw_done"), m - 1)
                            else:
                                act.wait_ge(sem("in_done"), first_tile[7])
                            split_high(act, g_hi[:, m % 2], g_raw[:, m % 2], sem("gw_high"))

                        def root(n, t):
                            act.wait_ge(sem("qk_summed"), n + 1)
                            act.activation(stat[:, 0:t * 8], stat[:, 0:t * 8], ACT.Sqrt, bias=eps[:, 0:1], scale=1.0 / DH)\
                               .then_inc(sem("qk_rooted"), 1)

                        for k in range(KT):
                            norm_x.scalar_high(act, k)
                        high(1)
                        for k in range(KT):
                            norm_c.scalar_high(act, k)
                        act.wait_ge(sem("x_spilled"), 16 * KT)
                        for u in range(N_UNITS):
                            if 0 < u < N_UNITS - 1:
                                high(u + 1)
                            if u == 4:
                                root(0, KEYT)
                            if u == N_UNITS - 1:
                                g_high(0)
                                g_high(1)
                            half = HALF_GROUP * (u % 2)
                            for i in range(tiles_of[u]):
                                n = first_tile[u] + i
                                act.wait_ge(sem("in_done"), n + 1)
                                if u < 4:
                                    dst = kv[:, u // 2, row_tile(u, i), half:half + HALF_GROUP]
                                else:
                                    dst = fq[:, (u - 4) // 2, i, half:half + HALF_GROUP]
                                act.activation(dst, ps[:, n % 8, 0:HALF_GROUP], ACT.Copy).then_inc(sem("in_copied"), 1)
                        root(1, RT)
                        for m in range(KT):
                            act.wait_ge(sem("gw_done"), m + 1)
                            if m >= 2:
                                act.wait_ge(sem(f"gate_spilled{m % 2}"), 16 * (m // 2))
                            act.activation(gate[:, m % 2, :], pair[m % 4], ACT.Silu).then_inc(sem("gate_ready"), 1)
                            if m + 2 < KT:
                                g_high(m + 2)

                    @block.gpsimd
                    def _(pool):
                        for u in range(1, N_UNITS):
                            pool.wait_ge(sem("in_high"), u + 1)
                            if u >= 2:
                                pool.wait_ge(sem("in_done"), first_tile[u - 1])
                            split_low(pool, w_lo[:, u % 2], raw[:, :, :], w_hi[:, u % 2], sem("in_low"))
                        for m in range(KT):
                            pool.wait_ge(sem("gw_high"), m + 1)
                            split_low(pool, g_lo[:, m % 2], g_raw[:, m % 2], g_hi[:, m % 2], sem("gw_low"))

                    @block.tensor
                    def _(pe):
                        def part_products(u, n, k, hi, lo, r):
                            for x, w in ((hi, w_hi), (hi, w_lo), (lo, w_hi)):
                                last = pe.matmul(ps[:, n % 8, 0:HALF_GROUP], x[:, k, r * P:(r + 1) * P], w[:, u % 2, k, :],
                                                 start=(k == 0 and x is hi and w is w_hi), stop=(k == KT - 1 and x is lo))
                            return last

                        pe.wait_ge(sem("in_low"), 1)
                        for k in range(KT):
                            pe.wait_ge(norm_x.s("low"), k + 1)
                            for r in range(RT):
                                last = part_products(0, r, k, h_hi, h_lo, r)
                                if k == KT - 1:
                                    last.then_inc(sem("in_done"), 1)
                        pe.wait_ge(norm_c.s("low"), KT)
                        for u in range(N_UNITS):
                            pe.wait_ge(sem("in_low"), u + 1)
                            for i in range(RT if u == 0 else 0, tiles_of[u]):
                                n = first_tile[u] + i
                                if n >= 8:
                                    pe.wait_ge(sem("in_copied"), n - 7)
                                ctx_tile = i >= RT
                                hi, lo = (hc_hi, hc_lo) if ctx_tile else (h_hi, h_lo)
                                for k in range(KT):
                                    last = part_products(u, n, k, hi, lo, i - RT if ctx_tile else i)
                                last.then_inc(sem("in_done"), 1)
                        for m in range(KT):
                            pe.wait_ge(sem("gw_low"), m + 1)
                            if m < 4:
                                pe.wait_ge(sem("in_copied"), N_TILES - 8 + 2 * m + 2)
                            else:
                                pe.wait_ge(sem("gate_ready"), m - 3)
                            matmul3(pe, pair[m % 4], lambda k: g_hi[:, m % 2, k, :], lambda k: g_lo[:, m % 2, k, :],
                                    lambda k, c, e: h_hi[:, k, c:e], lambda k, c, e: h_lo[:, k, c:e], KT, SEQ)\
                                .then_inc(sem("gw_done"), 1)

                    @block.vector
                    def _(dve):
                        norm_x.vector_scale(dve)
                        dve.wait_ge(norm_x.s("low"), KT)
                        norm_c.vector_scale(dve)
                        rs = sem("rot_step")
                        n_rs = [0]

                        def step(instruction):
                            instruction.then_inc(rs, 1)
                            n_rs[0] += 1

                        def wait_steps():
                            dve.wait_ge(rs, n_rs[0])

                        def norm_and_rotate(n, nat, t):
                            heads = nat.rearrange("p t n -> p (t n)").rearrange("p (h d) -> p h d", d=DH)
                            for i in range(t):
                                step(dve.tensor_tensor(turn[:, :], nat[:, i, :], nat[:, i, :], ALU.mult))
                                wait_steps()
                                last = dve.tensor_reduce(stat[:, i * 8:(i + 1) * 8],
                                                         turn[:, :].rearrange("p (h d) -> p h d", d=DH), AX_X, ALU.add)
                                if i + 1 < t:
                                    step(last)
                                    wait_steps()
                            last.then_inc(sem("qk_summed"), 1)
                            dve.wait_ge(sem("qk_rooted"), n + 1)
                            step(dve.reciprocal(stat[:, 0:t * 8], stat[:, 0:t * 8]))
                            wait_steps()
                            step(dve.tensor_tensor(heads, heads, stat[:, 0:t * 8].unsqueeze(2).broadcast_to([P, t * 8, DH]),
                                                   ALU.mult))
                            wait_steps()
                            dve.wait_ge(*(sem("rope_in"), 48) if n == 0 else (sem("q_gain_in"), 16))
                            scaled = sem("q_scaled" if n else "k_scaled")
                            dve.tensor_tensor(heads, heads, gain[:, :].unsqueeze(1).broadcast_to([P, t * 8, DH]), ALU.mult)\
                               .then_inc(scaled, 1)
                            dve.wait_ge(scaled, 1)
                            for r in range(RT):
                                x_row = nat[:, t - RT + r, :].rearrange("p (h c j f) -> p h c j f", c=2, j=2, f=16)
                                x1, x2 = x_row[:, :, :, 0, :], x_row[:, :, :, 1, :]
                                cs, sn = (tab[:, r, :, :].unsqueeze(1).broadcast_to([P, 8, 2, 16]) for tab in (cos, sin))
                                s1, s2 = (turn[:, i * 2 * P:(i + 1) * 2 * P].rearrange("p (h c f) -> p h c f", h=8, c=2)
                                          for i in range(2))
                                step(dve.tensor_tensor(s1, x1, sn, ALU.mult))
                                step(dve.tensor_tensor(s2, x2, sn, ALU.mult))
                                wait_steps()
                                step(dve.tensor_tensor(x1, x1, cs, ALU.mult))
                                step(dve.tensor_tensor(x2, x2, cs, ALU.mult))
                                wait_steps()
                                step(dve.tensor_tensor(x1, x1, s2, ALU.subtract))
                                step(dve.tensor_tensor(x2, x2, s1, ALU.add))
                                wait_steps()

                        dve.wait_ge(sem("in_copied"), first_tile[2])
                        norm_and_rotate(0, k_nat, KEYT)

                        dve.wait_ge(sem("in_copied"), first_tile[6])
                        spare = turn[:, 0:BANK]
                        v = [u_f[:, i] for i in range(RT)]
                        even = [spare, v[0], v[1], v[2]]
                        for i in range(4):
                            step(dve.tensor_tensor(even[i], v[i], v[i + 4], ALU.add))
                            wait_steps()
                            step(dve.tensor_tensor(v[i + 4], v[i], v[i + 4], ALU.subtract))
                            wait_steps()
                        for sum_to, diff_to, p, q, plus, minus in ((v[3], v[2], even[3], even[1], ALU.add, ALU.subtract),
                                                                   (v[0], v[1], even[0], even[2], ALU.add, ALU.subtract),
                                                                   (spare, v[5], v[5], v[7], ALU.add, ALU.subtract)):
                            step(dve.tensor_tensor(sum_to, p, q, plus))
                            wait_steps()
                            step(dve.tensor_tensor(diff_to, p, q, minus))
                            wait_steps()
                        step(dve.tensor_tensor(v[7], v[0], v[3], ALU.add))
                        wait_steps()
                        step(dve.tensor_tensor(v[0], v[0], v[3], ALU.subtract))
                        wait_steps()
                        for s, dst, src, base, op in ((ROOT, v[3], v[5], v[4], ALU.add), (-ROOT, v[4], v[5], v[4], ALU.add),
                                                      (-ROOT, v[5], spare, v[6], ALU.subtract),
                                                      (-ROOT, v[6], spare, v[6], ALU.add)):
                            step(dve.scalar_tensor_tensor(out=dst, in0=src, scalar=s, in1=base, op0=ALU.mult, op1=op))
                            wait_steps()

                        dve.wait_ge(sem("in_copied"), N_TILES)
                        norm_and_rotate(1, q_nat, RT)

        even_projections()
        end_stage()
        h_stack.close()

        y_f = sb(fq_stack, "y_f", [P, F_GROUPS, SEQ])

        def fourier():
            with ExitStack() as st:
                tables = sb(st, "tables", [P, RADIX, 2, 2 * P])
                channel_dft = sb(st, "channel_dft", [P, 2, P])
                ft = sb(st, "ft", [P, 2, RADIX, 2, P])
                N_RAW = 5
                cond = sb(st, "cond_rest", [P, KT, 32])
                ada_raw = sb(st, "ada_raw_rest", [P, N_RAW, len(ADA_REST) * BANK])
                ada_rows = ada_raw[:, 0, 0:2 * BANK].rearrange("p (b n) -> p b n", b=2)
                GATE0 = ADA - GATE_COL
                STEPS = F_GROUPS * RADIX // 2

                with nc.Block(name="fourier") as block:
                    @block.sync
                    def _(sp):
                        sp.dma_start(tables[:, :, :, :], a["seq_dft"]).then_inc(sem("tables_in"), 16)
                        sp.dma_start(channel_dft[:, :, :], a["channel_dft"]).then_inc(sem("tables_in"), 16)
                        for k in range(KT):
                            if k >= N_RAW:
                                sp.wait_ge(sem("rest_ada_used"), k - N_RAW + 1)
                            rows = slice(k * P, (k + 1) * P)
                            sp.dma_start(ada_raw[:, k % N_RAW, 0:GATE0], a["ada_w"][0, rows, GATE_COL:ADA])\
                              .then_inc(sem(f"rest_ada_in{k % N_RAW}"), 16)
                            sp.dma_start(ada_raw[:, k % N_RAW, GATE0:], a["ada_w"][1, rows, :])\
                              .then_inc(sem(f"rest_ada_in{k % N_RAW}"), 16)

                    @block.tensor
                    def _(pe):
                        def ada(k):
                            pe.wait_ge(sem(f"rest_ada_in{k % N_RAW}"), 32 * (k // N_RAW + 1))
                            ada_product(pe, ADA_REST, 2, k, cond, ada_raw[:, k % N_RAW, :]).then_inc(sem("rest_ada_used"), 1)

                        pe.wait_ge(sem("tables_in"), 32)
                        pe.wait_ge(sem("rest_cond_ready"), 1)
                        for g in range(F_GROUPS):
                            for k1 in range(RADIX):
                                n = g * RADIX // 2 + k1 // 2
                                if n >= 2 and k1 % 2 == 0:
                                    pe.wait_ge(sem("ft_copied"), n - 1)
                                m = min(k1, RADIX - k1)
                                part = ps[:, n % 2, (k1 % 2) * 2 * P:(k1 % 2 + 1) * 2 * P]
                                complex_part = m not in (0, 4)
                                cols_g = slice(g * P, (g + 1) * P)
                                last = pe.matmul(part, fq[:, 0, FOLDED[m], cols_g], tables[:, k1, 0, :], start=True,
                                                 stop=not complex_part)
                                if complex_part:
                                    last = pe.matmul(part, fq[:, 0, FOLDED[m + 4], cols_g], tables[:, k1, 1, :],
                                                     start=False, stop=True)
                                if k1 % 2:
                                    last.then_inc(sem("ft_done"), 1)
                            ada(g)
                            pe.wait_ge(sem("ft_copied"), (g + 1) * RADIX // 2)
                            if g >= 2:
                                pe.wait_ge(sem("y_f_copied"), g - 1)
                            for half in range(2):
                                for part in range(2):
                                    last = pe.matmul(pair[2 + g % 2][:, half * BANK:(half + 1) * BANK],
                                                     channel_dft[:, part, :], ft[:, g % 2, 4 * half:4 * half + 4, part, :],
                                                     start=(part == 0), stop=(part == 1))
                            last.then_inc(sem("y_f_done"), 1)
                        for k in range(F_GROUPS, KT):
                            ada(k)
                        pe.wait_ge(sem("rest_ada_rows"), 1)
                        ada_turn(pe, ADA_REST, ada_rows).then_inc(sem("rest_ada_turned"), 1)

                    @block.scalar
                    def _(act):
                        for g in range(F_GROUPS):
                            for q in range(RADIX // 2):
                                n = g * RADIX // 2 + q
                                act.wait_ge(sem("ft_done"), n + 1)
                                if g >= 2 and q == 0:
                                    act.wait_ge(sem("y_f_done"), g - 1)
                                act.activation(ft[:, g % 2, 2 * q:2 * q + 2, :, :].rearrange("p k c n -> p (k c n)"),
                                               ps[:, n % 2, :], ACT.Copy).then_inc(sem("ft_copied"), 1)
                            act.wait_ge(sem("y_f_done"), g + 1)
                            act.activation(y_f[:, g, :].rearrange("p (k2 k1) -> p k1 k2", k1=RADIX),
                                           pair[2 + g % 2].rearrange("p (k1 k2) -> p k1 k2", k1=RADIX), ACT.Copy)\
                               .then_inc(sem("y_f_copied"), 1)

                    @block.vector
                    def _(dve):
                        dve.memset(cond[:, :, :], 0.0).then_inc(sem("rest_cond_zero"), 1)
                        dve.wait_ge(sem("rest_cond_zero"), 1)
                        dve.tensor_copy(cond[:, :, 0:2], cond_col[:, :, :]).then_inc(sem("rest_cond_ready"), 1)
                        dve.wait_ge(sem("rest_ada_used"), KT)
                        dve.tensor_copy(ada_rows[:, :, :], ps[:, 2:4, :]).then_inc(sem("rest_ada_rows"), 1)
                        dve.wait_ge(sem("rest_ada_turned"), 1)
                        ada_bias(dve, ADA_REST).then_inc(sem("rest_ada_cols"), 1)
                        dve.wait_ge(sem("rest_ada_cols"), 1)
                        ada_gain(dve, 2, 1, 0)

        fourier()
        end_stage()

        def attention():
            with ExitStack() as st:
                k_parts = sb(st, "k_parts", [P, KEYT, 2, 4, DH], F32R)
                q_parts = sb(st, "q_parts", [P, RT, 2, 2, DH], F32R)
                k_turned = sb(st, "k_turned", [P, 2, 2, KEYS], F32R)
                q_turned = sb(st, "q_turned", [P, 2, SEQ], F32R)
                prob = sb(st, "prob", [P, 2, 2, KEYS])
                mixed = sb(st, "mixed", [P, 2, KEYS])
                mixed_t = sb(st, "mixed_t", [P, 2, KEYS])
                v_head = sb(st, "v_head", [P, KEYT, DV])
                o_all = fq[:, 0].rearrange("p r n -> p (r n)").rearrange("p (h r n) -> p h r n", h=HEADS, r=RT)
                o_sq = prob[:, :, :, :].rearrange("p b m n -> p (b m n)")[:, 0:HEADS * RT * DV]
                o_stat = sb(st, "o_stat", [P, HEADS * RT])
                peak = sb(st, "peak", [P, RT, 2])
                neg_peak = sb(st, "neg_peak", [P, RT, 2])
                total = sb(st, "total", [P, RT, 2])
                inverse = sb(st, "inverse", [P, RT, 2])
                weight = sb(st, "weight", [P, RT])
                subln_gain = sb(st, "subln_gain", [P, 1])
                k_nat, v_nat, q_nat = kv[:, 0], kv[:, 1], fq[:, 1]
                ao_t = fq[:, 1].rearrange("p r n -> p (r n)").rearrange("p (h n) -> p h n", h=HEADS)
                score = [ps[:, 3 * m:3 * m + 3, :].rearrange("p b n -> p (b n)")[:, 0:KEYS] for m in range(2)]
                SPLIT, COMBINE = 1, 2
                chunks = [(k_turned[:, m, part, t * P:min(t + 4, KEYT) * P], [k_parts[:, i, m, 2 * part:2 * part + 2, :]
                           for i in range(t, min(t + 4, KEYT))]) for m in range(2) for part in range(2)
                          for t in range(0, KEYT, 4)]
                chunks += [(q_turned[:, m, t * P:(t + 4) * P], [q_parts[:, i, m, :, :] for i in range(t, t + 4)])
                           for m in range(2) for t in range(0, RT, 4)]
                NC = len(chunks)
                rounds = [(t, min(t + 4, KEYT)) for t in range(0, KEYT, 4)]
                NR = len(rounds)

                with nc.Block(name="attention") as block:
                    @block.scalar
                    def _(act):
                        with act.Fori(0, HEADS) as h:
                            hd = bass.ds(h * DV, DV)
                            k_src = k_nat[:, :, hd].rearrange("p t (m d) -> p t m d", m=2)
                            q_src = q_nat[:, :, hd].rearrange("p t (m d) -> p t m d", m=2)
                            act.wait_ge(sem("head_start"), h + 1)
                            act.activation(k_parts[:, :, :, 0, :], k_src, ACT.Copy).then_inc(sem("k_high"), 1)
                            act.activation(q_parts[:, :, :, 0, :], q_src, ACT.Copy).then_inc(sem("q_high"), 1)
                            act.activation(v_head[:, :, :], v_nat[:, :, hd], ACT.Copy).then_inc(sem("v_ready"), 1)
                            for c in range(0, NC, 2):
                                act.wait_ge(sem("part_turned"), h * NC + c + 1)
                                act.activation(chunks[c][0], ps[:, c % 8, 0:len(chunks[c][1]) * P], ACT.Copy)\
                                   .then_inc(sem("part_copied_act"), 1)

                            def turn_out(t, i):
                                b, e = rounds[i]
                                act.wait_ge(sem("mix_turned"), h * RT * NR + t * NR + i + 1)
                                if i == 0 and t >= 2:
                                    act.wait_ge(sem("o_done"), h * RT + t - 1)
                                act.activation(mixed_t[:, t % 2, b * P:e * P], ps[:, 6, 0:(e - b) * P], ACT.Copy)\
                                   .then_inc(sem(f"mix_copied{i}"), 1)

                            for t in range(RT):
                                if t >= 1:
                                    turn_out(t - 1, 0)
                                for m in range(2):
                                    act.wait_ge(sem("peaked"), h * 2 * RT + 2 * t + m + 1)
                                    if t >= 2 and m == 0:
                                        act.wait_ge(sem("mixed"), h * RT + t - 1)
                                    act.activation(prob[:, t % 2, m, :], score[m], ACT.Exp, bias=neg_peak[:, t, m:m + 1],
                                                   scale=ATTN_SCALE, accum_out=total[:, t, m:m + 1]).then_inc(sem("exped"), 1)
                                if t >= 1:
                                    turn_out(t - 1, 2)
                            turn_out(RT - 1, 0)
                            turn_out(RT - 1, 2)
                        act.wait_ge(sem("o_squared"), 1)
                        act.activation(o_stat[:, :], o_stat[:, :], ACT.Sqrt, bias=eps[:, 0:1], scale=1.0 / DV)\
                           .then_inc(sem("o_rooted"), 1)
                        for c in range(HEADS * RT // 4):
                            act.wait_ge(sem("o_turned"), c + 1)
                            act.activation(ao_t[:, c // 2, (c % 2) * BANK:(c % 2 + 1) * BANK], ps[:, c, :], ACT.Copy,
                                           scale=subln_gain[:, 0:1])

                    @block.vector
                    def _(dve):
                        dve.tensor_scalar(subln_gain[:, :], col(SUBLN, 0), 1.0 - LAMBDA_INIT, None, ALU.mult)
                        dve.sem_inc(sem("head_start"), 1)
                        with dve.Fori(0, HEADS) as h:
                            hd = bass.ds(h * DV, DV)
                            k_src = k_nat[:, :, hd].rearrange("p t (m d) -> p t m d", m=2)
                            q_src = q_nat[:, :, hd].rearrange("p t (m d) -> p t m d", m=2)
                            dve.wait_ge(sem("k_high"), h + 1)
                            for m in range(2):
                                dve.tensor_tensor(k_parts[:, :, m, 2, :], k_src[:, :, m, :], k_parts[:, :, m, 0, :].bitcast(F32),
                                                  ALU.subtract).then_inc(sem("k_low"), 1)
                            dve.wait_ge(sem("q_high"), h + 1)
                            for m in range(2):
                                dve.tensor_tensor(q_parts[:, :, m, 1, :], q_src[:, :, m, :], q_parts[:, :, m, 0, :].bitcast(F32),
                                                  ALU.subtract).then_inc(sem("q_low"), 1)
                            dve.wait_ge(sem("k_low"), h * 2 + 2)
                            for m in range(2):
                                for part in range(2):
                                    dve.tensor_copy(k_parts[:, :, m, 2 * part + 1, :],
                                                    k_parts[:, :, m, 2 * part, :].bitcast(F32)).then_inc(sem("k_twice"), 1)
                            for c in range(1, NC, 2):
                                dve.wait_ge(sem("part_turned"), h * NC + c + 1)
                                dve.tensor_copy(chunks[c][0], ps[:, c % 8, 0:len(chunks[c][1]) * P])\
                                   .then_inc(sem("part_copied_dve"), 1)

                            def combine(t):
                                dve.wait_ge(sem("exped"), h * 2 * RT + 2 * t + 2)
                                dve.reciprocal(inverse[:, t, :], total[:, t, :]).then_inc(sem("inverted"), 1)
                                dve.wait_ge(sem("inverted"), h * RT + t + 1)
                                dve.scalar_tensor_tensor(out=weight[:, t:t + 1], in0=total[:, t, 0:1], scalar=neg_lam[:, 0:1],
                                                         in1=inverse[:, t, 1:2], op0=ALU.mult, op1=ALU.mult)\
                                   .then_inc(sem("weighed"), 1)
                                dve.wait_ge(sem("weighed"), h * RT + t + 1)
                                if t >= 2:
                                    dve.wait_ge(sem("mix_turned"), h * RT * NR + (t - 1) * NR)
                                dve.scalar_tensor_tensor(out=mixed[:, t % 2, :], in0=prob[:, t % 2, 1, :],
                                                         scalar=weight[:, t:t + 1], in1=prob[:, t % 2, 0, :],
                                                         op0=ALU.mult, op1=ALU.add).then_inc(sem("mixed"), 1)

                            def finish(t):
                                dve.wait_ge(sem("o_done"), h * RT + t + 1)
                                dst = o_all[:, h, t, :]
                                dve.tensor_scalar(dst, ps[:, 7, (t % 2) * P:(t % 2 + 1) * P], inverse[:, t, 0:1], None, ALU.mult)\
                                   .then_inc(sem("o_scaled"), 1)

                            def turn_out(t):
                                b, e = rounds[1]
                                dve.wait_ge(sem("mix_turned"), h * RT * NR + t * NR + 2)
                                if t >= 2:
                                    dve.wait_ge(sem("o_done"), h * RT + t - 1)
                                dve.tensor_copy(mixed_t[:, t % 2, b * P:e * P], ps[:, 6, 0:(e - b) * P])\
                                   .then_inc(sem("mix_copied1"), 1)

                            for t in range(RT + 2):
                                if 1 <= t <= RT:
                                    combine(t - 1)
                                if t < RT:
                                    for m in range(2):
                                        n = h * 2 * RT + 2 * t + m
                                        dve.wait_ge(sem("scored"), n + 1)
                                        dve.tensor_reduce(peak[:, t, m:m + 1], score[m], AX_X, ALU.max).then_inc(sem("peak"), 1)
                                        dve.wait_ge(sem("peak"), n + 1)
                                        dve.tensor_scalar(neg_peak[:, t, m:m + 1], peak[:, t, m:m + 1], -ATTN_SCALE, None,
                                                          ALU.mult).then_inc(sem("peaked"), 1)
                                if 1 <= t <= RT:
                                    turn_out(t - 1)
                                if t >= 2:
                                    finish(t - 2)
                            dve.wait_ge(sem("o_scaled"), h * RT + RT)
                            dve.sem_inc(sem("head_start"), 1)
                        flat = fq[:, 0].rearrange("p r n -> p (r n)")
                        rows = flat.rearrange("p (n d) -> p n d", d=DV)
                        dve.tensor_tensor(o_sq, flat, flat, ALU.mult).then_inc(sem("o_sq"), 1)
                        dve.wait_ge(sem("o_sq"), 1)
                        dve.tensor_reduce(o_stat[:, :], o_sq.rearrange("p (n d) -> p n d", d=DV), AX_X, ALU.add)\
                           .then_inc(sem("o_squared"), 1)
                        dve.wait_ge(sem("o_rooted"), 1)
                        dve.reciprocal(o_stat[:, :], o_stat[:, :]).then_inc(sem("o_sq"), 1)
                        dve.wait_ge(sem("o_sq"), 2)
                        dve.tensor_tensor(rows, rows, o_stat[:, :].unsqueeze(2).broadcast_to([P, HEADS * RT, DV]), ALU.mult)\
                           .then_inc(sem("o_normed"), 1)

                    @block.tensor
                    def _(pe):
                        with pe.Fori(0, HEADS) as h:
                            pe.wait_ge(sem("k_twice"), h * 4 + 4)
                            pe.wait_ge(sem("q_low"), h * 2 + 2)
                            for c, (_, tiles) in enumerate(chunks):
                                if c >= 8:
                                    pe.wait_ge(sem("part_copied_act" if c % 2 == 0 else "part_copied_dve"),
                                               h * (NC // 2) + (c - 8) // 2 + 1)
                                for i, tile in enumerate(tiles):
                                    last = pe.transpose(ps[:, c % 8, i * P:(i + 1) * P],
                                                        tile.rearrange("p a d -> p (a d)").bitcast(F32), ident[:, :])
                                last.then_inc(sem("part_turned"), 1)
                            pe.wait_ge(sem("part_copied_act"), h * (NC // 2) + NC // 2)
                            pe.wait_ge(sem("part_copied_dve"), h * (NC // 2) + NC // 2)
                            pe.wait_ge(sem("v_ready"), h + 1)

                            def scores(t):
                                for m in range(2):
                                    if t >= 1:
                                        pe.wait_ge(sem("exped"), h * 2 * RT + 2 * (t - 1) + m + 1)
                                    for b in range(0, KEYS, BANK):
                                        e = min(b + BANK, KEYS)
                                        for part in range(2):
                                            last = pe.matmul(score[m][:, b:e], q_turned[:, m, t * P:(t + 1) * P],
                                                             k_turned[:, m, part, b:e], start=(part == 0), stop=(part == 1))
                                    last.then_inc(sem("scored"), 1)

                            def turn(t, i):
                                b, e = rounds[i]
                                if i == 0:
                                    pe.wait_ge(sem("mixed"), h * RT + t + 1)
                                if i or t:
                                    pe.wait_ge(sem(f"mix_copied{(i - 1) % NR}"), h * RT + t + (i > 0))
                                for j in range(b, e):
                                    last = pe.transpose(ps[:, 6, (j - b) * P:(j - b + 1) * P],
                                                        mixed[:, t % 2, j * P:(j + 1) * P], ident[:, :])
                                last.then_inc(sem("mix_turned"), 1)

                            def values(t, b, e):
                                if b == 0:
                                    for i in range(NR):
                                        pe.wait_ge(sem(f"mix_copied{i}"), h * RT + t + 1)
                                    if t >= 1:
                                        pe.wait_ge(sem("o_scaled"), h * RT + t)
                                for j in range(b, e):
                                    last = pe.matmul(ps[:, 7, (t % 2) * P:(t % 2 + 1) * P],
                                                     mixed_t[:, t % 2, j * P:(j + 1) * P], v_head[:, j, :],
                                                     start=(j == 0), stop=(j == KEYT - 1))
                                if e == KEYT:
                                    last.then_inc(sem("o_done"), 1)

                            for t in range(RT + 2):
                                if t < RT:
                                    scores(t)
                                turns, vals = 1 <= t <= RT, t >= 2
                                if turns:
                                    turn(t - 1, 0)
                                if vals:
                                    values(t - 2, 0, KEYT // 2)
                                if turns:
                                    turn(t - 1, 1)
                                if vals:
                                    values(t - 2, KEYT // 2, KEYT)
                                if turns:
                                    turn(t - 1, 2)
                        pe.wait_ge(sem("o_normed"), 1)
                        for c in range(HEADS * RT // 4):
                            for i in range(4):
                                t = 4 * (c % 2) + i
                                last = pe.transpose(ps[:, c, i * P:(i + 1) * P], o_all[:, c // 2, t, :], ident[:, :])
                            last.then_inc(sem("o_turned"), 1)

        attention()
        end_stage()

        res = residual[:, 0:KT, :]
        square_totals = [residual[:, KT + p, :] for p in range(2)]

        def even_output():
            with ExitStack() as st:
                y_hi = sb(st, "y_hi", [P, KT, SEQ], F32R)
                y_lo = sb(st, "y_lo", [P, KT, SEQ], F32R)
                gate = sb(st, "gate_in", [P, KT, SEQ])
                raw = fq[:, 0].rearrange("p r n -> p (r n)")[:, 0:2 * KT * P].rearrange("p (s k n) -> p s k n", s=2, k=KT)
                w_hi = sb(st, "out_hi", [P, 2, KT, P], F32R)
                w_lo = sb(st, "out_lo", [P, 2, KT, P], F32R)
                w_out = a["even_w_out"].rearrange("e (k p) n -> p (e k) n", p=P)
                attended = fq[:, 1].rearrange("p r n -> p (r n)").rearrange("p (k n) -> p k n", k=HEADS)

                squares = SquareSum("sq1", [gate[:, p, :] for p in range(2)])

                def mixed(k):
                    return y_f[:, k, :] if k < F_GROUPS else attended[:, k - F_GROUPS, :]


                with nc.Block(name="even_out") as block:
                    @block.sync
                    def _(sp):
                        for m in range(2):
                            sp.dma_start(raw[:, m], w_out[:, :, m * P:(m + 1) * P]).then_inc(sem(f"ow_landed{m}"), 16)
                        for k in range(KT):
                            sp.dma_start(gate[:, k, :], gate_scratch[k]).then_inc(sem(f"gate_back{k}"), 16)
                        sp.dma_start(res, x_scratch.rearrange("k p n -> p k n")).then_inc(sem("x_back"), 16)
                        for m in range(2, KT):
                            sp.wait_ge(sem("ow_low"), m - 1)
                            sp.dma_start(raw[:, m % 2], w_out[:, :, m * P:(m + 1) * P]).then_inc(sem(f"ow_landed{m % 2}"), 16)

                    @block.scalar
                    def _(act):
                        def high(m):
                            act.wait_ge(sem(f"ow_landed{m % 2}"), 16 * (m // 2 + 1))
                            if m >= 2:
                                act.wait_ge(sem("ow_done"), m - 1)
                            split_high(act, w_hi[:, m % 2], raw[:, m % 2], sem("ow_high"))

                        high(0)
                        high(1)
                        for k in range(KT):
                            act.wait_ge(sem("y_gated"), k + 1)
                            split_high(act, y_hi[:, k, :], gate[:, k, :], sem("y_high"))
                        for m in range(KT):
                            if m + 2 < KT:
                                high(m + 2)
                            act.wait_ge(sem("ow_added"), m + 1)
                            squares.scalar(act, m)

                    @block.gpsimd
                    def _(pool):
                        for m in range(KT):
                            pool.wait_ge(sem("ow_high"), m + 1)
                            split_low(pool, w_lo[:, m % 2], raw[:, m % 2], w_hi[:, m % 2], sem("ow_low"))
                            if m >= 5 and m % 2:
                                squares.add(pool, m - 2)
                        squares.add(pool, KT - 1)

                    @block.vector
                    def _(dve):
                        def low(k):
                            dve.wait_ge(sem("y_high"), k + 1)
                            split_low(dve, y_lo[:, k, :], gate[:, k, :], y_hi[:, k, :], sem("y_low"))

                        for k in range(KT):
                            dve.wait_ge(sem(f"gate_back{k}"), 16)
                            dve.tensor_tensor(gate[:, k, :], gate[:, k, :], mixed(k), ALU.mult).then_inc(sem("y_gated"), 1)
                            if k:
                                low(k - 1)
                        low(KT - 1)
                        dve.wait_ge(sem("x_back"), 16)
                        for m in range(KT):
                            dve.wait_ge(sem("ow_done"), m + 1)
                            dve.scalar_tensor_tensor(out=res[:, m, :], in0=pair[m % 2], scalar=ada_col[:, 0, 2 * KT + m, 0:1],
                                                     in1=res[:, m, :], op0=ALU.mult, op1=ALU.add).then_inc(sem("ow_added"), 1)
                            if m >= 2 and m % 2 == 0:
                                squares.add(dve, m)

                    @block.tensor
                    def _(pe):
                        pe.wait_ge(sem("ow_low"), 2)
                        for k in range(KT):
                            pe.wait_ge(sem("y_low"), k + 1)
                            for m in range(2):
                                last = channel_products(pe, pair[m], k, w_hi[:, m, k, :], w_lo[:, m, k, :], y_hi, y_lo)
                                if k == KT - 1:
                                    last.then_inc(sem("ow_done"), 1)
                        for m in range(2, KT):
                            pe.wait_ge(sem("ow_low"), m + 1)
                            pe.wait_ge(sem("ow_added"), m - 1)
                            matmul3(pe, pair[m % 2], lambda k: w_hi[:, m % 2, k, :], lambda k: w_lo[:, m % 2, k, :],
                                    lambda k, c, e: y_hi[:, k, c:e], lambda k, c, e: y_lo[:, k, c:e], KT, SEQ)\
                                .then_inc(sem("ow_done"), 1)

        even_output()
        end_stage()
        fq_stack.close()

        def load_unit(sp, kind, i, raw, src):
            sp.wait_ge(sem(kind + "_low"), i + 1)
            sp.dma_start(raw, src).then_inc(sem(kind + "_landed"), 16)

        def high_unit(act, kind, i, raw, hi, done_per_unit=1):
            act.wait_ge(sem(kind + "_landed"), (i + 1) * 16)
            act.wait_ge(sem(kind + "_done"), i * done_per_unit + 1)
            split_high(act, hi, raw, sem(kind + "_high"))

        def low_unit(pool, kind, i, raw, hi, lo, done_per_unit=1):
            pool.wait_ge(sem(kind + "_high"), i + 1)
            pool.wait_ge(sem(kind + "_done"), i * done_per_unit + 1)
            split_low(pool, lo, raw, hi, sem(kind + "_low"))

        def up_product(pe, kind, i, psum, hi, lo, h_hi, h_lo):
            pe.wait_ge(sem(kind + "_low"), i + 2)
            pe.wait_ge(sem(kind + "_free"), i + 1)
            matmul3(pe, psum, lambda k: hi[:, k, :], lambda k: lo[:, k, :],
                    lambda k, c, e: h_hi[:, k, c:e], lambda k, c, e: h_lo[:, k, c:e], KT, SEQ)\
                .then_inc(sem(kind + "_done"), 1)

        DOWN_PAIR = [(2, 3, 0)[d % 3] for d in range(KT)]

        def down_product(pe, kind, i, lent, lent_value, hi, lo, y_hi, y_lo, after=None):
            pe.wait_ge(sem(kind + "_low"), i + 2)
            pe.wait_ge(sem(kind + "_y_low"), i + 1)
            for d in range(KT):
                if d == 2:
                    pe.wait_ge(sem(lent), lent_value)
                else:
                    pe.wait_ge(sem(kind + "_free"), i * KT + (d if d > 2 else d + 1))
                matmul3(pe, pair[DOWN_PAIR[d]], lambda k: hi[:, d * P:(d + 1) * P], lambda k: lo[:, d * P:(d + 1) * P],
                        lambda k, c, e: y_hi[:, c:e], lambda k, c, e: y_lo[:, c:e], 1, SEQ)\
                    .then_inc(sem(kind + "_done"), 1)
                if after is not None:
                    after(d)

        def pair_0_returned(pe, kind, i):
            pe.wait_ge(sem(kind + "_free"), i * KT + 8)

        def odd_layer():
            with ExitStack() as st:
                h1_hi = sb(st, "h1_hi", [P, KT, SEQ], F32R)
                h1_lo = sb(st, "h1_lo", [P, KT, SEQ], F32R)
                kinds = ("cg", "xt", "bg", "gt")
                quarter = {"bg": 0, "cg": 1, "xt": 2, "gt": 3}
                raw = {k: sb(st, "raw_" + k, [P, KT, P]) for k in kinds}
                hi = {k: sb(st, "hi_" + k, [P, KT, P], F32R) for k in kinds}
                lo = {k: sb(st, "lo_" + k, [P, KT, P], F32R) for k in kinds}
                d_raw, d_hi, d_lo = sb(st, "d_raw", [P, D]), sb(st, "d_hi", [P, D], F32R), sb(st, "d_lo", [P, D], F32R)
                gates = sb(st, "gates", [P, 2, SEQ])
                c_gate, silu = gates[:, 0, :], gates[:, 1, :]
                u = sb(st, "u", [P, SEQ + 2])
                conv = sb(st, "conv", [P, SEQ])
                compact = sb(st, "compact1", [P, RT])
                norm = Norm("norm1", lambda k: res[:, k, :], SEQ, gain_col(2), shift_col(1, 0), lambda k: h1_hi[:, k, :],
                            lambda k: h1_lo[:, k, :], square_totals, pair[2], scaled=gates, mean=ps[:, 6, 0:RT],
                            compact=compact[:, :])
                squares = SquareSum("sq2", [c_gate, silu])
                y_hi = sb(st, "yo_hi", [P, SEQ], F32R)
                y_lo = sb(st, "yo_lo", [P, SEQ], F32R)
                taps = sb(st, "taps", [P, 3, KT])
                w_in = a["odd_w_in"].rearrange("e (k p) n -> p (e k) n", p=P)
                w_out = a["odd_w_out"].rearrange("e k n -> (e k) n")
                N = KT
                up_pair = {"cg": 0, "xt": 1, "bg": 0, "gt": 1}

                with nc.Block(name="odd") as block:
                    @block.sync
                    def _(sp):
                        def loads(j):
                            for k in ("bg", "cg", "xt", "gt"):
                                load_unit(sp, k, j, raw[k][:, :, :], w_in[:, :, bass.ds(j * P + quarter[k] * D, P)])
                            load_unit(sp, "dn", j, d_raw[:, :], w_out[bass.ds(j * P, P), :])

                        with sp.Fori(0, N) as j:
                            loads(j)

                    @block.scalar
                    def _(act):
                        def block_step(j, splits=True):
                            def next_high(k):
                                if splits:
                                    high_unit(act, k, j + 1, raw[k][:, :, :], hi[k][:, :, :])

                            act.wait_ge(sem("cg_done"), j + 2)
                            act.wait_ge(sem("u_done"), j + 1)
                            act.activation(c_gate, pair[0], ACT.Copy).then_inc(sem("cg_copied"), 1)
                            next_high("cg")
                            next_high("xt")
                            next_high("bg")
                            act.wait_ge(sem("gt_done"), j + 2)
                            act.wait_ge(sem("y_done"), j + 1)
                            act.activation(silu, pair[1], ACT.Silu).then_inc(sem("gt_silu"), 1)
                            next_high("gt")
                            act.wait_ge(sem("y_done"), j + 2)
                            high_unit(act, "dn", j, d_raw[:, :], d_hi[:, :], KT)
                            split_high(act, y_hi[:, :], conv[:, :], sem("y_split"))

                        norm.scalar_root(act)
                        for k in kinds[0:2]:
                            high_unit(act, k, 0, raw[k][:, :, :], hi[k][:, :, :])
                        for k in range(KT):
                            norm.scalar_high(act, k)
                        for k in kinds[2:4]:
                            high_unit(act, k, 0, raw[k][:, :, :], hi[k][:, :, :])
                        with act.Fori(0, N - 1) as j:
                            block_step(j)
                        block_step(N - 1, splits=False)
                        for d in range(KT):
                            act.wait_ge(sem("dn_free"), (N - 1) * KT + d + 3)
                            squares.scalar(act, d)

                    @block.gpsimd
                    def _(pool):
                        def lows(j):
                            for k in kinds:
                                low_unit(pool, k, j, raw[k][:, :, :], hi[k][:, :, :], lo[k][:, :, :])

                        def rest(j):
                            low_unit(pool, "dn", j, d_raw[:, :], d_hi[:, :], d_lo[:, :], KT)
                            pool.wait_ge(sem("y_split"), j + 1)
                            split_low(pool, y_lo[:, :], conv[:, :], y_hi[:, :], sem("dn_y_low"))

                        lows(0)
                        with pool.Fori(0, N - 1) as j:
                            lows(j + 1)
                            rest(j)
                        rest(N - 1)
                        for d in range(3, KT, 2):
                            squares.add(pool, d)

                    @block.vector
                    def _(dve):
                        for t in range(3):
                            dve.tensor_copy(taps[:, t, :], cols[:, ODD_CONV[0], ODD_CONV[1] + t * KT:ODD_CONV[1] + (t + 1) * KT])\
                               .then_inc(sem("taps_ready"), 1)
                        dve.memset(u[:, 0:1], 0.0).then_inc(sem("taps_ready"), 1)
                        dve.memset(u[:, SEQ + 1:SEQ + 2], 0.0).then_inc(sem("taps_ready"), 1)
                        dve.wait_ge(sem("taps_ready"), 5)
                        for name in [k + "_low" for k in kinds] + [k + "_done" for k in kinds] + \
                                [k + "_free" for k in ("cg", "xt")] + ["dn_low", "dn_done", "u_done", "y_done"]:
                            dve.sem_inc(sem(name), 1)
                        dve.sem_inc(sem("dn_free"), 2)

                        norm.vector_inverse(dve)
                        norm.vector_scale(dve)

                        def block_step(j):
                            dve.wait_ge(sem("cg_copied"), j + 1)
                            dve.wait_ge(sem("xt_done"), j + 2)
                            dve.tensor_tensor(u[:, 1:SEQ + 1], c_gate, pair[1], ALU.mult).then_inc(sem("u_done"), 1)
                            dve.wait_ge(sem("u_done"), j + 2)
                            dve.wait_ge(sem("dn_y_low"), j) if not isinstance(j, int) or j > 0 else None
                            conv_step = sem("conv_step")
                            dve.tensor_scalar(conv[:, :], u[:, 1:SEQ + 1], taps[:, 1, bass.ds(j, 1)], None, ALU.mult)\
                               .then_inc(conv_step, 1)
                            dve.wait_ge(conv_step, j * 3 + 1)
                            dve.scalar_tensor_tensor(out=conv[:, :], in0=u[:, 0:SEQ], scalar=taps[:, 0, bass.ds(j, 1)],
                                                     in1=conv[:, :], op0=ALU.mult, op1=ALU.add).then_inc(conv_step, 1)
                            dve.wait_ge(conv_step, j * 3 + 2)
                            dve.scalar_tensor_tensor(out=conv[:, :], in0=u[:, 2:SEQ + 2], scalar=taps[:, 2, bass.ds(j, 1)],
                                                     in1=conv[:, :], op0=ALU.mult, op1=ALU.add).then_inc(conv_step, 1)
                            dve.wait_ge(conv_step, j * 3 + 3)
                            dve.wait_ge(sem("bg_done"), j + 2)
                            dve.tensor_tensor(conv[:, :], pair[0], conv[:, :], ALU.mult).then_inc(sem("bg_used"), 1)

                        def last_product(j):
                            dve.wait_ge(sem("bg_used"), j + 1)
                            dve.wait_ge(sem("gt_silu"), j + 1)
                            dve.tensor_tensor(conv[:, :], conv[:, :], silu, ALU.mult).then_inc(sem("y_done"), 1)

                        def add(j, squared=False):
                            for d in range(KT):
                                dve.wait_ge(sem("dn_done"), j * KT + d + 2)
                                dve.scalar_tensor_tensor(out=res[:, d, :], in0=pair[DOWN_PAIR[d]],
                                                         scalar=ada_col[:, 1, 2 * KT + d, 0:1], in1=res[:, d, :],
                                                         op0=ALU.mult, op1=ALU.add).then_inc(sem("dn_free"), 1)
                                if squared and d >= 4 and d % 2 == 0:
                                    squares.add(dve, d - 2)
                            if squared:
                                squares.add(dve, KT - 2)

                        block_step(0)
                        last_product(0)
                        with dve.Fori(1, N) as j:
                            block_step(j)
                            add(j - 1)
                            last_product(j)
                        add(N - 1, squared=True)

                    @block.tensor
                    def _(pe):
                        def first_up():
                            for k in ("cg", "xt"):
                                pe.wait_ge(sem(k + "_low"), 2)
                            for q in range(KT):
                                pe.wait_ge(norm.s("low"), q + 1)
                                for k in ("cg", "xt"):
                                    last = channel_products(pe, pair[up_pair[k]], q, hi[k][:, q, :], lo[k][:, q, :], h1_hi, h1_lo)
                                    if q == KT - 1:
                                        last.then_inc(sem(k + "_done"), 1)

                        def up(j, units=(("cg", "bg_used"), ("xt", "gt_silu"), ("bg", "cg_copied"), ("gt", "u_done"))):
                            for k, free in units:
                                pe.wait_ge(sem(k + "_low"), j + 2)
                                if k in ("cg", "xt"):
                                    pe.wait_ge(sem(free), j)
                                elif k == "bg":
                                    pe.wait_ge(sem(free), j + 1)
                                else:
                                    pe.wait_ge(sem(free), j + 2)
                                matmul3(pe, pair[up_pair[k]], lambda q: hi[k][:, q, :], lambda q: lo[k][:, q, :],
                                        lambda q, c, e: h1_hi[:, q, c:e], lambda q, c, e: h1_lo[:, q, c:e], KT, SEQ)\
                                    .then_inc(sem(k + "_done"), 1)

                        def down(j, blocks_up):
                            down_product(pe, "dn", j, "bg_used", blocks_up, d_hi[:, :], d_lo[:, :], y_hi[:, :], y_lo[:, :])

                        norm.tensor(pe)
                        first_up()
                        up(0, (("bg", "cg_copied"), ("gt", "u_done")))
                        up(1)
                        down(0, 2)
                        with pe.Fori(2, N) as j:
                            pair_0_returned(pe, "dn", j - 2)
                            up(j)
                            down(j - 1, j + 1)
                        down(N - 1, N)

        odd_layer()
        end_stage()

        def pool_layer():
            with ExitStack() as st:
                h = sb(st, "hp", [P, KT, PAD + SEQ])
                raw = sb(st, "pw_raw", [P, 4 * 2, HALF_GROUP])
                w_hi = sb(st, "pw_hi", [P, 4 * 2, HALF_GROUP], F32R)
                w_lo = sb(st, "pw_lo", [P, 4 * 2, HALF_GROUP], F32R)
                inv = sb(st, "inv_count", [P, 4, PAD])
                d_hi = sb(st, "dp_hi", [P, KT, SEQ], F32R)
                window = sb(st, "window", [P, 2, PAD + SEQ])
                bias = sb(st, "pool_bias", [P, KT])
                d_lo = sb(st, "dp_lo", [P, KT, SEQ], F32R)
                edge = sb(st, "edge", [P, PAD])
                window_p = sb(st, "window_p", [P, 4, PAD + SEQ])
                compact = sb(st, "compact2", [P, RT])
                rstd = pair[0]
                norm = Norm("norm2", None, SEQ, None, None, None, None, square_totals, rstd, mean=ps[:, 2, 0:RT],
                            compact=compact[:, :])
                squares = SquareSum("sq3", [window_p[:, p, PAD:PAD + SEQ] for p in range(2)])
                ON_POOL = (5, 7)
                SCALE_ORDER = ON_POOL + tuple(k for k in range(KT) if k not in ON_POOL)

                def window_sums(eng, k, buffers, step, n_steps):
                    src, width, b = h[:, k], 1, 0
                    while width < WINDOWS[k // 2]:
                        if n_steps:
                            eng.wait_ge(step, n_steps)
                        eng.tensor_tensor(buffers[:, b, PAD:PAD + SEQ], src[:, PAD:PAD + SEQ],
                                          src[:, PAD - width:PAD + SEQ - width], ALU.add).then_inc(step, 1)
                        n_steps += 1
                        src, width, b = buffers[:, b], 2 * width, 1 - b
                    return src, n_steps

                with nc.Block(name="pool") as block:
                    @block.sync
                    def _(sp):
                        sp.dma_start(raw[:, :, :], a["pool_w_2"].rearrange("a g (k p) n -> p (a g k) n", p=P))\
                          .then_inc(sem("pw_landed"), 16)
                        sp.dma_start(inv[:, :, :], a["inv_count"].partition_broadcast(P)).then_inc(sem("inv_landed"), 16)

                    @block.scalar
                    def _(act):
                        norm.scalar_root(act)
                        act.wait_ge(sem("pw_landed"), 16)
                        split_high(act, w_hi[:, :, :], raw[:, :, :], sem("pw_high"))
                        for k in range(KT):
                            act.wait_ge(sem("pool_diff"), k + 1)
                            split_high(act, d_hi[:, k, :], h[:, k, PAD:PAD + SEQ], sem("pool_high"))
                        for m in range(KT + 1):
                            if m < KT:
                                act.wait_ge(sem("pool_done"), m + 1)
                                act.activation(h[:, m, PAD:PAD + SEQ], pair[m % 4], ACT.Identity, scale=col(POOL_SCALE, m),
                                               bias=bias[:, m:m + 1]).then_inc(sem("pool_scaled"), 1)
                            if m:
                                act.wait_ge(sem("pool_added"), m)
                                squares.scalar(act, m - 1)

                    @block.gpsimd
                    def _(pool):
                        for b in range(4):
                            pool.memset(window_p[:, b, 0:PAD], 0.0).then_inc(sem("window_p_step"), 1)
                        n_steps = 4
                        pool.wait_ge(sem("pw_high"), 1)
                        split_low(pool, w_lo[:, :, :], raw[:, :, :], w_hi[:, :, :], sem("pw_low"))
                        for i, k in enumerate(ON_POOL):
                            pool.wait_ge(sem("pool_normed"), i + 1)
                            _, n_steps = window_sums(pool, k, window_p[:, 2 * i:2 * i + 2], sem("window_p_step"), n_steps)
                            pool.wait_ge(sem("window_p_step"), n_steps)
                            pool.sem_inc(sem("window_p_ready"), 1)
                        for k in range(KT - 1):
                            pool.wait_ge(sem("pool_high"), k + 1)
                            split_low(pool, d_lo[:, k, :], h[:, k, PAD:PAD + SEQ], d_hi[:, k, :], sem("pool_low"))
                        for m in range(3, KT, 2):
                            squares.add(pool, m)

                    @block.vector
                    def _(dve):
                        ws = sem("window_step")
                        n_ws = 0
                        for k in range(KT):
                            dve.memset(h[:, k, 0:PAD], 0.0).then_inc(ws, 1)
                        for b in range(2):
                            dve.memset(window[:, b, 0:PAD], 0.0).then_inc(ws, 1)
                        dve.tensor_tensor(bias[:, :], cols[:, POOL_B[0], POOL_B[1]:POOL_B[1] + KT],
                                          cols[:, POOL_SCALE[0], POOL_SCALE[1]:POOL_SCALE[1] + KT], ALU.mult).then_inc(ws, 1)
                        n_ws = KT + 3
                        norm.vector_inverse(dve)
                        dve.wait_ge(norm.s("spread"), 1)
                        for k in SCALE_ORDER:
                            dve.scalar_tensor_tensor(out=h[:, k, PAD:PAD + SEQ], in0=res[:, k, :], scalar=col(MIX_G, k), in1=rstd,
                                                     op0=ALU.mult, op1=ALU.mult).then_inc(sem("pool_normed"), 1)
                        dve.wait_ge(sem("inv_landed"), 16)
                        dve.wait_ge(sem("pool_normed"), KT)

                        def difference(k, src):
                            nonlocal n_ws
                            dve.tensor_tensor(edge[:, :], src[:, PAD:2 * PAD], inv[:, k // 2, :], ALU.mult).then_inc(ws, 1)
                            n_ws += 1
                            dve.wait_ge(ws, n_ws)
                            dve.tensor_tensor(h[:, k, PAD:2 * PAD], edge[:, :], h[:, k, PAD:2 * PAD], ALU.subtract)\
                               .then_inc(ws, 1)
                            n_ws += 1
                            dve.wait_ge(ws, n_ws)
                            dve.scalar_tensor_tensor(out=h[:, k, 2 * PAD:PAD + SEQ], in0=src[:, 2 * PAD:PAD + SEQ],
                                                     scalar=1.0 / WINDOWS[k // 2], in1=h[:, k, 2 * PAD:PAD + SEQ],
                                                     op0=ALU.mult, op1=ALU.subtract).then_inc(sem("pool_diff"), 1)
                            dve.wait_ge(sem("pool_diff"), k + 1)

                        for k in range(KT):
                            if k in ON_POOL:
                                i = ON_POOL.index(k)
                                dve.wait_ge(sem("window_p_ready"), i + 1)
                                src = window_p[:, 2 * i + k // 2 % 2]
                            else:
                                src, n_ws = window_sums(dve, k, window, ws, n_ws)
                                dve.wait_ge(ws, n_ws)
                            difference(k, src)
                        dve.wait_ge(sem("pool_high"), KT)
                        split_low(dve, d_lo[:, KT - 1, :], h[:, KT - 1, PAD:PAD + SEQ], d_hi[:, KT - 1, :], sem("pool_last_low"))
                        for m in range(KT):
                            dve.wait_ge(sem("pool_scaled"), m + 1)
                            dve.tensor_tensor(res[:, m, :], res[:, m, :], h[:, m, PAD:PAD + SEQ], ALU.add)\
                               .then_inc(sem("pool_added"), 1)
                            if m >= 3 and m % 2:
                                squares.add(dve, m - 1)

                    @block.tensor
                    def _(pe):
                        norm.tensor(pe)
                        pe.wait_ge(sem("pw_low"), 1)
                        for m in range(KT):
                            g, half = m // 2, (m % 2) * P
                            pe.wait_ge(sem("pool_low"), min(2 * g + 2, KT - 1))
                            if m == KT - 2:
                                pe.wait_ge(sem("pool_last_low"), 1)
                            if m >= 4:
                                pe.wait_ge(sem("pool_scaled"), m - 3)
                            matmul3(pe, pair[m % 4], lambda k: w_hi[:, 2 * g + k, half:half + P],
                                    lambda k: w_lo[:, 2 * g + k, half:half + P],
                                    lambda k, c, e: d_hi[:, 2 * g + k, c:e], lambda k, c, e: d_lo[:, 2 * g + k, c:e], 2, SEQ)\
                                .then_inc(sem("pool_done"), 1)

        pool_layer()
        end_stage()

        def ffn_layer():
            with ExitStack() as st:
                zero = sb(st, "zero", [P, KT])
                h2_hi = sb(st, "h2_hi", [P, KT, SEQ], F32R)
                h2_lo = sb(st, "h2_lo", [P, KT, SEQ], F32R)
                kinds = ("va", "ga")
                raw = {k: sb(st, "raw_" + k, [P, KT, P]) for k in kinds}
                hi = {k: sb(st, "hi_" + k, [P, KT, P], F32R) for k in kinds}
                lo = {k: sb(st, "lo_" + k, [P, KT, P], F32R) for k in kinds}
                f_raw, f_hi, f_lo = sb(st, "f_raw", [P, D]), sb(st, "f_hi", [P, D], F32R), sb(st, "f_lo", [P, D], F32R)
                branch = {k: sb(st, "branch_" + k, [P, SEQ]) for k in kinds}
                scaled = sb(st, "scaled3", [P, 2, SEQ])
                compact = sb(st, "compact3", [P, RT])
                norm = Norm("norm3", lambda k: res[:, k, :], SEQ, lambda k: col(FFN_G, k), lambda k: zero[:, k:k + 1],
                            lambda k: h2_hi[:, k, :], lambda k: h2_lo[:, k, :], square_totals, pair[2], scaled=scaled,
                            mean=ps[:, 6, 0:RT], compact=compact[:, :])
                rows_out = sb(st, "rows_out", [P, RT, D])
                out_rows = out.rearrange("b (r p) d -> p (b r) d", p=P)
                y_hi = sb(st, "yf_hi", [P, SEQ], F32R)
                y_lo = sb(st, "yf_lo", [P, SEQ], F32R)
                w_in = a["ffn_w_in_2"].rearrange("e (k p) n -> p (e k) n", p=P)
                w_out = a["ffn_w_out_2"].rearrange("e k n -> (e k) n")
                first = {"va": 0, "ga": FFN_T}
                up_pair = {"va": 0, "ga": 1}
                N = FFN_T

                def tap(where, k, j):
                    return cols[:, where[0], bass.ds(j + (where[1] + first[k]), 1)]

                with nc.Block(name="ffn") as block:
                    @block.sync
                    def _(sp):
                        with sp.Fori(0, N) as j:
                            for k in kinds:
                                load_unit(sp, k, j, raw[k][:, :, :], w_in[:, :, bass.ds(j * P + first[k] * P, P)])
                            load_unit(sp, "fd", j, f_raw[:, :], w_out[bass.ds(j * P, P), :])
                        for d in range(KT):
                            sp.wait_ge(sem("out_copied"), 2 * d + 2)
                            sp.dma_start(out_rows[:, :, d * P:(d + 1) * P], rows_out[:, :, d * P:(d + 1) * P])\
                              .then_inc(sem("stored"), 16)
                        sp.wait_ge(sem("stored"), 16 * KT)

                    @block.scalar
                    def _(act):
                        def block_step(j, splits=True):
                            for k in kinds:
                                act.wait_ge(sem(k + "_done"), j + 2)
                                act.wait_ge(sem("fd_y_free"), j + 1)
                                act.activation(branch[k][:, :], pair[up_pair[k]], ACT.Identity, scale=tap(FFN_TAP2, k, j),
                                               bias=tap(FFN_B, k, j)).then_inc(sem(k + "_tap2"), 1)
                                if splits:
                                    high_unit(act, k, j + 1, raw[k][:, :, :], hi[k][:, :, :])
                            high_unit(act, "fd", j, f_raw[:, :], f_hi[:, :], KT)
                            act.wait_ge(sem("ga_free"), j + 2)
                            act.activation(branch["ga"][:, :], branch["ga"][:, :], ACT.Silu).then_inc(sem("ga_silu"), 1)
                            act.wait_ge(sem("fy_done"), j + 1)
                            split_high(act, y_hi[:, :], branch["va"][:, :], sem("fy_split"))

                        norm.scalar_root(act)
                        for k in kinds:
                            high_unit(act, k, 0, raw[k][:, :, :], hi[k][:, :, :])
                        for k in range(KT):
                            norm.scalar_high(act, k)
                        with act.Fori(0, N - 1) as j:
                            block_step(j)
                        block_step(N - 1, splits=False)
                        for n in range(2 * KT):
                            d, half = n // 2, n % 2
                            act.wait_ge(sem("out_turned"), n + 1)
                            act.activation(rows_out[:, 4 * half:4 * half + 4, d * P:(d + 1) * P],
                                           ps[:, 2 + half, :].rearrange("p (r n) -> p r n", n=P), ACT.Copy)\
                               .then_inc(sem("out_copied"), 1)

                    @block.gpsimd
                    def _(pool):
                        def lows(j):
                            for k in kinds:
                                low_unit(pool, k, j, raw[k][:, :, :], hi[k][:, :, :], lo[k][:, :, :])

                        def rest(j):
                            low_unit(pool, "fd", j, f_raw[:, :], f_hi[:, :], f_lo[:, :], KT)
                            pool.wait_ge(sem("fy_split"), j + 1)
                            split_low(pool, y_lo[:, :], branch["va"][:, :], y_hi[:, :], sem("fd_y_low"))
                            pool.wait_ge(sem("fd_y_low"), j + 1)
                            pool.sem_inc(sem("fd_y_free"), 1)

                        lows(0)
                        with pool.Fori(0, N - 1) as j:
                            lows(j + 1)
                            rest(j)
                        rest(N - 1)

                    @block.vector
                    def _(dve):
                        dve.memset(zero[:, :], 0.0).then_inc(sem("zeroed"), 1)
                        for name in [k + s for k in kinds for s in ("_low", "_done", "_free")] + ["fd_low", "fd_done", "fd_y_free"]:
                            dve.sem_inc(sem(name), 1)
                        dve.sem_inc(sem("fd_free"), 2)
                        dve.wait_ge(sem("zeroed"), 1)
                        norm.vector_inverse(dve)
                        norm.vector_scale(dve)

                        def taps(k, j):
                            x, y = pair[up_pair[k]], branch[k]
                            dve.wait_ge(sem(k + "_tap2"), j + 1)
                            dve.scalar_tensor_tensor(out=y[:, 1:SEQ], in0=x[:, 0:SEQ - 1], scalar=tap(FFN_TAP1, k, j),
                                                     in1=y[:, 1:SEQ], op0=ALU.mult, op1=ALU.add).then_inc(sem(k + "_tap1"), 1)
                            dve.wait_ge(sem(k + "_tap1"), j + 1)
                            dve.scalar_tensor_tensor(out=y[:, 2:SEQ], in0=x[:, 0:SEQ - 2], scalar=tap(FFN_TAP0, k, j),
                                                     in1=y[:, 2:SEQ], op0=ALU.mult, op1=ALU.add).then_inc(sem(k + "_free"), 1)

                        def product(j):
                            dve.wait_ge(sem("ga_silu"), j + 1)
                            dve.wait_ge(sem("va_free"), j + 2)
                            dve.tensor_tensor(branch["va"][:, :], branch["va"][:, :], branch["ga"][:, :], ALU.mult)\
                               .then_inc(sem("fy_done"), 1)

                        def add(j):
                            for d in range(KT):
                                dve.wait_ge(sem("fd_done"), j * KT + d + 2)
                                dve.tensor_tensor(res[:, d, :], pair[DOWN_PAIR[d]], res[:, d, :], ALU.add)\
                                   .then_inc(sem("fd_free"), 1)

                        taps("va", 0)
                        taps("ga", 0)
                        product(0)
                        with dve.Fori(1, N) as j:
                            taps("va", j)
                            add(j - 1)
                            taps("ga", j)
                            product(j)
                        add(N - 1)

                    @block.tensor
                    def _(pe):
                        def up(j):
                            for k in kinds:
                                up_product(pe, k, j, pair[up_pair[k]], hi[k], lo[k], h2_hi, h2_lo)

                        def down(j, blocks_up, after=None):
                            down_product(pe, "fd", j, "va_free", blocks_up + 1, f_hi[:, :], f_lo[:, :], y_hi[:, :], y_lo[:, :],
                                         after)

                        def turn_out(d):
                            pe.wait_ge(sem("fd_free"), (N - 1) * KT + d + 3)
                            for half in range(2):
                                if d:
                                    pe.wait_ge(sem("out_copied"), 2 * d - 1 + half)
                                for r in range(4 * half, 4 * half + 4):
                                    last = pe.transpose(ps[:, 2 + half, (r % 4) * P:(r % 4 + 1) * P],
                                                        res[:, d, r * P:(r + 1) * P], ident[:, :])
                                last.then_inc(sem("out_turned"), 1)

                        norm.tensor(pe)
                        for k in kinds:
                            pe.wait_ge(sem(k + "_low"), 2)
                        for q in range(KT):
                            pe.wait_ge(norm.s("low"), q + 1)
                            for k in kinds:
                                last = channel_products(pe, pair[up_pair[k]], q, hi[k][:, q, :], lo[k][:, q, :], h2_hi, h2_lo)
                                if q == KT - 1:
                                    last.then_inc(sem(k + "_done"), 1)
                        up(1)
                        down(0, 2)
                        with pe.Fori(2, N) as j:
                            pair_0_returned(pe, "fd", j - 2)
                            up(j)
                            down(j - 1, j + 1)
                        down(N - 1, N, lambda d: turn_out(d - 2) if d >= 2 else None)
                        turn_out(KT - 2)
                        turn_out(KT - 1)

        ffn_layer()


_INS = ["x", "c", "ctx", "c_ctx", "norm_g", "ada_w", "ada_b", "even_w_in", "even_q_norm", "even_k_norm",
        "even_lambda_q1", "even_lambda_k1", "even_lambda_q2", "even_lambda_k2", "even_subln", "even_w_out",
        "odd_w_in", "odd_conv_w", "odd_w_out", "norm_mix_g_2", "norm_ffn_g_2", "pool_w_2", "pool_b_2",
        "pool_scale_2", "ffn_w_in_2", "ffn_conv_w_2", "ffn_conv_b_2", "ffn_w_out_2"]


def _constants():
    import numpy as np
    c = {"identity": np.eye(P, dtype=np.float32)}
    grid = 64
    pos = np.arange(SEQ)
    half = DH // 2
    freqs = np.float32(10000.0) ** (-np.arange(0, half, 2, dtype=np.float32) / np.float32(half))
    ang = np.stack([(p.astype(np.float32)[:, None] * freqs) for p in (pos // grid, pos % grid)], axis=1)
    c["rope_cos"] = np.cos(ang.astype(np.float64)).astype(np.float32)
    c["rope_sin"] = np.sin(ang.astype(np.float64)).astype(np.float32)
    p, k2 = np.arange(P)[:, None], np.arange(P)[None, :]
    dft = np.zeros((P, RADIX, 2, 2 * P))
    for k1 in range(RADIX):
        th = 2 * np.pi * ((p * (k1 + RADIX * k2)) % SEQ) / SEQ
        conj = -1.0 if k1 > RADIX // 2 else 1.0
        dft[:, k1, 0] = np.concatenate([np.cos(th), -np.sin(th)], axis=1)
        dft[:, k1, 1] = conj * np.concatenate([np.sin(th), np.cos(th)], axis=1)
    c["seq_dft"] = dft.astype(np.float32)
    th = 2 * np.pi * ((p * k2) % P) / P
    c["channel_dft"] = (np.stack([np.cos(th), np.sin(th)], axis=1) / np.sqrt(SEQ * P)).astype(np.float32)
    t = np.arange(PAD)
    c["inv_count"] = np.stack([1.0 / np.minimum(t + 1, w) for w in WINDOWS]).astype(np.float32)
    return c


def kernel(**inputs):
    import numpy as np
    import concourse.bacc as bacc
    from concourse.bass_utils import run_bass_kernel_spmd

    nc = bacc.Bacc("TRN2", target_bir_lowering=False, num_devices=1)
    arrays, aps = {}, {}
    named = {n: np.ascontiguousarray(inputs[n]) for n in _INS}
    for name, value in {**named, **_constants()}.items():
        arrays[f"in_{name}"] = value
        aps[name] = nc.dram_tensor(f"in_{name}", value.shape, mybir.dt.from_np(value.dtype), kind="ExternalInput").ap()
    out = nc.dram_tensor("out", (1, SEQ, D), F32, kind="ExternalOutput").ap()
    program(nc, aps, out)
    result = run_bass_kernel_spmd(nc, [arrays], core_ids=[0])
    return result.results[0]["out"]
```

```python
from contextlib import ExitStack

import concourse.bass as bass
from concourse import mybir

ALU = mybir.AluOpType
ACT = mybir.ActivationFunctionType
F32 = mybir.dt.float32
F32R = mybir.dt.float32r
AX_X = mybir.AxisListType.X

P = 128
D = 1024
KT = D // P
SEQ = 1024
RT = SEQ // P
CTX = 256
CT = CTX // P
BANK = 512
EPS = 1e-6
HEADS = 4
DH = 64
DV = 2 * DH
QK = HEADS * 2 * DH
KEYS = CTX + SEQ
KEYT = KEYS // P
ATTN_SCALE = DH ** -0.5
LAMBDA_INIT = 0.2
F_GROUPS = 4
RADIX = 8
HALF_GROUP = 256
ADA = 3 * D
ADA_T = ADA // P
FFN = 2816
FFN_T = FFN // P
WINDOWS = (2, 4, 8, 16)
PAD = 16
GATE_COL = 2048
KV_COL = 1024

NORM_G, ADA_B, ODD_CONV, MIX_G, FFN_G, C_VEC, C_CTX = ((0, o) for o in (0, 16, 64, 88, 96, 104, 112))
POOL_B, POOL_SCALE, FFN_B, FFN_TAP0 = ((1, o) for o in (0, 8, 16, 60))
FFN_TAP1, FFN_TAP2, SUBLN = ((2, o) for o in (0, 44, 88))
ROWS = (120, 104, 89)


def program(nc, a, out):
    ctx = ExitStack()
    with ctx:
        sems = {}

        def sem(name):
            if name not in sems:
                sems[name] = nc.alloc_semaphore(name)
            return sems[name]

        def end_stage():
            nc.clear_and_free_semaphores(list(sems.values()))
            sems.clear()
            nc.all_engine_barrier()

        def sb(stack, name, shape, dt=F32):
            return stack.enter_context(nc.sbuf_tensor(name, shape, dt))

        ps = ctx.enter_context(nc.psum_tensor("ps", [P, 8, BANK], F32))
        pair = [ps[:, 2 * i:2 * i + 2, :].rearrange("p b n -> p (b n)") for i in range(4)]

        ident = sb(ctx, "ident", [P, P])
        ones = sb(ctx, "ones", [P, P])
        eps = sb(ctx, "eps", [P, 1])
        cols = sb(ctx, "cols", [P, 3, P])
        ada_col = sb(ctx, "ada_col", [P, 2, ADA_T, 2])
        mod_gain = sb(ctx, "mod_gain", [P, 3, KT])
        neg_lam = sb(ctx, "neg_lam", [P, 1])
        cond_col = sb(ctx, "cond_col", [P, KT, 2])
        residual = sb(ctx, "residual", [P, KEYT, D])
        fq_stack = ExitStack()
        fq = sb(fq_stack, "fq", [P, 2, RT, QK])
        gate = sb(fq_stack, "gate", [P, 2, SEQ])
        SPILLED = KT - 2

        x_scratch = nc.dram_tensor("x_scratch", [KT, P, SEQ], F32).ap()
        gate_scratch = nc.dram_tensor("gate_scratch", [KT - 2, P, SEQ], F32).ap()

        def col(where, j):
            return cols[:, where[0], where[1] + j:where[1] + j + 1]

        def matmul3(pe, psum, w_hi, w_lo, a_hi, a_lo, n_k, n):
            for k in range(n_k):
                for w, act in ((w_hi, a_hi), (w_hi, a_lo), (w_lo, a_hi)):
                    for c in range(0, n, BANK):
                        e = min(c + BANK, n)
                        last = pe.matmul(psum[:, c:e], w(k), act(k, c, e), start=(k == 0 and w is w_hi and act is a_hi),
                                         stop=(k == n_k - 1 and w is w_lo))
            return last

        def channel_products(pe, psum, k, step, w_hi, w_lo, a_hi, a_lo):
            for part, (w, act) in enumerate(((w_hi, a_hi), (w_hi, a_lo), (w_lo, a_hi))):
                for c in range(0, SEQ, BANK):
                    last = pe.matmul(psum[:, c:c + BANK], w, act[:, k, c:c + BANK],
                                     start=(step == 0 and part == 0), stop=(step == KT - 1 and part == 2))
            return last

        def split_high(act, dst, src, done):
            return act.activation(dst, src, ACT.Copy).then_inc(done, 1)

        def split_low(eng, dst, src, high, done):
            return eng.tensor_tensor(dst, src, high.bitcast(F32), ALU.subtract).then_inc(done, 1)

        class Norm:

            def __init__(self, tag, x, n, gain, shift, high, low, total, rstd, square=None, scaled=None,
                         mean=None, compact=None, kept=None, rstd_elsewhere=False):
                self.tag, self.x, self.n, self.gain, self.shift = tag, x, n, gain, shift
                self.high, self.low, self.mean = high, low, mean
                self.square, self.total, self.rstd, self.scaled = square, total, rstd, scaled
                self.compact, self.kept = compact, kept
                self.rstd_elsewhere = rstd_elsewhere

            def s(self, what):
                return sem(self.tag + "_" + what)

            def scalar_square(self, act, k):
                dst = self.total if k == 0 else self.square[:, k % 2, 0:self.n]
                if k >= 3:
                    act.wait_ge(self.s("summed"), k - 2)
                act.activation(dst, self.x(k), ACT.Square).then_inc(self.s("squared"), 1)

            def scalar_root(self, act):
                if self.total is not None:
                    act.wait_ge(self.s("meaned"), 1)
                act.activation(self.compact, self.mean, ACT.Sqrt, bias=eps[:, 0:1], scale=1.0 / D)\
                   .then_inc(self.s("rooted"), 1)

            def scalar_high(self, act, k):
                act.wait_ge(self.s("scaled"), k + 1)
                act.activation(self.high(k), self.scaled[:, k % 2, 0:self.n], ACT.Identity, bias=self.shift(k))\
                   .then_inc(self.s("high"), 1)

            def vector_sum(self, dve):
                for k in range(1, KT):
                    dve.wait_ge(self.s("squared"), k + 1)
                    if k > 1:
                        dve.wait_ge(self.s("summed"), k - 1)
                    dve.tensor_tensor(self.total, self.total, self.square[:, k % 2, 0:self.n], ALU.add)\
                       .then_inc(self.s("summed"), 1)

            def vector_inverse(self, dve):
                dve.wait_ge(self.s("rooted"), 1)
                dve.reciprocal(self.compact, self.compact).then_inc(self.s("inverse"), 1)

            def vector_keep(self, dve):
                dve.wait_ge(self.s("spread"), 1)
                return dve.tensor_copy(self.kept, self.rstd)

            def vector_scale(self, dve):
                if not self.rstd_elsewhere:
                    dve.wait_ge(self.s("spread"), 1)

                def scale(k):
                    dst = self.scaled[:, k % 2, 0:self.n]
                    dve.scalar_tensor_tensor(out=dst, in0=self.x(k), scalar=self.gain(k), in1=self.rstd,
                                             op0=ALU.mult, op1=ALU.mult).then_inc(self.s("scaled"), 1)

                scale(0)
                for k in range(KT):
                    if k + 1 < KT:
                        if k >= 1:
                            dve.wait_ge(self.s("low"), k)
                        scale(k + 1)
                    dve.wait_ge(self.s("high"), k + 1)
                    dve.scalar_tensor_tensor(out=self.low(k), in0=self.scaled[:, k % 2, 0:self.n], scalar=self.shift(k),
                                             in1=self.high(k).bitcast(F32), op0=ALU.add, op1=ALU.subtract)\
                       .then_inc(self.s("low"), 1)

            def tensor_mean(self, pe, sums):
                pe.wait_ge(self.s("summed"), sums)
                for r in range(self.n // P):
                    last = pe.matmul(self.mean[:, r:r + 1], self.total[:, r * P:(r + 1) * P], ones[:, 0:1],
                                     start=True, stop=True)
                last.then_inc(self.s("meaned"), 1)

            def tensor_spread(self, pe):
                pe.wait_ge(self.s("inverse"), 1)
                for r in range(self.n // P):
                    last = pe.transpose(self.rstd[:, r * P:(r + 1) * P], self.compact[:, r:r + 1].broadcast_to([P, P]),
                                        ident[:, :])
                last.then_inc(self.s("spread"), 1)

        class SquareSum:
            ON_POOL, ON_VECTOR = (2, 4), (3, 5, 6, 7)

            def __init__(self, tag, buffers, mean):
                self.tag, self.buffers, self.mean = tag, buffers, mean

            def s(self, what):
                return sem(self.tag + "_" + what)

            def summed(self, m):
                total, tiles = (0, self.ON_POOL) if m in self.ON_POOL else (1, self.ON_VECTOR)
                return self.s(f"summed{total}"), tiles.index(m) + 1

            def scalar(self, act, m):
                if m >= 4:
                    act.wait_ge(*self.summed(m - 2))
                act.activation(square_totals[m] if m < 2 else self.buffers[m % 2], res[:, m, :], ACT.Square)\
                   .then_inc(self.s("squared"), 1)

            def add(self, eng, m):
                done, count = self.summed(m)
                total = square_totals[0 if m in self.ON_POOL else 1]
                eng.wait_ge(self.s("squared"), m + 1)
                if count > 1:
                    eng.wait_ge(done, count - 1)
                eng.tensor_tensor(total, total, self.buffers[m % 2], ALU.add).then_inc(done, 1)

            def tensor(self, pe):
                for p, tiles in enumerate((self.ON_POOL, self.ON_VECTOR)):
                    pe.wait_ge(*self.summed(tiles[-1]))
                    for r in range(RT):
                        pe.matmul(self.mean[:, r:r + 1], square_totals[p][:, r * P:(r + 1) * P], ones[:, 0:1],
                                  start=(p == 0 and r == 0), stop=(p == 1 and r == RT - 1))

        ADA_FIRST = [(0, m) for m in range(4)]
        ADA_REST = [(0, 4), (0, 5)] + [(1, m) for m in range(6)]

        def ada_product(pe, pieces, first_bank, k, cond, raw):
            for i in range(len(pieces)):
                j = 32 * (i % 4)
                last = pe.matmul(ps[j:j + 32, first_bank + i // 4, :], cond[:, k, :], raw[i],
                                 start=(k == 0), stop=(k == KT - 1))
            return last

        def ada_turn(pe, pieces, rows):
            for b in range(len(pieces) // 4):
                for t in range(4):
                    last = pe.transpose(ps[:, b, t * P:(t + 1) * P], rows[:, b, t * P:(t + 1) * P], ident[:, :])
            return last

        def ada_bias(dve, pieces):
            for i, (l, m) in enumerate(pieces):
                b = ADA_B[1] + l * ADA_T + 4 * m
                j = 32 * (i % 4)
                last = dve.tensor_tensor(ada_col[:, l, 4 * m:4 * m + 4, :],
                                         ps[:, i // 4, :].rearrange("p (t n) -> p t n", n=P)[:, :, j:j + 2],
                                         cols[:, ADA_B[0], b:b + 4].unsqueeze(2).broadcast_to([P, 4, 2]), ALU.add)
            return last

        def ada_gain(dve, n, l, v):
            dve.scalar_tensor_tensor(out=mod_gain[:, n, :], in0=ada_col[:, l, KT:2 * KT, v], scalar=1.0,
                                     in1=cols[:, NORM_G[0], NORM_G[1] + l * KT:NORM_G[1] + (l + 1) * KT],
                                     op0=ALU.add, op1=ALU.mult)

        def adaptive_parameters():
            with ExitStack() as st:
                rows = sb(st, "rows", [P, 3, P])
                lam_in = sb(st, "lam_in", [P, 4, DH])
                lam_pair = sb(st, "lam_pair", [P, 2, DH])
                lam_dot = sb(st, "lam_dot", [P, 2])
                lam_exp = sb(st, "lam_exp", [P, 2])
                cond = sb(st, "cond", [P, KT, 32])
                ada_raw = sb(st, "ada_raw", [P, KT, len(ADA_FIRST) * BANK])
                ada_rows = sb(st, "ada_rows", [P, 1, BANK])
                square = gate
                square_c = sb(st, "square_c", [P, KT, CTX])
                total = sb(st, "square_sum", [P, SEQ])
                total_c = sb(st, "square_sum_c", [P, CTX])
                compact = sb(st, "compact", [P, KEYT])
                stats = Norm("stats", lambda k: x_t[:, k, :], SEQ, None, None, None, None, total[:, :], pair[2], square,
                             mean=ps[:, 7, 0:RT], compact=compact[:, 0:RT], kept=rstd_x)
                stats_c = Norm("stats_c", lambda k: ctx_t[:, k, :], CTX, None, None, None, None, total_c[:, :],
                               ps[:, 2, 0:CTX], mean=ps[:, 3, 0:CT], compact=compact[:, RT:KEYT], kept=rstd_c)
                ctx_t = ctx_xt
                x_t = fq[:, :, :, :].rearrange("p a b n -> p (a b n)").rearrange("p (k n) -> p k n", k=KT)
                nat = residual
                row_sources = [
                    (0, NORM_G[1], a["norm_g"].rearrange("l (k p) -> (l k) p", p=P)),
                    (0, ADA_B[1], a["ada_b"].rearrange("l (k p) -> (l k) p", p=P)),
                    (0, ODD_CONV[1], a["odd_conv_w"].rearrange("a t (k p) -> (a t k) p", p=P)),
                    (0, MIX_G[1], a["norm_mix_g_2"].rearrange("a (k p) -> (a k) p", p=P)),
                    (0, FFN_G[1], a["norm_ffn_g_2"].rearrange("a (k p) -> (a k) p", p=P)),
                    (0, C_VEC[1], a["c"].rearrange("a (k p) -> (a k) p", p=P)),
                    (0, C_CTX[1], a["c_ctx"].rearrange("(k p) -> k p", p=P)),
                    (1, POOL_B[1], a["pool_b_2"].rearrange("a (k p) -> (a k) p", p=P)),
                    (1, POOL_SCALE[1], a["pool_scale_2"].rearrange("a (k p) -> (a k) p", p=P)),
                    (1, FFN_B[1], a["ffn_conv_b_2"].rearrange("a (k p) -> (a k) p", p=P)),
                    (1, FFN_TAP0[1], a["ffn_conv_w_2"][0, 0:1, :].rearrange("a (k p) -> (a k) p", p=P)),
                    (2, FFN_TAP1[1], a["ffn_conv_w_2"][0, 1:3, :].rearrange("a (k p) -> (a k) p", p=P)),
                    (2, SUBLN[1], a["even_subln"]),
                ]
                x_rows = a["x"].rearrange("b (r p) d -> p (b r) d", p=P)
                ctx_rows = a["ctx"].rearrange("b (r p) d -> p (b r) d", p=P)

                with nc.Block(name="ada") as block:
                    @block.sync
                    def _(sp):
                        sp.dma_start(ident[:, :], a["identity"]).then_inc(sem("rows_in"), 16)
                        sp.dma_start(nat[:, 0:4, :], x_rows[:, 0:4, :]).then_inc(sem("x_in_lo"), 16)
                        sp.dma_start(nat[:, 4:8, :], x_rows[:, 4:8, :]).then_inc(sem("x_in_hi"), 16)
                        for t, r, src in row_sources:
                            sp.dma_start(rows[r:r + src.shape[0], t, :], src).then_inc(sem("rows_in"), 16)
                        for n, name in enumerate(("even_lambda_q1", "even_lambda_k1", "even_lambda_q2", "even_lambda_k2")):
                            sp.dma_start(lam_in[:, n, :], a[name].broadcast_to([P, DH])).then_inc(sem("lam_in"), 16)
                        sp.dma_start(nat[:, RT:KEYT, :], ctx_rows).then_inc(sem("ctx_in"), 16)
                        for k in range(KT):
                            sp.dma_start(ada_raw[:, k, :], a["ada_w"][0, k * P:(k + 1) * P, 0:len(ADA_FIRST) * BANK])\
                              .then_inc(sem(f"ada_in{k}"), 16)
                        sp.dma_start(in_raw[:, :, :], w_in[:, :, KV_COL:KV_COL + HALF_GROUP]).then_inc(sem("in_landed"), 16)

                    @block.tensor
                    def _(pe):
                        pe.wait_ge(sem("rows_in"), 16 * (1 + len(row_sources)))
                        for t in range(3):
                            last = pe.transpose(ps[:, 7, t * P:t * P + ROWS[t]], rows[0:ROWS[t], t, :],
                                                ident[0:ROWS[t], 0:ROWS[t]])
                        last.then_inc(sem("rows_turned"), 1)
                        pe.wait_ge(sem("x_in_lo"), 16)
                        pe.wait_ge(sem("x_in_hi"), 16)
                        for k in range(KT):
                            if k >= 2:
                                pe.wait_ge(sem("xt_copied"), k - 1)
                            for r in range(RT):
                                last = pe.transpose(pair[k % 2][:, r * P:(r + 1) * P], nat[:, r, k * P:(k + 1) * P],
                                                    ident[:, :])
                            last.then_inc(sem("xt_turned"), 1)
                        pe.wait_ge(sem("cond_ready"), 1)

                        def ada(first, end):
                            for k in range(first, end):
                                pe.wait_ge(sem(f"ada_in{k}"), 16)
                                last = ada_product(pe, ADA_FIRST, 6, k, cond,
                                                   [ada_raw[:, k, i * BANK:(i + 1) * BANK] for i in range(len(ADA_FIRST))])
                            return last

                        ada(0, 3)
                        pe.wait_ge(sem("ctx_in"), 16)
                        for k in range(0, KT, 4):
                            for i in range(4):
                                for r in range(CT):
                                    last = pe.transpose(pair[2][:, (i * CT + r) * P:(i * CT + r + 1) * P],
                                                        nat[:, RT + r, (k + i) * P:(k + i + 1) * P], ident[:, :])
                            last.then_inc(sem("ct_turned"), 1)
                            pe.wait_ge(sem("ct_copied"), k // 4 + 1)
                        ada(3, 6)
                        pe.wait_ge(sem("cols_copied"), 3)
                        stats.tensor_mean(pe, KT - 1)
                        ada(6, 7)
                        pe.wait_ge(sem("xt_copied"), KT)
                        stats_c.tensor_mean(pe, 1)
                        stats.tensor_spread(pe)
                        ada(7, KT).then_inc(sem("ada_summed"), 1)
                        stats_c.tensor_spread(pe)
                        pe.wait_ge(sem("ada_rows"), 1)
                        ada_turn(pe, ADA_FIRST, ada_rows).then_inc(sem("ada_turned"), 1)

                    @block.scalar
                    def _(act):
                        act.wait_ge(sem("cols_copied"), 3)
                        act.wait_ge(sem("cond_zero"), 1)
                        for v, vec in enumerate((C_VEC, C_CTX)):
                            act.activation(cond_col[:, :, v], cols[:, vec[0], vec[1]:vec[1] + KT], ACT.Silu)\
                               .then_inc(sem("cond_col"), 1)
                        act.wait_ge(sem("cond_col"), 2)
                        act.activation(cond[:, :, 0:2], cond_col[:, :, :], ACT.Copy).then_inc(sem("cond_ready"), 1)
                        act.wait_ge(sem("lam_dots"), 2)
                        act.activation(lam_exp[:, :], lam_dot[:, :], ACT.Exp).then_inc(sem("lam_exped"), 1)
                        for k in range(KT):
                            act.wait_ge(sem("xt_turned"), k + 1)
                            act.activation(x_t[:, k, :], pair[k % 2], ACT.Copy).then_inc(sem("xt_copied"), 1)
                            if k:
                                act.wait_ge(sem("xt_copied"), k)
                                stats.scalar_square(act, k - 1)
                        for k in range(0, KT, 4):
                            act.wait_ge(sem("ct_turned"), k // 4 + 1)
                            act.activation(ctx_t[:, k:k + 4, :].rearrange("p k n -> p (k n)"), pair[2], ACT.Copy)\
                               .then_inc(sem("ct_copied"), 1)
                        act.wait_ge(sem("xt_copied"), KT)
                        stats.scalar_square(act, KT - 1)
                        act.wait_ge(sem("ct_copied"), 2)
                        act.activation(square_c[:, :, :], ctx_t, ACT.Square).then_inc(stats_c.s("squared"), 1)
                        stats.scalar_root(act)
                        stats_c.scalar_root(act)
                        act.wait_ge(sem("in_landed"), 16)
                        split_high(act, in_hi[:, 0], in_raw[:, :, :], sem("in_high"))

                    @block.vector
                    def _(dve):
                        dve.memset(ones[:, :], 1.0)
                        dve.memset(eps[:, :], EPS)
                        dve.memset(cond[:, :, :], 0.0).then_inc(sem("cond_zero"), 1)
                        dve.wait_ge(sem("rows_turned"), 1)
                        for t in range(3):
                            dve.tensor_copy(cols[:, t, 0:ROWS[t]], ps[:, 7, t * P:t * P + ROWS[t]])\
                               .then_inc(sem("cols_copied"), 1)
                        dve.wait_ge(sem("lam_in"), 64)
                        for n in range(2):
                            dve.tensor_tensor(lam_pair[:, n, :], lam_in[:, 2 * n, :], lam_in[:, 2 * n + 1, :], ALU.mult)\
                               .then_inc(sem("lam_pairs"), 1)
                        dve.wait_ge(sem("lam_pairs"), 2)
                        for n in range(2):
                            dve.tensor_reduce(lam_dot[:, n:n + 1], lam_pair[:, n, :], AX_X, ALU.add)\
                               .then_inc(sem("lam_dots"), 1)
                        dve.wait_ge(sem("lam_exped"), 1)
                        dve.tensor_tensor(lam_dot[:, 0:1], lam_exp[:, 1:2], lam_exp[:, 0:1], ALU.subtract)\
                           .then_inc(sem("lam_diff"), 1)
                        dve.wait_ge(sem("lam_diff"), 1)
                        dve.tensor_scalar(neg_lam[:, :], lam_dot[:, 0:1], -LAMBDA_INIT, None, ALU.add)
                        stats.vector_sum(dve)
                        dve.wait_ge(stats_c.s("squared"), 1)
                        dve.tensor_reduce(total_c[:, :], square_c[:, :, :].rearrange("p k n -> p n k"), AX_X, ALU.add)\
                           .then_inc(stats_c.s("summed"), 1)
                        stats.vector_inverse(dve)
                        stats_c.vector_inverse(dve)
                        stats.vector_keep(dve)
                        stats_c.vector_keep(dve)
                        dve.wait_ge(sem("ada_summed"), 1)
                        dve.tensor_copy(ada_rows[:, 0, :], ps[:, 6, :]).then_inc(sem("ada_rows"), 1)
                        dve.wait_ge(sem("ada_turned"), 1)
                        ada_bias(dve, ADA_FIRST).then_inc(sem("ada_cols"), 1)
                        dve.wait_ge(sem("ada_cols"), 1)
                        ada_gain(dve, 0, 0, 0)
                        ada_gain(dve, 1, 0, 1)

        def gain_col(n):
            return lambda k: mod_gain[:, n, k:k + 1]

        def shift_col(l, v):
            return lambda k: ada_col[:, l, k, v:v + 1]

        h_stack = ExitStack()
        ctx_xt = residual[:, 5:7, :].rearrange("p r n -> p (r n)").rearrange("p (k n) -> p k n", k=KT)
        rstd_x, rstd_c = residual[:, 7, :], residual[:, 8, 0:CTX]
        in_raw = sb(h_stack, "in_raw", [P, KT, HALF_GROUP])
        in_hi = sb(h_stack, "in_hi", [P, 2, KT, HALF_GROUP], F32R)
        in_lo = sb(h_stack, "in_lo", [P, 2, KT, HALF_GROUP], F32R)
        w_in = a["even_w_in"].rearrange("e (k p) n -> p (e k) n", p=P)
        adaptive_parameters()
        h_hi = sb(h_stack, "h_hi", [P, KT, SEQ], F32R)
        h_lo = sb(h_stack, "h_lo", [P, KT, SEQ], F32R)
        hc_hi = sb(h_stack, "hc_hi", [P, KT, CTX], F32R)
        hc_lo = sb(h_stack, "hc_lo", [P, KT, CTX], F32R)
        x_t = fq[:, :, :, :].rearrange("p a b n -> p (a b n)").rearrange("p (k n) -> p k n", k=KT)

        kv = residual[:, :, :].rearrange("p r n -> p (r n)").rearrange("p (g t n) -> p g t n", g=2, t=KEYT)
        ROOT = 0.5 ** 0.5
        FOLDED = (7, 3, 1, 4, 0, 5, 2, 6)

        def even_projections():
            with ExitStack() as st:
                raw, w_hi, w_lo = in_raw, in_hi, in_lo
                cos = sb(st, "cos", [P, RT, 2, 16])
                sin = sb(st, "sin", [P, RT, 2, 16])
                gain = sb(st, "qk_gain", [P, DH])
                stat = sb(st, "stat", [P, KEYT * 8])
                turn = sb(st, "turn", [P, BANK])
                u_f = fq[:, 0]
                k_nat, q_nat = kv[:, 0], fq[:, 1]
                norm_x = Norm("norm0", lambda k: x_t[:, k, :], SEQ, gain_col(0), shift_col(0, 0), lambda k: h_hi[:, k, :],
                              lambda k: h_lo[:, k, :], None, rstd_x, scaled=gate, rstd_elsewhere=True)
                norm_c = Norm("norm0c", lambda k: ctx_xt[:, k, :], CTX, gain_col(1), shift_col(0, 1),
                              lambda k: hc_hi[:, k, :], lambda k: hc_lo[:, k, :], None, rstd_c, scaled=gate,
                              rstd_elsewhere=True)
                g_raw = raw[:, :, :].rearrange("p k n -> p (k n)").rearrange("p (s k n) -> p s k n", s=2, k=KT)
                g_hi, g_lo = (w[:, :, :, :].rearrange("p s k n -> p (s k n)").rearrange("p (s k n) -> p s k n", s=4, k=KT)
                              for w in (w_hi, w_lo))
                N_UNITS = 8
                tiles_of = [KEYT if u < 4 else RT for u in range(N_UNITS)]
                first_tile = [sum(tiles_of[:u]) for u in range(N_UNITS + 1)]
                N_TILES = first_tile[N_UNITS]

                def row_tile(u, i):
                    return i if u >= 4 else (i + CT) % KEYT

                with nc.Block(name="even_in") as block:
                    @block.sync
                    def _(sp):
                        def load(u):
                            c = (KV_COL + HALF_GROUP * u) if u < 4 else HALF_GROUP * (u - 4)
                            sp.wait_ge(sem("in_low"), u)
                            sp.dma_start(raw[:, :, :], w_in[:, :, c:c + HALF_GROUP]).then_inc(sem("in_landed"), 16)

                        load(1)
                        for tile, name in ((cos, "rope_cos"), (sin, "rope_sin")):
                            sp.dma_start(tile[:, :, :, :], a[name].rearrange("(r p) c f -> p r c f", p=P))\
                              .then_inc(sem("rope_in"), 16)
                        sp.dma_start(gain[:, :], a["even_k_norm"].broadcast_to([P, DH])).then_inc(sem("rope_in"), 16)
                        for k in range(KT):
                            sp.dma_start(x_scratch[k], x_t[:, k, :]).then_inc(sem("x_spilled"), 16)
                        for u in range(2, N_UNITS):
                            load(u)
                        sp.wait_ge(sem("k_scaled"), 1)
                        sp.dma_start(gain[:, :], a["even_q_norm"].broadcast_to([P, DH])).then_inc(sem("q_gain_in"), 16)
                        sp.wait_ge(sem("in_low"), N_UNITS)
                        for m in range(KT + 2):
                            if 2 <= m < KT:
                                sp.wait_ge(sem("gw_low"), m - 1)
                            if m < KT:
                                c = GATE_COL + m * P
                                sp.dma_start(g_raw[:, m % 2], w_in[:, :, c:c + P]).then_inc(sem(f"gw_landed{m % 2}"), 16)
                            if 2 <= m < SPILLED + 2:
                                sp.wait_ge(sem("gate_ready"), m - 1)
                                sp.dma_start(gate_scratch[m - 2], gate[:, m % 2, :]).then_inc(sem(f"gate_spilled{m % 2}"), 16)
                        for s in range(2):
                            sp.wait_ge(sem(f"gate_spilled{s}"), 16 * SPILLED // 2)

                    @block.scalar
                    def _(act):
                        def high(u):
                            act.wait_ge(sem("in_landed"), 16 * (u + 1))
                            if u >= 2:
                                act.wait_ge(sem("in_done"), first_tile[u - 1])
                            split_high(act, w_hi[:, u % 2], raw[:, :, :], sem("in_high"))

                        def g_high(m):
                            act.wait_ge(sem(f"gw_landed{m % 2}"), 16 * (m // 2 + 1))
                            if m >= 2:
                                act.wait_ge(sem("gw_done"), m - 1)
                            else:
                                act.wait_ge(sem("in_done"), first_tile[7])
                            split_high(act, g_hi[:, m % 2], g_raw[:, m % 2], sem("gw_high"))

                        def root(n, t):
                            act.wait_ge(sem("qk_summed"), n + 1)
                            act.activation(stat[:, 0:t * 8], stat[:, 0:t * 8], ACT.Sqrt, bias=eps[:, 0:1], scale=1.0 / DH)\
                               .then_inc(sem("qk_rooted"), 1)

                        for k in range(KT):
                            norm_x.scalar_high(act, k)
                        high(1)
                        for k in range(KT):
                            norm_c.scalar_high(act, k)
                        for u in range(N_UNITS):
                            if 0 < u < N_UNITS - 1:
                                high(u + 1)
                            if u == 4:
                                root(0, KEYT)
                                act.wait_ge(sem("x_spilled"), 16 * KT)
                            if u == N_UNITS - 1:
                                g_high(0)
                                g_high(1)
                            half = HALF_GROUP * (u % 2)
                            for i in range(tiles_of[u]):
                                n = first_tile[u] + i
                                act.wait_ge(sem("in_done"), n + 1)
                                if u < 4:
                                    dst = kv[:, u // 2, row_tile(u, i), half:half + HALF_GROUP]
                                else:
                                    dst = fq[:, (u - 4) // 2, i, half:half + HALF_GROUP]
                                act.activation(dst, ps[:, n % 8, 0:HALF_GROUP], ACT.Copy).then_inc(sem("in_copied"), 1)
                        root(1, RT)
                        for m in range(KT):
                            act.wait_ge(sem("gw_done"), m + 1)
                            if m >= 2:
                                act.wait_ge(sem(f"gate_spilled{m % 2}"), 16 * (m // 2))
                            act.activation(gate[:, m % 2, :], pair[m % 4], ACT.Silu).then_inc(sem("gate_ready"), 1)
                            if m + 2 < KT:
                                g_high(m + 2)

                    @block.gpsimd
                    def _(pool):
                        for u in range(N_UNITS):
                            pool.wait_ge(sem("in_high"), u + 1)
                            if u >= 2:
                                pool.wait_ge(sem("in_done"), first_tile[u - 1])
                            split_low(pool, w_lo[:, u % 2], raw[:, :, :], w_hi[:, u % 2], sem("in_low"))
                        for m in range(KT):
                            pool.wait_ge(sem("gw_high"), m + 1)
                            split_low(pool, g_lo[:, m % 2], g_raw[:, m % 2], g_hi[:, m % 2], sem("gw_low"))

                    @block.tensor
                    def _(pe):
                        def part_products(u, n, k, hi, lo, r):
                            for x, w in ((hi, w_hi), (hi, w_lo), (lo, w_hi)):
                                last = pe.matmul(ps[:, n % 8, 0:HALF_GROUP], x[:, k, r * P:(r + 1) * P], w[:, u % 2, k, :],
                                                 start=(k == 0 and x is hi and w is w_hi), stop=(k == KT - 1 and x is lo))
                            return last

                        pe.wait_ge(sem("in_low"), 1)
                        for k in range(KT):
                            pe.wait_ge(norm_x.s("low"), k + 1)
                            for r in range(RT):
                                last = part_products(0, r, k, h_hi, h_lo, r)
                                if k == KT - 1:
                                    last.then_inc(sem("in_done"), 1)
                        pe.wait_ge(norm_c.s("low"), KT)
                        for u in range(N_UNITS):
                            pe.wait_ge(sem("in_low"), u + 1)
                            for i in range(RT if u == 0 else 0, tiles_of[u]):
                                n = first_tile[u] + i
                                if n >= 8:
                                    pe.wait_ge(sem("in_copied"), n - 7)
                                ctx_tile = i >= RT
                                hi, lo = (hc_hi, hc_lo) if ctx_tile else (h_hi, h_lo)
                                for k in range(KT):
                                    last = part_products(u, n, k, hi, lo, i - RT if ctx_tile else i)
                                last.then_inc(sem("in_done"), 1)
                        for m in range(KT):
                            pe.wait_ge(sem("gw_low"), m + 1)
                            if m < 4:
                                pe.wait_ge(sem("in_copied"), N_TILES - 8 + 2 * m + 2)
                            else:
                                pe.wait_ge(sem("gate_ready"), m - 3)
                            matmul3(pe, pair[m % 4], lambda k: g_hi[:, m % 2, k, :], lambda k: g_lo[:, m % 2, k, :],
                                    lambda k, c, e: h_hi[:, k, c:e], lambda k, c, e: h_lo[:, k, c:e], KT, SEQ)\
                                .then_inc(sem("gw_done"), 1)

                    @block.vector
                    def _(dve):
                        norm_x.vector_scale(dve)
                        dve.wait_ge(norm_x.s("low"), KT)
                        norm_c.vector_scale(dve)
                        rs = sem("rot_step")
                        n_rs = [0]

                        def step(instruction):
                            instruction.then_inc(rs, 1)
                            n_rs[0] += 1

                        def wait_steps():
                            dve.wait_ge(rs, n_rs[0])

                        def norm_and_rotate(n, nat, t):
                            heads = nat.rearrange("p t n -> p (t n)").rearrange("p (h d) -> p h d", d=DH)
                            for i in range(t):
                                step(dve.tensor_tensor(turn[:, :], nat[:, i, :], nat[:, i, :], ALU.mult))
                                wait_steps()
                                last = dve.tensor_reduce(stat[:, i * 8:(i + 1) * 8],
                                                         turn[:, :].rearrange("p (h d) -> p h d", d=DH), AX_X, ALU.add)
                                if i + 1 < t:
                                    step(last)
                                    wait_steps()
                            last.then_inc(sem("qk_summed"), 1)
                            dve.wait_ge(sem("qk_rooted"), n + 1)
                            step(dve.reciprocal(stat[:, 0:t * 8], stat[:, 0:t * 8]))
                            wait_steps()
                            step(dve.tensor_tensor(heads, heads, stat[:, 0:t * 8].unsqueeze(2).broadcast_to([P, t * 8, DH]),
                                                   ALU.mult))
                            wait_steps()
                            dve.wait_ge(*(sem("rope_in"), 48) if n == 0 else (sem("q_gain_in"), 16))
                            scaled = sem("q_scaled" if n else "k_scaled")
                            dve.tensor_tensor(heads, heads, gain[:, :].unsqueeze(1).broadcast_to([P, t * 8, DH]), ALU.mult)\
                               .then_inc(scaled, 1)
                            dve.wait_ge(scaled, 1)
                            for r in range(RT):
                                x_row = nat[:, t - RT + r, :].rearrange("p (h c j f) -> p h c j f", c=2, j=2, f=16)
                                x1, x2 = x_row[:, :, :, 0, :], x_row[:, :, :, 1, :]
                                cs, sn = (tab[:, r, :, :].unsqueeze(1).broadcast_to([P, 8, 2, 16]) for tab in (cos, sin))
                                s1, s2 = (turn[:, i * 2 * P:(i + 1) * 2 * P].rearrange("p (h c f) -> p h c f", h=8, c=2)
                                          for i in range(2))
                                step(dve.tensor_tensor(s1, x1, sn, ALU.mult))
                                step(dve.tensor_tensor(s2, x2, sn, ALU.mult))
                                wait_steps()
                                step(dve.tensor_tensor(x1, x1, cs, ALU.mult))
                                step(dve.tensor_tensor(x2, x2, cs, ALU.mult))
                                wait_steps()
                                step(dve.tensor_tensor(x1, x1, s2, ALU.subtract))
                                step(dve.tensor_tensor(x2, x2, s1, ALU.add))
                                wait_steps()

                        dve.wait_ge(sem("in_copied"), first_tile[2])
                        norm_and_rotate(0, k_nat, KEYT)

                        dve.wait_ge(sem("in_copied"), first_tile[6])
                        spare = turn[:, 0:BANK]
                        v = [u_f[:, i] for i in range(RT)]
                        even = [spare, v[0], v[1], v[2]]
                        for i in range(4):
                            step(dve.tensor_tensor(even[i], v[i], v[i + 4], ALU.add))
                            wait_steps()
                            step(dve.tensor_tensor(v[i + 4], v[i], v[i + 4], ALU.subtract))
                            wait_steps()
                        for sum_to, diff_to, p, q, plus, minus in ((v[3], v[2], even[3], even[1], ALU.add, ALU.subtract),
                                                                   (v[0], v[1], even[0], even[2], ALU.add, ALU.subtract),
                                                                   (spare, v[5], v[5], v[7], ALU.add, ALU.subtract)):
                            step(dve.tensor_tensor(sum_to, p, q, plus))
                            wait_steps()
                            step(dve.tensor_tensor(diff_to, p, q, minus))
                            wait_steps()
                        step(dve.tensor_tensor(v[7], v[0], v[3], ALU.add))
                        wait_steps()
                        step(dve.tensor_tensor(v[0], v[0], v[3], ALU.subtract))
                        wait_steps()
                        for s, dst, src, base, op in ((ROOT, v[3], v[5], v[4], ALU.add), (-ROOT, v[4], v[5], v[4], ALU.add),
                                                      (-ROOT, v[5], spare, v[6], ALU.subtract),
                                                      (-ROOT, v[6], spare, v[6], ALU.add)):
                            step(dve.scalar_tensor_tensor(out=dst, in0=src, scalar=s, in1=base, op0=ALU.mult, op1=op))
                            wait_steps()

                        dve.wait_ge(sem("in_copied"), N_TILES)
                        norm_and_rotate(1, q_nat, RT)

        even_projections()
        end_stage()
        h_stack.close()

        y_f = sb(fq_stack, "y_f", [P, F_GROUPS, SEQ])
        turned_stack = ExitStack()
        k_turned = sb(turned_stack, "k_turned", [P, 2, 2, KEYS], F32R)
        q_turned = sb(turned_stack, "q_turned", [P, 2, SEQ], F32R)
        k_nat, v_nat, q_nat = kv[:, 0], kv[:, 1], fq[:, 1]

        def head_columns(src, h, m):
            part = src[:, :, bass.ds(h * DV + m * DH, DH)]
            return part.unsqueeze(2).broadcast_to([P, src.shape[1], 2, DH])

        def turn_rows(pe, psum, twice, tiles):
            for i in range(tiles):
                last = pe.transpose(psum[:, i * P:(i + 1) * P], twice[:, i, :, :].rearrange("p a d -> p (a d)"), ident[:, :])
            return last

        def high_k(act, h, m, src, k="k"):
            act.wait_ge(sem(k + "_turned"), h * 2 + m + 1)
            act.activation(k_turned[:, m, 0, :], src, ACT.Copy).then_inc(sem(k + "_high"), 1)

        def high_q(act, h, m, src, q="q"):
            act.wait_ge(sem(q + "_turned"), h * 2 + m + 1)
            act.activation(q_turned[:, m, :], src, ACT.Copy, scale=ATTN_SCALE).then_inc(sem(q + "_high"), 1)

        def low_k(dve, h, m, src, k="k"):
            dve.wait_ge(sem(k + "_high"), h * 2 + m + 1)
            dve.tensor_tensor(k_turned[:, m, 1, :], src, k_turned[:, m, 0, :].bitcast(F32), ALU.subtract)\
               .then_inc(sem(k + "_low"), 1)

        def low_q(dve, h, m, src, q="q"):
            dve.wait_ge(sem(q + "_high"), h * 2 + m + 1)
            upper = q_turned[DH:P, m, :]
            dve.scalar_tensor_tensor(out=upper, in0=src[DH:P, :], scalar=ATTN_SCALE, in1=upper.bitcast(F32),
                                     op0=ALU.mult, op1=ALU.subtract).then_inc(sem(q + "_low"), 1)

        def fourier():
            with ExitStack() as st:
                PAIRS = RADIX // 2
                tables_hi = sb(st, "tables_hi", [P, RADIX, 3, P], F32R)
                channel_hi = sb(st, "channel_hi", [P, 2, P], F32R)
                u_hi, u_lo = (sb(st, "u_" + part, [P, RT, P], F32R) for part in ("hi", "lo"))
                cond = sb(st, "cond_rest", [P, KT, 32])
                with ExitStack() as early:
                    tables = sb(early, "tables", [P, RADIX, 3, P])
                    channel_dft = sb(early, "channel_dft", [P, 2, P])
                    k_first = sb(early, "k_first", [P, 2, KEYT, 2, DH])
                    q_first = sb(early, "q_first", [P, 2, RT, 2, DH])
                tables_lo = sb(st, "tables_lo", [P, RADIX, 3, P], F32R)
                channel_lo = sb(st, "channel_lo", [P, 2, P], F32R)
                ft_hi, ft_lo = (sb(st, "ft_" + part, [P, RADIX, 2, P], F32R) for part in ("hi", "lo"))
                UNITS, N_RAW = 4 * KT, 7
                ada_raw = sb(st, "ada_raw_rest", [P, N_RAW, 2 * BANK])
                ada_rows = ada_raw[:, 0, :].rearrange("p (b n) -> p b n", b=2)

                def slot(u):
                    return (u + 1) % N_RAW

                def group_input(g):
                    return fq[:, 0, :, g * P:(g + 1) * P]

                def table(part, k1, imaginary):
                    third = int(imaginary) if k1 > RADIX // 2 else 1 - int(imaginary)
                    return part[:, k1, third:third + 2, :].rearrange("p c n -> p (c n)")

                def ft_pair(part, q):
                    return part[:, 2 * q:2 * q + 2, :, :].rearrange("p k c n -> p (k c n)")

                k_banks = [ps[:, 3 * m:3 * m + 3, :].rearrange("p b n -> p (b n)")[:, 0:KEYS] for m in range(2)]
                q_banks = [pair[3], k_banks[1][:, 0:SEQ]]

                with nc.Block(name="fourier") as block:
                    @block.sync
                    def _(sp):
                        sp.dma_start(tables[:, :, :, :], a["seq_dft"]).then_inc(sem("tables_in"), 16)
                        sp.dma_start(channel_dft[:, :, :], a["channel_dft"]).then_inc(sem("channel_in"), 16)
                        for u in range(UNITS):
                            if slot(u) == 0 and u < N_RAW:
                                sp.wait_ge(sem("first_q_turned"), 2)
                            if u >= N_RAW:
                                sp.wait_ge(sem("rest_ada_used"), (u - N_RAW) // 2 + 1)
                            l, m = ADA_REST[2 * (u % 4)]
                            rows = slice(u // 4 * P, (u // 4 + 1) * P)
                            sp.dma_start(ada_raw[:, slot(u), :], a["ada_w"][l, rows, m * BANK:(m + 2) * BANK])\
                              .then_inc(sem(f"rest_ada_in{slot(u)}"), 16)

                    @block.tensor
                    def _(pe):
                        def ada(n):
                            k, b = n // 2, n % 2
                            for u in (2 * n, 2 * n + 1):
                                pe.wait_ge(sem(f"rest_ada_in{slot(u)}"), 16 * (u // N_RAW + 1))
                            if n == 0:
                                pe.wait_ge(sem("first_q_low"), 2)
                                pe.wait_ge(sem("rest_cond_ready"), 1)
                            ada_product(pe, ADA_REST[4 * b:4 * b + 4], 2 + b, k, cond,
                                        [ada_raw[:, slot(2 * n + i // 2), i % 2 * BANK:(i % 2 + 1) * BANK] for i in range(4)])\
                                .then_inc(sem("rest_ada_used"), 1)

                        for m in range(2):
                            pe.wait_ge(sem("first_k_twice"), m + 1)
                            turn_rows(pe, k_banks[m], k_first[:, m], KEYT).then_inc(sem("first_k_turned"), 1)
                        for m in range(2):
                            pe.wait_ge(sem("first_q_twice"), m + 1)
                            if m == 1:
                                pe.wait_ge(sem("first_k_low"), 2)
                            turn_rows(pe, q_banks[m], q_first[:, m], RT).then_inc(sem("first_q_turned"), 1)
                        def parts(psum, terms):
                            passes = [(w[i], x[j]) for w, x in terms for i, j in ((0, 0), (0, 1), (1, 0))]
                            for i, (w, x) in enumerate(passes):
                                last = pe.matmul(psum, w, x, start=(i == 0), stop=(i == len(passes) - 1))
                            return last

                        units_after = (0, 1, 1, 2)
                        units = iter(range(UNITS // 2))
                        for g in range(F_GROUPS):
                            pe.wait_ge(sem("u_low"), g + 1)
                            for k1 in range(RADIX):
                                n = g * PAIRS + k1 // 2
                                if g == 0:
                                    pe.wait_ge(sem("tables_low"), k1 // 2 + 1)
                                if n >= 2 and k1 % 2 == 0:
                                    pe.wait_ge(sem("ft_low"), n - 1)
                                m = min(k1, RADIX - k1)
                                terms = [((u_hi[:, row, :], u_lo[:, row, :]),
                                          (table(tables_hi, k1, imaginary), table(tables_lo, k1, imaginary)))
                                         for imaginary, row in enumerate([FOLDED[m]] + ([FOLDED[m + 4]] if m % 4 else []))]
                                last = parts(ps[:, n % 2, (k1 % 2) * 2 * P:(k1 % 2 + 1) * 2 * P], terms)
                                if k1 % 2:
                                    last.then_inc(sem("ft_done"), 1)
                                    for _ in range(units_after[k1 // 2]):
                                        ada(next(units))
                            pe.wait_ge(sem("ft_low"), (g + 1) * PAIRS)
                            if g == 0:
                                pe.wait_ge(sem("channel_low"), 1)
                            if g >= 2:
                                pe.wait_ge(sem("y_f_copied"), g - 1)
                            for half in range(2):
                                k1s = slice(half * PAIRS, (half + 1) * PAIRS)
                                last = parts(pair[2 + g % 2][:, half * BANK:(half + 1) * BANK],
                                             [((channel_hi[:, part, :], channel_lo[:, part, :]),
                                               (ft_hi[:, k1s, part, :], ft_lo[:, k1s, part, :])) for part in range(2)])
                            last.then_inc(sem("y_f_done"), 1)
                        pe.wait_ge(sem("rest_ada_rows"), 1)
                        ada_turn(pe, ADA_REST, ada_rows).then_inc(sem("rest_ada_turned"), 1)

                    @block.scalar
                    def _(act):
                        for m in range(2):
                            act.activation(q_first[:, m], head_columns(q_nat, 0, m), ACT.Copy).then_inc(sem("first_q_twice"), 1)
                        split_high(act, u_hi[:, :, :], group_input(0), sem("u_high"))
                        for m in range(2):
                            high_k(act, 0, m, k_banks[m], "first_k")
                        high_q(act, 0, 0, q_banks[0], "first_q")
                        act.wait_ge(sem("tables_in"), 16)
                        for q in range(PAIRS):
                            split_high(act, tables_hi[:, 2 * q:2 * q + 2], tables[:, 2 * q:2 * q + 2], sem("tables_high"))
                            if q == 0:
                                high_q(act, 0, 1, q_banks[1], "first_q")
                        act.wait_ge(sem("channel_in"), 16)
                        split_high(act, channel_hi[:, :, :], channel_dft[:, :, :], sem("channel_high"))
                        for g in range(F_GROUPS):
                            for q in range(PAIRS):
                                n = g * PAIRS + q
                                act.wait_ge(sem("ft_done"), n + 1)
                                if g and q == 0:
                                    act.wait_ge(sem("y_f_done"), g)
                                split_high(act, ft_pair(ft_hi, q), ps[:, n % 2, :], sem("ft_high"))
                            if g < F_GROUPS - 1:
                                split_high(act, u_hi[:, :, :], group_input(g + 1), sem("u_high"))
                            act.wait_ge(sem("y_f_done"), g + 1)
                            act.activation(y_f[:, g, :].rearrange("p (k2 k1) -> p k1 k2", k1=RADIX),
                                           pair[2 + g % 2].rearrange("p (k1 k2) -> p k1 k2", k1=RADIX), ACT.Copy)\
                               .then_inc(sem("y_f_copied"), 1)

                    @block.vector
                    def _(dve):
                        for m in range(2):
                            dve.tensor_copy(k_first[:, m], head_columns(k_nat, 0, m)).then_inc(sem("first_k_twice"), 1)
                        dve.memset(cond[:, :, :], 0.0).then_inc(sem("rest_cond_zero"), 1)
                        dve.wait_ge(sem("rest_cond_zero"), 1)
                        dve.tensor_copy(cond[:, :, 0:2], cond_col[:, :, :]).then_inc(sem("rest_cond_ready"), 1)

                        def low_u(g):
                            dve.wait_ge(sem("u_high"), g + 1)
                            split_low(dve, u_lo[:, :, :], group_input(g), u_hi[:, :, :], sem("u_low"))

                        def low_table(q):
                            dve.wait_ge(sem("tables_high"), q + 1)
                            k1s = slice(2 * q, 2 * q + 2)
                            split_low(dve, tables_lo[:, k1s], tables[:, k1s], tables_hi[:, k1s], sem("tables_low"))

                        low_u(0)
                        for m in range(2):
                            low_k(dve, 0, m, k_banks[m], "first_k")
                        low_q(dve, 0, 0, q_banks[0], "first_q")
                        low_table(0)
                        low_q(dve, 0, 1, q_banks[1], "first_q")
                        for q in range(1, PAIRS):
                            low_table(q)
                        dve.wait_ge(sem("channel_high"), 1)
                        split_low(dve, channel_lo[:, :, :], channel_dft[:, :, :], channel_hi[:, :, :], sem("channel_low"))
                        for g in range(F_GROUPS):
                            for q in range(PAIRS):
                                n = g * PAIRS + q
                                dve.wait_ge(sem("ft_high"), n + 1)
                                split_low(dve, ft_pair(ft_lo, q), ps[:, n % 2, :], ft_pair(ft_hi, q), sem("ft_low"))
                            if g < F_GROUPS - 1:
                                low_u(g + 1)
                        dve.wait_ge(sem("rest_ada_used"), UNITS // 2)
                        dve.tensor_copy(ada_rows[:, :, :], ps[:, 2:4, :]).then_inc(sem("rest_ada_rows"), 1)
                        dve.wait_ge(sem("rest_ada_turned"), 1)
                        ada_bias(dve, ADA_REST).then_inc(sem("rest_ada_cols"), 1)
                        dve.wait_ge(sem("rest_ada_cols"), 1)
                        ada_gain(dve, 2, 1, 0)

        fourier()
        end_stage()

        def attention():
            with ExitStack() as st:
                k_head = sb(st, "k_head", [P, 2, KEYT, 2, DH])
                q_head = sb(st, "q_head", [P, 2, RT, 2, DH])
                prob = sb(st, "prob", [P, 2, 2, KEYS])
                mixed = sb(st, "mixed", [P, 2, KEYS])
                mixed_t = sb(st, "mixed_t", [P, 2, KEYS])
                o_all = fq[:, 0].rearrange("p r n -> p (r n)").rearrange("p (h r n) -> p h r n", h=HEADS, r=RT)
                o_square = sb(st, "o_square", [P, DV])
                o_stat = sb(st, "o_stat", [P, HEADS, RT])
                neg_peak = sb(st, "neg_peak", [P, RT, 2])
                total = sb(st, "total", [P, RT, 2])
                inverse = sb(st, "inverse", [P, RT, 2])
                weight = sb(st, "weight", [P, RT])
                subln_gain = sb(st, "subln_gain", [P, 1])
                ao_t = fq[:, 1].rearrange("p r n -> p (r n)").rearrange("p (h n) -> p h n", h=HEADS)
                score = [ps[:, 3 * m:3 * m + 3, :].rearrange("p b n -> p (b n)")[:, 0:KEYS] for m in range(2)]
                MIX_BANK, OUT_BANK = 6, 7
                rounds = [(t, min(t + 4, KEYT)) for t in range(0, KEYT, 4)]
                LAST = len(rounds) - 1
                CREDIT = 2
                credited = ["mixed", f"mix_turned{LAST}", f"mix_copied{LAST}", "o_done", "o_scaled"]
                credited += [x + state for x in "kq" for state in ("_twice", "_turned", "_high", "_low")]

                L1, L2 = RT - 1, RT - 2

                with nc.Block(name="attention") as block:
                    @block.tensor
                    def _(pe):
                        def turn_k(h, m):
                            pe.wait_ge(sem("exped"), (h * RT - 1) * 2 + m + 1)
                            pe.wait_ge(sem("k_twice"), h * 2 + m + 1)
                            turn_rows(pe, score[m], k_head[:, m], KEYT).then_inc(sem("k_turned"), 1)

                        def turn_q(h, m):
                            pe.wait_ge(sem("k_low"), h * 2 + m + 1)
                            pe.wait_ge(sem("q_twice"), h * 2 + m + 1)
                            turn_rows(pe, score[m], q_head[:, m], RT).then_inc(sem("q_turned"), 1)

                        def scores(h, t, m):
                            n = h * RT + t
                            if t == 0:
                                pe.wait_ge(sem("q_low"), h * 2 + m + 1)
                            else:
                                pe.wait_ge(sem("exped"), (n - 1) * 2 + m + 1)
                            for b in range(0, KEYS, BANK):
                                e = min(b + BANK, KEYS)
                                for part in range(2):
                                    last = pe.matmul(score[m][:, b:e], q_turned[:, m, t * P:(t + 1) * P],
                                                     k_turned[:, m, part, b:e], start=(part == 0), stop=(part == 1))
                            last.then_inc(sem("scored"), 1)

                        def turn(h, t, i):
                            n = h * RT + t
                            b, e = rounds[i]
                            if i == 0:
                                pe.wait_ge(sem("mixed"), n + 1 + CREDIT)
                                pe.wait_ge(sem(f"mix_copied{LAST}"), n + CREDIT)
                            else:
                                pe.wait_ge(sem(f"mix_copied{i - 1}"), n + 1)
                            for j in range(b, e):
                                last = pe.transpose(ps[:, MIX_BANK, (j - b) * P:(j - b + 1) * P],
                                                    mixed[:, t % 2, j * P:(j + 1) * P], ident[:, :])
                            last.then_inc(sem(f"mix_turned{i}"), 1)

                        def values(h, t, i):
                            n = h * RT + t
                            pe.wait_ge(sem(f"mix_copied{i}"), n + 1 + (CREDIT if i == LAST else 0))
                            if i == 0:
                                pe.wait_ge(sem("o_scaled"), n + CREDIT)
                            for j in range(*rounds[i]):
                                last = pe.matmul(ps[:, OUT_BANK, (t % 2) * P:(t % 2 + 1) * P],
                                                 mixed_t[:, t % 2, j * P:(j + 1) * P], v_nat[:, j, bass.ds(h * DV, DV)],
                                                 start=(j == 0), stop=(j == KEYT - 1))
                            if i == LAST:
                                last.then_inc(sem("o_done"), 1)

                        def step(h, t, h2, t2, h1, t1):
                            scores(h, t, 0)
                            turn(h2, t2, 1)
                            scores(h, t, 1)
                            turn(h2, t2, 2)
                            for i in range(3):
                                values(h2, t2, i)
                            turn(h1, t1, 0)

                        def tiles(h):
                            for t in range(2, RT):
                                step(h, t, h, t - 2, h, t - 1)

                        for t in range(2):
                            for m in range(2):
                                scores(0, t, m)
                        turn(0, 0, 0)
                        with pe.Fori(0, HEADS - 1) as h:
                            tiles(h)
                            turn_k(h + 1, 0)
                            turn(h, L2, 1)
                            turn_k(h + 1, 1)
                            turn_q(h + 1, 0)
                            turn(h, L2, 2)
                            turn_q(h + 1, 1)
                            for m in range(2):
                                scores(h + 1, 0, m)
                            for i in range(3):
                                values(h, L2, i)
                            turn(h, L1, 0)
                            step(h + 1, 1, h, L1, h + 1, 0)
                        tiles(HEADS - 1)
                        for i in range(1, 3):
                            turn(HEADS - 1, L2, i)
                        for i in range(3):
                            values(HEADS - 1, L2, i)
                        for i in range(3):
                            turn(HEADS - 1, L1, i)
                        for i in range(3):
                            values(HEADS - 1, L1, i)
                        for c in range(HEADS * RT // 4):
                            pe.wait_ge(sem("o_normed"), c // 2 + 1)
                            for i in range(4):
                                last = pe.transpose(ps[:, c, i * P:(i + 1) * P], o_all[:, c // 2, 4 * (c % 2) + i, :],
                                                    ident[:, :])
                            last.then_inc(sem("o_turned"), 1)

                    @block.scalar
                    def _(act):
                        def exps(h, t, m):
                            n = h * RT + t
                            act.wait_ge(sem("peaked"), n * 2 + m + 1)
                            if m == 0:
                                act.wait_ge(sem("mixed"), n - 1 + CREDIT)
                            act.activation(prob[:, t % 2, m, :], score[m], ACT.Exp, bias=neg_peak[:, t, m:m + 1],
                                           accum_out=total[:, t, m:m + 1]).then_inc(sem("exped"), 1)

                        def turn_out(h, t, i):
                            n = h * RT + t
                            b, e = rounds[i]
                            act.wait_ge(sem(f"mix_turned{i}"), n + 1 + (CREDIT if i == LAST else 0))
                            act.activation(mixed_t[:, t % 2, b * P:e * P], ps[:, MIX_BANK, 0:(e - b) * P], ACT.Copy)\
                               .then_inc(sem(f"mix_copied{i}"), 1)

                        def finish(h, t):
                            n = h * RT + t
                            act.wait_ge(sem("o_done"), n + 1 + CREDIT)
                            src = ps[:, OUT_BANK, (t % 2) * P:(t % 2 + 1) * P]
                            act.activation(o_all[:, h, t, :], src, ACT.Copy, scale=inverse[:, t, 0:1])
                            act.wait_ge(sem("o_scaled"), n + CREDIT)
                            act.activation(o_square[:, :], src, ACT.Square, scale=inverse[:, t, 0:1],
                                           accum_out=o_stat[:, h, t:t + 1]).then_inc(sem("o_scaled"), 1)

                        def last_rounds(h, t):
                            for i in range(1, 3):
                                turn_out(h, t, i)

                        def tiles(h):
                            for t in range(2, RT):
                                last_rounds(h, t - 2)
                                for m in range(2):
                                    exps(h, t, m)
                                if t < L1:
                                    finish(h, t - 2)

                        for t in range(2):
                            for m in range(2):
                                exps(0, t, m)
                        with act.Fori(0, HEADS - 1) as h:
                            tiles(h)
                            for m in range(2):
                                high_k(act, h + 1, m, score[m])
                            finish(h, L2 - 1)
                            turn_out(h, L2, 1)
                            high_q(act, h + 1, 0, score[0][:, 0:SEQ])
                            turn_out(h, L2, 2)
                            high_q(act, h + 1, 1, score[1][:, 0:SEQ])
                            for m in range(2):
                                exps(h + 1, 0, m)
                            finish(h, L2)
                            last_rounds(h, L1)
                            for m in range(2):
                                exps(h + 1, 1, m)
                            finish(h, L1)
                        tiles(HEADS - 1)
                        finish(HEADS - 1, L2 - 1)
                        last_rounds(HEADS - 1, L2)
                        finish(HEADS - 1, L2)
                        last_rounds(HEADS - 1, L1)
                        finish(HEADS - 1, L1)
                        act.wait_ge(sem("o_scaled"), HEADS * RT + CREDIT)
                        act.activation(o_stat[:, :, :], o_stat[:, :, :], ACT.Sqrt, bias=eps[:, 0:1], scale=1.0 / DV)\
                           .then_inc(sem("o_rooted"), 1)
                        for c in range(HEADS * RT // 4):
                            act.wait_ge(sem("o_turned"), c + 1)
                            act.activation(ao_t[:, c // 2, (c % 2) * BANK:(c % 2 + 1) * BANK], ps[:, c, :], ACT.Copy,
                                           scale=subln_gain[:, 0:1])

                    @block.gpsimd
                    def _(pool):
                        with pool.Fori(1, HEADS) as h:
                            for name, dst, src in (("k", k_head, k_nat), ("q", q_head, q_nat)):
                                pool.wait_ge(sem(name + "_turned"), h * 2)
                                for m in range(2):
                                    pool.tensor_copy(dst[:, m, :, :, :], head_columns(src, h, m))\
                                        .then_inc(sem(name + "_twice"), 1)

                    @block.vector
                    def _(dve):
                        def peaks(h, t, m):
                            n = h * RT + t
                            dve.wait_ge(sem("scored"), n * 2 + m + 1)
                            dve.tensor_reduce(neg_peak[:, t, m:m + 1], score[m], AX_X, ALU.max, negate=True)\
                               .then_inc(sem("peaked"), 1)

                        def combine(h, t):
                            n = h * RT + t
                            dve.wait_ge(sem("exped"), n * 2 + 2)
                            dve.reciprocal(inverse[:, t, :], total[:, t, :]).then_inc(sem("inverted"), 1)
                            dve.wait_ge(sem("inverted"), n + 1)
                            dve.scalar_tensor_tensor(out=weight[:, t:t + 1], in0=total[:, t, 0:1], scalar=neg_lam[:, 0:1],
                                                     in1=inverse[:, t, 1:2], op0=ALU.mult, op1=ALU.mult)\
                               .then_inc(sem("weighed"), 1)
                            dve.wait_ge(sem("weighed"), n + 1)
                            dve.wait_ge(sem(f"mix_turned{LAST}"), n - 1 + CREDIT)
                            dve.scalar_tensor_tensor(out=mixed[:, t % 2, :], in0=prob[:, t % 2, 1, :],
                                                     scalar=weight[:, t:t + 1], in1=prob[:, t % 2, 0, :],
                                                     op0=ALU.mult, op1=ALU.add).then_inc(sem("mixed"), 1)

                        def turn_out(h, t):
                            n = h * RT + t
                            b, e = rounds[0]
                            dve.wait_ge(sem("mix_turned0"), n + 1)
                            dve.wait_ge(sem("o_done"), n - 1 + CREDIT)
                            dve.tensor_copy(mixed_t[:, t % 2, b * P:e * P], ps[:, MIX_BANK, 0:(e - b) * P])\
                               .then_inc(sem("mix_copied0"), 1)

                        def step(h, t, h1, t1):
                            peaks(h, t, 0)
                            combine(h1, t1)
                            peaks(h, t, 1)
                            turn_out(h1, t1)

                        def tiles(h):
                            for t in range(2, RT):
                                step(h, t, h, t - 1)

                        for name in credited:
                            dve.sem_inc(sem(name), CREDIT)
                        dve.tensor_scalar(subln_gain[:, :], col(SUBLN, 0), 1.0 - LAMBDA_INIT, None, ALU.mult)
                        for m in range(2):
                            peaks(0, 0, m)
                        step(0, 1, 0, 0)
                        with dve.Fori(0, HEADS - 1) as h:
                            tiles(h)
                            for m in range(2):
                                low_k(dve, h + 1, m, score[m])
                            for m in range(2):
                                low_q(dve, h + 1, m, score[m][:, 0:SEQ])
                            step(h + 1, 0, h, L1)
                            step(h + 1, 1, h + 1, 0)
                        tiles(HEADS - 1)
                        combine(HEADS - 1, L1)
                        turn_out(HEADS - 1, L1)
                        dve.wait_ge(sem("o_rooted"), 1)
                        dve.reciprocal(o_stat[:, :, :], o_stat[:, :, :]).then_inc(sem("o_inverted"), 1)
                        dve.wait_ge(sem("o_inverted"), 1)
                        for h in range(HEADS):
                            rows = o_all[:, h, :, :]
                            dve.tensor_tensor(rows, rows, o_stat[:, h, :].unsqueeze(2).broadcast_to([P, RT, DV]), ALU.mult)\
                               .then_inc(sem("o_normed"), 1)

        attention()
        end_stage()
        turned_stack.close()

        res = residual[:, 0:KT, :]
        square_totals = [residual[:, KT + p, :] for p in range(2)]

        def even_output():
            with ExitStack() as st:
                y_hi = sb(st, "y_hi", [P, KT, SEQ], F32R)
                y_lo = sb(st, "y_lo", [P, KT, SEQ], F32R)
                SLOTS, GATE_SLOTS = 3, 4
                ORDER = [*range(SPILLED, KT), *range(SPILLED)]
                ON_CHIP = KT - SPILLED
                raw = fq[:, 0].rearrange("p r n -> p (r n)")[:, 0:SLOTS * KT * P].rearrange("p (s k n) -> p s k n", s=SLOTS, k=KT)
                gate_in = sb(st, "gate_in", [P, GATE_SLOTS, SEQ])
                w_hi = sb(st, "out_hi", [P, SLOTS, KT, P], F32R)
                w_lo = sb(st, "out_lo", [P, SLOTS, KT, P], F32R)
                w_out = a["even_w_out"].rearrange("e (k p) n -> p (e k) n", p=P)
                attended = fq[:, 1].rearrange("p r n -> p (r n)").rearrange("p (k n) -> p k n", k=HEADS)

                squares = SquareSum("sq1", [gate_in[:, p, :] for p in range(2)], ps[:, 6, 0:RT])

                def gate_tile(k):
                    return gate_in[:, k % GATE_SLOTS, :] if k < SPILLED else gate[:, k % 2, :]

                def mixed(k):
                    return y_f[:, k, :] if k < F_GROUPS else attended[:, k - F_GROUPS, :]

                def low_stands(eng, m):
                    if m == 1:
                        eng.wait_ge(sem("ow_low_second"), 1)
                    else:
                        eng.wait_ge(sem("ow_low"), max(m, 1))

                with nc.Block(name="even_out") as block:
                    @block.sync
                    def _(sp):
                        def load(m):
                            sp.dma_start(raw[:, m % SLOTS], w_out[:, :, m * P:(m + 1) * P])\
                              .then_inc(sem(f"ow_landed{m % SLOTS}"), 16)

                        load(0)
                        load(1)
                        for k in range(SPILLED):
                            if k >= GATE_SLOTS:
                                sp.wait_ge(sem("y_low"), ON_CHIP + k - GATE_SLOTS + 1)
                            sp.dma_start(gate_tile(k), gate_scratch[k]).then_inc(sem(f"gate_back{k}"), 16)
                        load(2)
                        sp.dma_start(res, x_scratch.rearrange("k p n -> p k n")).then_inc(sem("x_back"), 16)
                        for m in range(SLOTS, KT):
                            low_stands(sp, m - SLOTS)
                            load(m)

                    @block.scalar
                    def _(act):
                        def high(m):
                            act.wait_ge(sem(f"ow_landed{m % SLOTS}"), 16 * (m // SLOTS + 1))
                            if m >= SLOTS:
                                act.wait_ge(sem("ow_done"), m - SLOTS + 1)
                            split_high(act, w_hi[:, m % SLOTS], raw[:, m % SLOTS], sem("ow_high"))

                        for i, k in enumerate(ORDER):
                            if i == ON_CHIP:
                                high(0)
                                high(1)
                            act.wait_ge(sem("y_gated"), i + 1)
                            split_high(act, y_hi[:, k, :], gate_tile(k), sem("y_high"))
                        high(2)
                        for m in range(KT):
                            if m + SLOTS < KT:
                                high(m + SLOTS)
                            act.wait_ge(sem("ow_added"), m + 1)
                            squares.scalar(act, m)

                    @block.gpsimd
                    def _(pool):
                        for m in range(KT):
                            if m != 1:
                                pool.wait_ge(sem("ow_high"), m + 1)
                                split_low(pool, w_lo[:, m % SLOTS], raw[:, m % SLOTS], w_hi[:, m % SLOTS], sem("ow_low"))
                            if m - 2 in squares.ON_POOL:
                                squares.add(pool, m - 2)

                    @block.vector
                    def _(dve):
                        def low(i):
                            k = ORDER[i]
                            dve.wait_ge(sem("y_high"), i + 1)
                            split_low(dve, y_lo[:, k, :], gate_tile(k), y_hi[:, k, :], sem("y_low"))

                        for i, k in enumerate(ORDER):
                            if k < SPILLED:
                                dve.wait_ge(sem(f"gate_back{k}"), 16)
                            dve.tensor_tensor(gate_tile(k), gate_tile(k), mixed(k), ALU.mult).then_inc(sem("y_gated"), 1)
                            if i and i != ON_CHIP:
                                low(i - 1)
                            if i == ON_CHIP - 1:
                                low(i)
                                dve.wait_ge(sem("ow_high"), 2)
                                split_low(dve, w_lo[:, 1], raw[:, 1], w_hi[:, 1], sem("ow_low_second"))
                        low(KT - 1)
                        dve.wait_ge(sem("x_back"), 16)
                        for m in range(KT):
                            dve.wait_ge(sem("ow_done"), m + 1)
                            dve.scalar_tensor_tensor(out=res[:, m, :], in0=pair[m % 2], scalar=ada_col[:, 0, 2 * KT + m, 0:1],
                                                     in1=res[:, m, :], op0=ALU.mult, op1=ALU.add).then_inc(sem("ow_added"), 1)
                            if m - 1 in squares.ON_VECTOR:
                                squares.add(dve, m - 1)
                        squares.add(dve, KT - 1)

                    @block.tensor
                    def _(pe):
                        low_stands(pe, 0)
                        low_stands(pe, 1)
                        for i, k in enumerate(ORDER):
                            pe.wait_ge(sem("y_low"), i + 1)
                            for m in range(2):
                                last = channel_products(pe, pair[m], k, i, w_hi[:, m, k, :], w_lo[:, m, k, :], y_hi, y_lo)
                                if i == KT - 1:
                                    last.then_inc(sem("ow_done"), 1)
                        for m in range(2, KT):
                            low_stands(pe, m)
                            pe.wait_ge(sem("ow_added"), m - 1)
                            matmul3(pe, pair[m % 2], lambda k: w_hi[:, m % SLOTS, k, :], lambda k: w_lo[:, m % SLOTS, k, :],
                                    lambda k, c, e: y_hi[:, k, c:e], lambda k, c, e: y_lo[:, k, c:e], KT, SEQ)\
                                .then_inc(sem("ow_done"), 1)
                        squares.tensor(pe)

        even_output()
        end_stage()
        fq_stack.close()

        def load_unit(sp, kind, i, raw, src):
            sp.wait_ge(sem(kind + "_low"), i + 1)
            sp.dma_start(raw, src).then_inc(sem(kind + "_landed"), 16)

        def high_unit(act, kind, i, raw, hi, done_per_unit=1, spare=False):
            act.wait_ge(sem(kind + "_landed"), (i + 1) * 16)
            if not spare:
                act.wait_ge(sem(kind + "_done"), i * done_per_unit + 1)
            split_high(act, hi, raw, sem(kind + "_high"))

        def low_unit(pool, kind, i, raw, hi, lo, done_per_unit=1, spare=False):
            pool.wait_ge(sem(kind + "_high"), i + 1)
            if not spare:
                pool.wait_ge(sem(kind + "_done"), i * done_per_unit + 1)
            split_low(pool, lo, raw, hi, sem(kind + "_low"))

        def up_product(pe, kind, i, psum, hi, lo, h_hi, h_lo):
            pe.wait_ge(sem(kind + "_low"), i + 2)
            pe.wait_ge(sem(kind + "_free"), i + 1)
            matmul3(pe, psum, lambda k: hi[:, k, :], lambda k: lo[:, k, :],
                    lambda k, c, e: h_hi[:, k, c:e], lambda k, c, e: h_lo[:, k, c:e], KT, SEQ)\
                .then_inc(sem(kind + "_done"), 1)

        DOWN_PAIR = [(2, 3, 0)[d % 3] for d in range(KT)]

        def down_product(pe, kind, i, lent, lent_value, hi, lo, y_hi, y_lo, after=None):
            pe.wait_ge(sem(kind + "_low"), i + 2)
            pe.wait_ge(sem(kind + "_y_low"), i + 1)
            for d in range(KT):
                if d == 2:
                    pe.wait_ge(sem(lent), lent_value)
                else:
                    pe.wait_ge(sem(kind + "_free"), i * KT + (d if d > 2 else d + 1))
                matmul3(pe, pair[DOWN_PAIR[d]], lambda k: hi[:, d * P:(d + 1) * P], lambda k: lo[:, d * P:(d + 1) * P],
                        lambda k, c, e: y_hi[:, c:e], lambda k, c, e: y_lo[:, c:e], 1, SEQ)\
                    .then_inc(sem(kind + "_done"), 1)
                if after is not None:
                    after(d)

        def pair_0_returned(pe, kind, i):
            pe.wait_ge(sem(kind + "_free"), i * KT + 8)

        def odd_layer():
            with ExitStack() as st:
                h1_hi = sb(st, "h1_hi", [P, KT, SEQ], F32R)
                h1_lo = sb(st, "h1_lo", [P, KT, SEQ], F32R)
                kinds = ("cg", "xt", "bg", "gt")
                quarter = {"bg": 0, "cg": 1, "xt": 2, "gt": 3}
                raw = {k: sb(st, "raw_" + k, [P, KT, P]) for k in kinds}
                hi = {k: sb(st, "hi_" + k, [P, KT, P], F32R) for k in kinds}
                lo = {k: sb(st, "lo_" + k, [P, KT, P], F32R) for k in kinds}
                d_raw, d_hi, d_lo = sb(st, "d_raw", [P, D]), sb(st, "d_hi", [P, D], F32R), sb(st, "d_lo", [P, D], F32R)
                gates = sb(st, "gates", [P, 2, SEQ])
                c_gate, silu = gates[:, 0, :], gates[:, 1, :]
                u = sb(st, "u", [P, SEQ + 2])
                conv = sb(st, "conv", [P, SEQ])
                compact = sb(st, "compact1", [P, RT])
                norm = Norm("norm1", lambda k: res[:, k, :], SEQ, gain_col(2), shift_col(1, 0), lambda k: h1_hi[:, k, :],
                            lambda k: h1_lo[:, k, :], None, pair[2], scaled=gates, mean=ps[:, 6, 0:RT],
                            compact=compact[:, :])
                squares = SquareSum("sq2", [c_gate, silu], ps[:, 2, 0:RT])
                y_hi = sb(st, "yo_hi", [P, SEQ], F32R)
                y_lo = sb(st, "yo_lo", [P, SEQ], F32R)
                last_d_hi, last_d_lo = sb(st, "last_d_hi", [P, D], F32R), sb(st, "last_d_lo", [P, D], F32R)
                last_y_hi, last_y_lo = sb(st, "last_yo_hi", [P, SEQ], F32R), sb(st, "last_yo_lo", [P, SEQ], F32R)
                taps = sb(st, "taps", [P, 3, KT])
                w_in = a["odd_w_in"].rearrange("e (k p) n -> p (e k) n", p=P)
                w_out = a["odd_w_out"].rearrange("e k n -> (e k) n")
                N = KT
                up_pair = {"cg": 0, "xt": 1, "bg": 0, "gt": 1}

                with nc.Block(name="odd") as block:
                    @block.sync
                    def _(sp):
                        def loads(j, order):
                            for k in order:
                                load_unit(sp, k, j, raw[k][:, :, :], w_in[:, :, bass.ds(j * P + quarter[k] * D, P)])
                            load_unit(sp, "dn", j, d_raw[:, :], w_out[bass.ds(j * P, P), :])

                        loads(0, ("cg", "xt", "bg", "gt"))
                        with sp.Fori(1, N) as j:
                            loads(j, ("bg", "cg", "xt", "gt"))

                    @block.scalar
                    def _(act):
                        def block_step(j, last=False):
                            def next_high(k):
                                if not last:
                                    high_unit(act, k, j + 1, raw[k][:, :, :], hi[k][:, :, :])

                            act.wait_ge(sem("cg_done"), j + 2)
                            act.wait_ge(sem("u_done"), j + 1)
                            act.activation(c_gate, pair[0], ACT.Copy).then_inc(sem("cg_copied"), 1)
                            next_high("cg")
                            next_high("xt")
                            next_high("bg")
                            act.wait_ge(sem("gt_done"), j + 2)
                            act.wait_ge(sem("y_done"), j + 1)
                            act.activation(silu, pair[1], ACT.Silu).then_inc(sem("gt_silu"), 1)
                            next_high("gt")
                            if last:
                                high_unit(act, "dn", j, d_raw[:, :], last_d_hi[:, :], KT, spare=True)
                            act.wait_ge(sem("y_done"), j + 2)
                            if not last:
                                high_unit(act, "dn", j, d_raw[:, :], d_hi[:, :], KT)
                            split_high(act, (last_y_hi if last else y_hi)[:, :], conv[:, :], sem("y_split"))

                        norm.scalar_root(act)
                        for k in kinds[0:2]:
                            high_unit(act, k, 0, raw[k][:, :, :], hi[k][:, :, :])
                        for k in range(KT):
                            norm.scalar_high(act, k)
                        for k in kinds[2:4]:
                            high_unit(act, k, 0, raw[k][:, :, :], hi[k][:, :, :])
                        with act.Fori(0, N - 1) as j:
                            block_step(j)
                        block_step(N - 1, last=True)
                        for d in range(KT):
                            act.wait_ge(sem("dn_free"), (N - 1) * KT + d + 3)
                            squares.scalar(act, d)

                    @block.gpsimd
                    def _(pool):
                        def lows(j):
                            for k in kinds:
                                low_unit(pool, k, j, raw[k][:, :, :], hi[k][:, :, :], lo[k][:, :, :])

                        def rest(j):
                            low_unit(pool, "dn", j, d_raw[:, :], d_hi[:, :], d_lo[:, :], KT)
                            pool.wait_ge(sem("y_split"), j + 1)
                            split_low(pool, y_lo[:, :], conv[:, :], y_hi[:, :], sem("dn_y_low"))

                        def last_rest():
                            low_unit(pool, "dn", N - 1, d_raw[:, :], last_d_hi[:, :], last_d_lo[:, :], KT, spare=True)
                            pool.wait_ge(sem("y_split"), N)
                            split_low(pool, last_y_lo[:, :], conv[:, :], last_y_hi[:, :], sem("dn_y_low"))

                        lows(0)
                        with pool.Fori(0, N - 1) as j:
                            lows(j + 1)
                            rest(j)
                        last_rest()
                        for d in squares.ON_POOL:
                            squares.add(pool, d)

                    @block.vector
                    def _(dve):
                        for t in range(3):
                            dve.tensor_copy(taps[:, t, :], cols[:, ODD_CONV[0], ODD_CONV[1] + t * KT:ODD_CONV[1] + (t + 1) * KT])\
                               .then_inc(sem("taps_ready"), 1)
                        dve.memset(u[:, 0:1], 0.0).then_inc(sem("taps_ready"), 1)
                        dve.memset(u[:, SEQ + 1:SEQ + 2], 0.0).then_inc(sem("taps_ready"), 1)
                        dve.wait_ge(sem("taps_ready"), 5)
                        for name in [k + "_low" for k in kinds] + [k + "_done" for k in kinds] + \
                                [k + "_free" for k in ("cg", "xt")] + ["dn_low", "dn_done", "u_done", "y_done"]:
                            dve.sem_inc(sem(name), 1)
                        dve.sem_inc(sem("dn_free"), 2)

                        norm.vector_inverse(dve)
                        norm.vector_scale(dve)

                        def block_step(j):
                            dve.wait_ge(sem("cg_copied"), j + 1)
                            dve.wait_ge(sem("xt_done"), j + 2)
                            dve.tensor_tensor(u[:, 1:SEQ + 1], c_gate, pair[1], ALU.mult).then_inc(sem("u_done"), 1)
                            dve.wait_ge(sem("u_done"), j + 2)
                            dve.wait_ge(sem("dn_y_low"), j) if not isinstance(j, int) or j > 0 else None
                            conv_step = sem("conv_step")
                            dve.tensor_scalar(conv[:, :], u[:, 1:SEQ + 1], taps[:, 1, bass.ds(j, 1)], None, ALU.mult)\
                               .then_inc(conv_step, 1)
                            dve.wait_ge(conv_step, j * 3 + 1)
                            dve.scalar_tensor_tensor(out=conv[:, :], in0=u[:, 0:SEQ], scalar=taps[:, 0, bass.ds(j, 1)],
                                                     in1=conv[:, :], op0=ALU.mult, op1=ALU.add).then_inc(conv_step, 1)
                            dve.wait_ge(conv_step, j * 3 + 2)
                            dve.scalar_tensor_tensor(out=conv[:, :], in0=u[:, 2:SEQ + 2], scalar=taps[:, 2, bass.ds(j, 1)],
                                                     in1=conv[:, :], op0=ALU.mult, op1=ALU.add).then_inc(conv_step, 1)
                            dve.wait_ge(conv_step, j * 3 + 3)
                            dve.wait_ge(sem("bg_done"), j + 2)
                            dve.tensor_tensor(conv[:, :], pair[0], conv[:, :], ALU.mult).then_inc(sem("bg_used"), 1)

                        def last_product(j):
                            dve.wait_ge(sem("bg_used"), j + 1)
                            dve.wait_ge(sem("gt_silu"), j + 1)
                            dve.tensor_tensor(conv[:, :], conv[:, :], silu, ALU.mult).then_inc(sem("y_done"), 1)

                        def add(j, squared=False, tiles=range(KT)):
                            for d in tiles:
                                dve.wait_ge(sem("dn_done"), j * KT + d + 2)
                                dve.scalar_tensor_tensor(out=res[:, d, :], in0=pair[DOWN_PAIR[d]],
                                                         scalar=ada_col[:, 1, 2 * KT + d, 0:1], in1=res[:, d, :],
                                                         op0=ALU.mult, op1=ALU.add).then_inc(sem("dn_free"), 1)
                                if squared and d - 1 in squares.ON_VECTOR:
                                    squares.add(dve, d - 1)
                            if squared:
                                squares.add(dve, KT - 1)

                        block_step(0)
                        last_product(0)
                        with dve.Fori(1, N - 1) as j:
                            block_step(j)
                            add(j - 1)
                            last_product(j)
                        block_step(N - 1)
                        add(N - 2, tiles=range(0, 2))
                        last_product(N - 1)
                        add(N - 2, tiles=range(2, KT))
                        add(N - 1, squared=True)

                    @block.tensor
                    def _(pe):
                        def first_up():
                            for k in ("cg", "xt"):
                                pe.wait_ge(sem(k + "_low"), 2)
                            for q in range(KT):
                                pe.wait_ge(norm.s("low"), q + 1)
                                for k in ("cg", "xt"):
                                    last = channel_products(pe, pair[up_pair[k]], q, q, hi[k][:, q, :], lo[k][:, q, :],
                                                            h1_hi, h1_lo)
                                    if q == KT - 1:
                                        last.then_inc(sem(k + "_done"), 1)

                        def up(j, units=(("cg", "bg_used"), ("xt", "gt_silu"), ("bg", "cg_copied"), ("gt", "u_done"))):
                            for k, free in units:
                                pe.wait_ge(sem(k + "_low"), j + 2)
                                if k in ("cg", "xt"):
                                    pe.wait_ge(sem(free), j)
                                elif k == "bg":
                                    pe.wait_ge(sem(free), j + 1)
                                else:
                                    pe.wait_ge(sem(free), j + 2)
                                matmul3(pe, pair[up_pair[k]], lambda q: hi[k][:, q, :], lambda q: lo[k][:, q, :],
                                        lambda q, c, e: h1_hi[:, q, c:e], lambda q, c, e: h1_lo[:, q, c:e], KT, SEQ)\
                                    .then_inc(sem(k + "_done"), 1)

                        def down(j, blocks_up, operands=(d_hi, d_lo, y_hi, y_lo)):
                            down_product(pe, "dn", j, "bg_used", blocks_up, *(x[:, :] for x in operands))

                        norm.tensor_spread(pe)
                        first_up()
                        up(0, (("bg", "cg_copied"), ("gt", "u_done")))
                        up(1)
                        down(0, 2)
                        with pe.Fori(2, N) as j:
                            pair_0_returned(pe, "dn", j - 2)
                            up(j)
                            down(j - 1, j + 1)
                        down(N - 1, N, (last_d_hi, last_d_lo, last_y_hi, last_y_lo))
                        squares.tensor(pe)

        odd_layer()
        end_stage()

        def pool_layer():
            with ExitStack() as st:
                h = sb(st, "hp", [P, KT, PAD + SEQ])
                raw = sb(st, "pw_raw", [P, 4 * 2, HALF_GROUP])
                w_hi = sb(st, "pw_hi", [P, 4 * 2, HALF_GROUP], F32R)
                w_lo = sb(st, "pw_lo", [P, 4 * 2, HALF_GROUP], F32R)
                growth = sb(st, "growth", [P, 4, PAD])
                d_hi = sb(st, "dp_hi", [P, KT, SEQ], F32R)
                window = sb(st, "window", [P, 2, PAD + SEQ])
                bias = sb(st, "pool_bias", [P, KT])
                d_lo = sb(st, "dp_lo", [P, KT, SEQ], F32R)
                window_p = sb(st, "window_p", [P, 4, PAD + SEQ])
                compact = sb(st, "compact2", [P, RT])
                rstd = pair[0]
                norm = Norm("norm2", None, SEQ, None, None, None, None, None, rstd, mean=ps[:, 2, 0:RT],
                            compact=compact[:, :])
                squares = SquareSum("sq3", [window_p[:, p, PAD:PAD + SEQ] for p in range(2)], ps[:, 0, 0:RT])
                ON_POOL = (5, 7)
                SCALE_ORDER = ON_POOL + tuple(k for k in range(KT) if k not in ON_POOL)

                def window_sums(eng, k, buffers, step, n_steps):
                    src, width, b = h[:, k], 1, 0
                    while width < WINDOWS[k // 2]:
                        if n_steps:
                            eng.wait_ge(step, n_steps)
                        eng.tensor_tensor(buffers[:, b, PAD:PAD + SEQ], src[:, PAD:PAD + SEQ],
                                          src[:, PAD - width:PAD + SEQ - width], ALU.add).then_inc(step, 1)
                        n_steps += 1
                        src, width, b = buffers[:, b], 2 * width, 1 - b
                    return src, n_steps

                with nc.Block(name="pool") as block:
                    @block.sync
                    def _(sp):
                        sp.dma_start(raw[:, :, :], a["pool_w_2"].rearrange("a g (k p) n -> p (a g k) n", p=P))\
                          .then_inc(sem("pw_landed"), 16)
                        sp.dma_start(growth[:, :, :], a["growth"].partition_broadcast(P)).then_inc(sem("growth_landed"), 16)

                    @block.scalar
                    def _(act):
                        norm.scalar_root(act)
                        act.wait_ge(sem("pw_landed"), 16)
                        split_high(act, w_hi[:, :, :], raw[:, :, :], sem("pw_high"))
                        for k in SCALE_ORDER:
                            act.wait_ge(sem("pool_normed"), SCALE_ORDER.index(k) + 1)
                            act.activation(res[:, k, :], res[:, k, :], ACT.Identity, bias=bias[:, k:k + 1])\
                               .then_inc(sem("bias_added"), 1)
                        for k in range(KT):
                            act.wait_ge(sem("pool_diff"), k + 1)
                            split_high(act, d_hi[:, k, :], h[:, k, PAD:PAD + SEQ], sem("pool_high"))
                        for m in range(KT):
                            act.wait_ge(sem("pool_added"), m + 1)
                            squares.scalar(act, m)

                    @block.gpsimd
                    def _(pool):
                        for b in range(4):
                            pool.memset(window_p[:, b, 0:PAD], 0.0).then_inc(sem("window_p_step"), 1)
                        n_steps = 4
                        pool.wait_ge(sem("pw_high"), 1)
                        split_low(pool, w_lo[:, :, :], raw[:, :, :], w_hi[:, :, :], sem("pw_low"))
                        def lows(first, end):
                            for k in range(first, end):
                                pool.wait_ge(sem("pool_high"), k + 1)
                                split_low(pool, d_lo[:, k, :], h[:, k, PAD:PAD + SEQ], d_hi[:, k, :], sem("pool_low"))

                        for i, k in enumerate(ON_POOL):
                            pool.wait_ge(sem("pool_normed"), i + 1)
                            _, n_steps = window_sums(pool, k, window_p[:, 2 * i:2 * i + 2], sem("window_p_step"), n_steps)
                            pool.wait_ge(sem("window_p_step"), n_steps)
                            pool.sem_inc(sem("window_p_ready"), 1)
                            if i == 0:
                                lows(0, 2)
                        lows(2, KT - 1)
                        for m in squares.ON_POOL:
                            squares.add(pool, m)

                    @block.vector
                    def _(dve):
                        ws = sem("window_step")
                        n_ws = 0
                        for k in range(KT):
                            dve.memset(h[:, k, 0:PAD], 0.0).then_inc(ws, 1)
                        for b in range(2):
                            dve.memset(window[:, b, 0:PAD], 0.0).then_inc(ws, 1)
                        dve.tensor_tensor(bias[:, :], cols[:, POOL_B[0], POOL_B[1]:POOL_B[1] + KT],
                                          cols[:, POOL_SCALE[0], POOL_SCALE[1]:POOL_SCALE[1] + KT], ALU.mult).then_inc(ws, 1)
                        n_ws = KT + 3
                        norm.vector_inverse(dve)
                        dve.wait_ge(norm.s("spread"), 1)
                        for k in SCALE_ORDER:
                            dve.scalar_tensor_tensor(out=h[:, k, PAD:PAD + SEQ], in0=res[:, k, :], scalar=col(MIX_G, k), in1=rstd,
                                                     op0=ALU.mult, op1=ALU.mult).then_inc(sem("pool_normed"), 1)
                        dve.wait_ge(sem("growth_landed"), 16)
                        dve.wait_ge(sem("pool_normed"), KT)

                        def difference(k, src):
                            nonlocal n_ws
                            dve.tensor_tensor(src[:, PAD:2 * PAD], src[:, PAD:2 * PAD], growth[:, k // 2, :], ALU.mult)\
                               .then_inc(ws, 1)
                            n_ws += 1
                            dve.wait_ge(ws, n_ws)
                            dve.scalar_tensor_tensor(out=h[:, k, PAD:PAD + SEQ], in0=src[:, PAD:PAD + SEQ],
                                                     scalar=1.0 / WINDOWS[k // 2], in1=h[:, k, PAD:PAD + SEQ],
                                                     op0=ALU.mult, op1=ALU.subtract).then_inc(sem("pool_diff"), 1)
                            dve.wait_ge(sem("pool_diff"), k + 1)

                        def add(m):
                            dve.wait_ge(sem("bias_added"), SCALE_ORDER.index(m) + 1)
                            dve.wait_ge(sem("pool_done"), m + 1)
                            dve.scalar_tensor_tensor(out=res[:, m, :], in0=pair[m % 4], scalar=col(POOL_SCALE, m),
                                                     in1=res[:, m, :], op0=ALU.mult, op1=ALU.add).then_inc(sem("pool_added"), 1)

                        for k in range(KT):
                            if k in ON_POOL:
                                i = ON_POOL.index(k)
                                dve.wait_ge(sem("window_p_ready"), i + 1)
                                src = window_p[:, 2 * i + k // 2 % 2]
                            else:
                                src, n_ws = window_sums(dve, k, window, ws, n_ws)
                                dve.wait_ge(ws, n_ws)
                            difference(k, src)
                            if k == 5:
                                add(0)
                                add(1)
                        dve.wait_ge(sem("pool_high"), KT)
                        split_low(dve, d_lo[:, KT - 1, :], h[:, KT - 1, PAD:PAD + SEQ], d_hi[:, KT - 1, :], sem("pool_last_low"))
                        for m in range(2, KT):
                            add(m)
                            if m - 1 in squares.ON_VECTOR:
                                squares.add(dve, m - 1)
                        squares.add(dve, KT - 1)

                    @block.tensor
                    def _(pe):
                        norm.tensor_spread(pe)
                        pe.wait_ge(sem("pw_low"), 1)
                        for m in range(KT):
                            g, half = m // 2, (m % 2) * P
                            pe.wait_ge(sem("pool_low"), min(2 * g + 2, KT - 1))
                            if m == KT - 2:
                                pe.wait_ge(sem("pool_last_low"), 1)
                            if m >= 4:
                                pe.wait_ge(sem("pool_added"), m - 3)
                            matmul3(pe, pair[m % 4], lambda k: w_hi[:, 2 * g + k, half:half + P],
                                    lambda k: w_lo[:, 2 * g + k, half:half + P],
                                    lambda k, c, e: d_hi[:, 2 * g + k, c:e], lambda k, c, e: d_lo[:, 2 * g + k, c:e], 2, SEQ)\
                                .then_inc(sem("pool_done"), 1)
                        squares.tensor(pe)

        pool_layer()
        end_stage()

        def ffn_layer():
            with ExitStack() as st:
                zero = sb(st, "zero", [P, KT])
                h2_hi = sb(st, "h2_hi", [P, KT, SEQ], F32R)
                h2_lo = sb(st, "h2_lo", [P, KT, SEQ], F32R)
                kinds = ("va", "ga")
                raw = {k: sb(st, "raw_" + k, [P, KT, P]) for k in kinds}
                hi = {k: sb(st, "hi_" + k, [P, KT, P], F32R) for k in kinds}
                lo = {k: sb(st, "lo_" + k, [P, KT, P], F32R) for k in kinds}
                f_raw, f_hi, f_lo = sb(st, "f_raw", [P, D]), sb(st, "f_hi", [P, D], F32R), sb(st, "f_lo", [P, D], F32R)
                branches = sb(st, "branches", [P, 2, SEQ])
                branch = {k: branches[:, i, :] for i, k in enumerate(kinds)}
                compact = sb(st, "compact3", [P, RT])
                norm = Norm("norm3", lambda k: res[:, k, :], SEQ, lambda k: col(FFN_G, k), lambda k: zero[:, k:k + 1],
                            lambda k: h2_hi[:, k, :], lambda k: h2_lo[:, k, :], None, pair[2], scaled=branches,
                            mean=ps[:, 0, 0:RT], compact=compact[:, :])
                rows_out = sb(st, "rows_out", [P, RT, D])
                out_rows = out.rearrange("b (r p) d -> p (b r) d", p=P)
                y_hi = sb(st, "yf_hi", [P, SEQ], F32R)
                y_lo = sb(st, "yf_lo", [P, SEQ], F32R)
                spare = [sb(st, f"spare{i}", [P, D], F32R) for i in range(4)]
                first_hi, first_lo = ({k: spare[2 * i + part][:, :].rearrange("p (k n) -> p k n", k=KT)
                                       for i, k in enumerate(kinds)} for part in range(2))
                w_in = a["ffn_w_in_2"].rearrange("e (k p) n -> p (e k) n", p=P)
                w_out = a["ffn_w_out_2"].rearrange("e k n -> (e k) n")
                first = {"va": 0, "ga": FFN_T}
                up_pair = {"va": 0, "ga": 1}
                N = FFN_T

                def tap(where, k, j):
                    return cols[:, where[0], bass.ds(j + (where[1] + first[k]), 1)]

                with nc.Block(name="ffn") as block:
                    @block.sync
                    def _(sp):
                        with sp.Fori(0, N) as j:
                            for k in kinds:
                                load_unit(sp, k, j, raw[k][:, :, :], w_in[:, :, bass.ds(j * P + first[k] * P, P)])
                            load_unit(sp, "fd", j, f_raw[:, :], w_out[bass.ds(j * P, P), :])
                        for d in range(KT):
                            sp.wait_ge(sem("out_copied"), 2 * d + 2)
                            sp.dma_start(out_rows[:, :, d * P:(d + 1) * P], rows_out[:, :, d * P:(d + 1) * P])\
                              .then_inc(sem("stored"), 16)
                        sp.wait_ge(sem("stored"), 16 * KT)

                    @block.scalar
                    def _(act):
                        def block_step(j, splits=True, last=False):
                            for k in kinds:
                                act.wait_ge(sem(k + "_done"), j + 2)
                                act.wait_ge(sem("fd_y_free"), j + 1)
                                act.activation(branch[k][:, :], pair[up_pair[k]], ACT.Identity, scale=tap(FFN_TAP2, k, j),
                                               bias=tap(FFN_B, k, j)).then_inc(sem(k + "_tap2"), 1)
                                if splits:
                                    high_unit(act, k, j + 1, raw[k][:, :, :], hi[k][:, :, :])
                            high_unit(act, "fd", j, f_raw[:, :], (spare[0] if last else f_hi)[:, :], KT, spare=last)
                            act.wait_ge(sem("ga_free"), j + 2)
                            act.activation(branch["ga"][:, :], branch["ga"][:, :], ACT.Silu).then_inc(sem("ga_silu"), 1)
                            act.wait_ge(sem("fy_done"), j + 1)
                            split_high(act, (spare[2] if last else y_hi)[:, :], branch["va"][:, :], sem("fy_split"))

                        norm.scalar_root(act)
                        for k in kinds:
                            high_unit(act, k, 0, raw[k][:, :, :], first_hi[k], spare=True)
                        for k in range(KT):
                            norm.scalar_high(act, k)
                        for k in kinds:
                            high_unit(act, k, 1, raw[k][:, :, :], hi[k][:, :, :], spare=True)
                        block_step(0, splits=False)
                        with act.Fori(1, N - 1) as j:
                            block_step(j)
                        block_step(N - 1, splits=False, last=True)
                        for n in range(2 * KT):
                            d, half = n // 2, n % 2
                            act.wait_ge(sem("out_turned"), n + 1)
                            act.activation(rows_out[:, 4 * half:4 * half + 4, d * P:(d + 1) * P],
                                           ps[:, 2 + half, :].rearrange("p (r n) -> p r n", n=P), ACT.Copy)\
                               .then_inc(sem("out_copied"), 1)

                    @block.gpsimd
                    def _(pool):
                        def rest(j, last=False):
                            d_hi, d_lo, v_hi, v_lo = spare if last else (f_hi, f_lo, y_hi, y_lo)
                            low_unit(pool, "fd", j, f_raw[:, :], d_hi[:, :], d_lo[:, :], KT, spare=last)
                            pool.wait_ge(sem("fy_split"), j + 1)
                            split_low(pool, v_lo[:, :], branch["va"][:, :], v_hi[:, :], sem("fd_y_low"))
                            pool.wait_ge(sem("fd_y_low"), j + 1)
                            pool.sem_inc(sem("fd_y_free"), 1)

                        for k in kinds:
                            low_unit(pool, k, 0, raw[k][:, :, :], first_hi[k], first_lo[k], spare=True)
                        for k in kinds:
                            low_unit(pool, k, 1, raw[k][:, :, :], hi[k][:, :, :], lo[k][:, :, :], spare=True)
                        rest(0)
                        with pool.Fori(1, N - 1) as j:
                            for k in kinds:
                                low_unit(pool, k, j + 1, raw[k][:, :, :], hi[k][:, :, :], lo[k][:, :, :])
                            rest(j)
                        rest(N - 1, last=True)

                    @block.vector
                    def _(dve):
                        dve.memset(zero[:, :], 0.0).then_inc(sem("zeroed"), 1)
                        for name in [k + s for k in kinds for s in ("_low", "_done", "_free")] + ["fd_low", "fd_done", "fd_y_free"]:
                            dve.sem_inc(sem(name), 1)
                        dve.sem_inc(sem("fd_free"), 2)
                        dve.wait_ge(sem("zeroed"), 1)
                        norm.vector_inverse(dve)
                        norm.vector_scale(dve)

                        def taps(k, j):
                            x, y = pair[up_pair[k]], branch[k]
                            dve.wait_ge(sem(k + "_tap2"), j + 1)
                            dve.scalar_tensor_tensor(out=y[:, 1:SEQ], in0=x[:, 0:SEQ - 1], scalar=tap(FFN_TAP1, k, j),
                                                     in1=y[:, 1:SEQ], op0=ALU.mult, op1=ALU.add).then_inc(sem(k + "_tap1"), 1)
                            dve.wait_ge(sem(k + "_tap1"), j + 1)
                            dve.scalar_tensor_tensor(out=y[:, 2:SEQ], in0=x[:, 0:SEQ - 2], scalar=tap(FFN_TAP0, k, j),
                                                     in1=y[:, 2:SEQ], op0=ALU.mult, op1=ALU.add).then_inc(sem(k + "_free"), 1)

                        def product(j):
                            dve.wait_ge(sem("ga_silu"), j + 1)
                            dve.wait_ge(sem("va_free"), j + 2)
                            dve.tensor_tensor(branch["va"][:, :], branch["va"][:, :], branch["ga"][:, :], ALU.mult)\
                               .then_inc(sem("fy_done"), 1)

                        def add(j, tiles=range(KT)):
                            for d in tiles:
                                dve.wait_ge(sem("fd_done"), j * KT + d + 2)
                                dve.tensor_tensor(res[:, d, :], pair[DOWN_PAIR[d]], res[:, d, :], ALU.add)\
                                   .then_inc(sem("fd_free"), 1)

                        taps("va", 0)
                        taps("ga", 0)
                        product(0)
                        with dve.Fori(1, N - 1) as j:
                            taps("va", j)
                            add(j - 1)
                            taps("ga", j)
                            product(j)
                        taps("va", N - 1)
                        add(N - 2, range(0, 2))
                        taps("ga", N - 1)
                        add(N - 2, range(2, 4))
                        product(N - 1)
                        add(N - 2, range(4, KT))
                        add(N - 1)

                    @block.tensor
                    def _(pe):
                        def up(j):
                            for k in kinds:
                                up_product(pe, k, j, pair[up_pair[k]], hi[k], lo[k], h2_hi, h2_lo)

                        def down(j, blocks_up, operands=(f_hi, f_lo, y_hi, y_lo), after=None):
                            down_product(pe, "fd", j, "va_free", blocks_up + 1, *(x[:, :] for x in operands), after=after)

                        def turn_out(d):
                            pe.wait_ge(sem("fd_free"), (N - 1) * KT + d + 3)
                            for half in range(2):
                                if d:
                                    pe.wait_ge(sem("out_copied"), 2 * d - 1 + half)
                                for r in range(4 * half, 4 * half + 4):
                                    last = pe.transpose(ps[:, 2 + half, (r % 4) * P:(r % 4 + 1) * P],
                                                        res[:, d, r * P:(r + 1) * P], ident[:, :])
                                last.then_inc(sem("out_turned"), 1)

                        norm.tensor_spread(pe)
                        for k in kinds:
                            pe.wait_ge(sem(k + "_low"), 2)
                        for q in range(KT):
                            pe.wait_ge(norm.s("low"), q + 1)
                            for k in kinds:
                                last = channel_products(pe, pair[up_pair[k]], q, q, first_hi[k][:, q, :], first_lo[k][:, q, :],
                                                        h2_hi, h2_lo)
                                if q == KT - 1:
                                    last.then_inc(sem(k + "_done"), 1)
                        up(1)
                        down(0, 2)
                        with pe.Fori(2, N) as j:
                            pair_0_returned(pe, "fd", j - 2)
                            up(j)
                            down(j - 1, j + 1)
                        down(N - 1, N, spare, lambda d: turn_out(d - 2) if d >= 2 else None)
                        turn_out(KT - 2)
                        turn_out(KT - 1)

        ffn_layer()


_INS = ["x", "c", "ctx", "c_ctx", "norm_g", "ada_w", "ada_b", "even_w_in", "even_q_norm", "even_k_norm",
        "even_lambda_q1", "even_lambda_k1", "even_lambda_q2", "even_lambda_k2", "even_subln", "even_w_out",
        "odd_w_in", "odd_conv_w", "odd_w_out", "norm_mix_g_2", "norm_ffn_g_2", "pool_w_2", "pool_b_2",
        "pool_scale_2", "ffn_w_in_2", "ffn_conv_w_2", "ffn_conv_b_2", "ffn_w_out_2"]


def _constants():
    import numpy as np
    c = {"identity": np.eye(P, dtype=np.float32)}
    grid = 64
    pos = np.arange(SEQ)
    half = DH // 2
    freqs = np.float32(10000.0) ** (-np.arange(0, half, 2, dtype=np.float32) / np.float32(half))
    ang = np.stack([(p.astype(np.float32)[:, None] * freqs) for p in (pos // grid, pos % grid)], axis=1)
    c["rope_cos"] = np.cos(ang.astype(np.float64)).astype(np.float32)
    c["rope_sin"] = np.sin(ang.astype(np.float64)).astype(np.float32)
    p, k2 = np.arange(P)[:, None], np.arange(P)[None, :]
    dft = np.zeros((P, RADIX, 3, P))
    for k1 in range(RADIX):
        th = 2 * np.pi * ((p * (k1 + RADIX * k2)) % SEQ) / SEQ
        dft[:, k1] = np.stack([np.cos(th), -np.sin(th), -np.cos(th)] if k1 > RADIX // 2 else
                              [np.sin(th), np.cos(th), -np.sin(th)], axis=1)
    c["seq_dft"] = dft.astype(np.float32)
    th = 2 * np.pi * ((p * k2) % P) / P
    c["channel_dft"] = (np.stack([np.cos(th), np.sin(th)], axis=1) / np.sqrt(SEQ * P)).astype(np.float32)
    t = np.arange(PAD)
    c["growth"] = np.stack([w / np.minimum(t + 1, w) for w in WINDOWS]).astype(np.float32)
    return c


def kernel(**inputs):
    import numpy as np
    import concourse.bacc as bacc
    from concourse.bass_utils import run_bass_kernel_spmd

    nc = bacc.Bacc("TRN2", target_bir_lowering=False, num_devices=1)
    arrays, aps = {}, {}
    named = {n: np.ascontiguousarray(inputs[n]) for n in _INS}
    for name, value in {**named, **_constants()}.items():
        arrays[f"in_{name}"] = value
        aps[name] = nc.dram_tensor(f"in_{name}", value.shape, mybir.dt.from_np(value.dtype), kind="ExternalInput").ap()
    out = nc.dram_tensor("out", (1, SEQ, D), F32, kind="ExternalOutput").ap()
    program(nc, aps, out)
    result = run_bass_kernel_spmd(nc, [arrays], core_ids=[0])
    return result.results[0]["out"]
```
